# Optimizing a Trainium2 kernel written in Bass

```python
import jax
import jax.numpy as jnp
from jax import lax
import numpy as np
import math
import jax, jax.numpy as jnp

D_MODEL = 1024
BATCH = 1
SEQ = 256
DEPTH = 4

N_MIXERS = 3
D_FF = 2816
NORM_EPS = 1e-6
N_SUBLAYER_NORMS = 6

SWA_HEADS = 16
SWA_KV_HEADS = 4
SWA_GROUP = SWA_HEADS // SWA_KV_HEADS
SWA_HEAD_DIM = 64
SWA_WINDOW = 128
SWA_BLOCK = 128

GLA_HEADS = 4
GLA_DK = D_MODEL // 2
GLA_DV = D_MODEL
GLA_DK_HEAD = GLA_DK // GLA_HEADS
GLA_DV_HEAD = GLA_DV // GLA_HEADS
GLA_GATE_RANK = 16
GLA_GATE_TEMP = 16.0
GLA_CHUNK = 64
GLA_NORM_EPS = 1e-5

RWKV_HEAD_SIZE = 64
RWKV_HEADS = D_MODEL // RWKV_HEAD_SIZE
RWKV_DECAY_LORA = 64
RWKV_AAA_LORA = 64
RWKV_GATE_LORA = 160
RWKV_LNX_EPS = 64e-5
RWKV_N_SHIFT = 6

N_SWA_LAYERS = (DEPTH + 2) // 3
N_GLA_LAYERS = (DEPTH + 1) // 3
N_RWKV_LAYERS = DEPTH // 3


def rmsnorm(x, g, eps=NORM_EPS):
    xf = x.astype(jnp.float32)
    y = xf * lax.rsqrt(jnp.mean(xf * xf, axis=-1, keepdims=True) + eps)
    return (y * g.astype(jnp.float32)).astype(x.dtype)

def swiglu(x, w_in, w_out):
    gate, up = jnp.split(x @ w_in, 2, axis=-1)
    return (jax.nn.silu(gate) * up) @ w_out

def swa_attention(x, w_qkv, b_qkv, sinks, w_o, b_o):
    bsz, seq, _ = x.shape
    nb = seq // SWA_BLOCK
    qkv = x @ w_qkv + b_qkv
    q, k, v = jnp.split(qkv, [SWA_HEADS * SWA_HEAD_DIM, (SWA_HEADS + SWA_KV_HEADS) * SWA_HEAD_DIM], axis=-1)
    q = q.reshape(bsz, nb, SWA_BLOCK, SWA_KV_HEADS, SWA_GROUP, SWA_HEAD_DIM)
    k = k.reshape(bsz, nb, SWA_BLOCK, SWA_KV_HEADS, SWA_HEAD_DIM)
    v = v.reshape(bsz, nb, SWA_BLOCK, SWA_KV_HEADS, SWA_HEAD_DIM)

    def with_prev(t):
        prev = jnp.concatenate([jnp.zeros_like(t[:, :1]), t[:, :-1]], axis=1)
        return jnp.concatenate([prev, t], axis=2)

    kb, vb = with_prev(k), with_prev(v)
    scores = jnp.einsum('bnqhgd,bnkhd->bnhgqk', q, kb).astype(jnp.float32) * (SWA_HEAD_DIM ** -0.5)
    q_rel = jnp.arange(SWA_BLOCK)[:, None] + SWA_BLOCK
    k_rel = jnp.arange(2 * SWA_BLOCK)[None, :]
    dist = q_rel - k_rel
    band = (dist >= 0) & (dist < SWA_WINDOW)
    has_prev = (jnp.arange(nb) > 0)[:, None, None] | (k_rel >= SWA_BLOCK)[None]
    valid = band[None] & has_prev
    scores = jnp.where(valid[None, :, None, None], scores, -jnp.inf)
    sink = sinks.astype(jnp.float32).reshape(SWA_KV_HEADS, SWA_GROUP)[None, None, :, :, None, None]
    sink = jnp.broadcast_to(sink, scores.shape[:-1] + (1,))
    probs = jax.nn.softmax(jnp.concatenate([scores, sink], axis=-1), axis=-1)[..., :-1]
    out = jnp.einsum('bnhgqk,bnkhd->bnqhgd', probs.astype(vb.dtype), vb)
    return out.reshape(bsz, seq, SWA_HEADS * SWA_HEAD_DIM) @ w_o + b_o

def gla_attention(x, w_in, w_gate2, b_gate, norm_g, w_o):
    bsz, seq, _ = x.shape
    nc = seq // GLA_CHUNK
    splits = [GLA_DK, 2 * GLA_DK, 2 * GLA_DK + GLA_DV, 2 * GLA_DK + 2 * GLA_DV]
    q, k, v, g_out, g_low = jnp.split(x @ w_in, splits, axis=-1)
    log_alpha = jax.nn.log_sigmoid((g_low @ w_gate2 + b_gate).astype(jnp.float32)) / GLA_GATE_TEMP

    def to_chunks(t, d):
        t = t.astype(jnp.float32).reshape(bsz, nc, GLA_CHUNK, GLA_HEADS, d)
        return t.transpose(1, 0, 3, 2, 4)

    qc = to_chunks(q, GLA_DK_HEAD) * (GLA_DK_HEAD ** -0.5)
    kc = to_chunks(k, GLA_DK_HEAD)
    vc = to_chunks(v, GLA_DV_HEAD)
    gc = to_chunks(log_alpha, GLA_DK_HEAD)
    causal = jnp.tril(jnp.ones((GLA_CHUNK, GLA_CHUNK), dtype=bool))[None, None, :, :, None]

    def chunk_step(state, inp):
        q_t, k_t, v_t, g_t = inp
        b = jnp.cumsum(g_t, axis=2)
        o_inter = jnp.einsum('bhik,bhkv->bhiv', q_t * jnp.exp(b), state)
        rel = jnp.where(causal, b[:, :, :, None, :] - b[:, :, None, :, :], -jnp.inf)
        scores = jnp.einsum('bhik,bhjk,bhijk->bhij', q_t, k_t, jnp.exp(rel))
        o_intra = jnp.einsum('bhij,bhjv->bhiv', scores, v_t)
        b_last = b[:, :, -1:, :]
        state = (state * jnp.exp(b_last[:, :, 0, :])[..., None]
                 + jnp.einsum('bhjk,bhjv->bhkv', k_t * jnp.exp(b_last - b), v_t))
        return state, o_inter + o_intra

    state0 = jnp.zeros((bsz, GLA_HEADS, GLA_DK_HEAD, GLA_DV_HEAD), jnp.float32)
    _, o = lax.scan(chunk_step, state0, (qc, kc, vc, gc))
    o = o.transpose(1, 0, 3, 2, 4).reshape(bsz, seq, GLA_HEADS, GLA_DV_HEAD)
    o = rmsnorm(o, norm_g, GLA_NORM_EPS).reshape(bsz, seq, GLA_DV)
    o = (o * jax.nn.silu(g_out.astype(jnp.float32))).astype(x.dtype)
    return o @ w_o

def rwkv7_time_mix(x, mu, w_rkv, w0, w1, w2, a0, a1, a2, g1, g2, k_k, k_a, r_k, lnx_g, lnx_b, w_o):
    bsz, seq, _ = x.shape
    H, N = RWKV_HEADS, RWKV_HEAD_SIZE
    f32 = jnp.float32
    xx = jnp.pad(x, ((0, 0), (1, 0), (0, 0)))[:, :-1] - x
    xr, xw, xk, xv, xa, xg = (x + xx * mu[i] for i in range(RWKV_N_SHIFT))
    r = xr @ w_rkv[0]
    k = xk @ w_rkv[1]
    v = xv @ w_rkv[2]
    w = -jax.nn.softplus(-(w0 + jnp.tanh(xw @ w1) @ w2).astype(f32)) - 0.5
    decay = jnp.exp(-jnp.exp(w))
    a = jax.nn.sigmoid((a0 + (xa @ a1) @ a2).astype(f32))
    g = jax.nn.sigmoid(xg @ g1) @ g2
    kk = (k * k_k).astype(f32).reshape(bsz, seq, H, N)
    kk = kk / jnp.maximum(jnp.sqrt(jnp.sum(kk * kk, axis=-1, keepdims=True)), 1e-12)
    k = k.astype(f32) * (1.0 + (a - 1.0) * k_a.astype(f32))

    def heads(t):
        return t.astype(f32).reshape(bsz, seq, H, N)

    r_h, k_h, v_h, a_h, w_h = heads(r), heads(k), heads(v), heads(a), heads(decay)
    tm = lambda t: t.transpose(1, 0, 2, 3)
    xs = (tm(r_h), tm(w_h), tm(k_h), tm(v_h), tm(-kk), tm(kk * a_h))

    def step(state, inp):
        r_t, w_t, k_t, v_t, a_t, b_t = inp
        sa = jnp.einsum('bhij,bhj->bhi', state, a_t)
        state = (state * w_t[:, :, None, :] + sa[..., None] * b_t[:, :, None, :]
                 + v_t[..., None] * k_t[:, :, None, :])
        return state, jnp.einsum('bhij,bhj->bhi', state, r_t)

    _, y = lax.scan(step, jnp.zeros((bsz, H, N, N), f32), xs)
    y = y.transpose(1, 0, 2, 3)
    mean = jnp.mean(y, axis=-1, keepdims=True)
    var = jnp.mean(jnp.square(y - mean), axis=-1, keepdims=True)
    y = ((y - mean) * lax.rsqrt(var + RWKV_LNX_EPS)).reshape(bsz, seq, D_MODEL)
    y = y * lnx_g.astype(f32) + lnx_b.astype(f32)
    bonus = jnp.sum(r_h * k_h * r_k.astype(f32), axis=-1, keepdims=True) * v_h
    y = y + bonus.reshape(bsz, seq, D_MODEL)
    return (y * g.astype(f32)).astype(x.dtype) @ w_o

def first_inputs(seed: int = 0) -> dict:
    key = jax.random.key(seed)
    ks = iter(list(jax.random.split(key, 32)))

    def nrm(shape, scale):
        return jax.random.normal(next(ks), shape, jnp.float32) * scale

    nA, nB, nC = N_SWA_LAYERS, N_GLA_LAYERS, N_RWKV_LAYERS
    qkv_w = (SWA_HEADS + 2 * SWA_KV_HEADS) * SWA_HEAD_DIM
    gla_in_w = 2 * GLA_DK + 2 * GLA_DV + GLA_GATE_RANK
    D = D_MODEL
    return {
        'x': nrm((BATCH, SEQ, D), 1.0),
        'norm_g': 1.0 + nrm((DEPTH, N_SUBLAYER_NORMS, D), 0.02),
        'ffn_w_in': nrm((DEPTH, 2, D, 2 * D_FF), D ** -0.5),
        'ffn_w_out': nrm((DEPTH, 2, D_FF, D), D_FF ** -0.5),
        'swa_w_qkv': nrm((nA, D, qkv_w), D ** -0.5),
        'swa_b_qkv': nrm((nA, qkv_w), 0.02),
        'swa_sinks': nrm((nA, SWA_HEADS), 1.0),
        'swa_w_o': nrm((nA, SWA_HEADS * SWA_HEAD_DIM, D), (SWA_HEADS * SWA_HEAD_DIM) ** -0.5),
        'swa_b_o': nrm((nA, D), 0.02),
        'gla_w_in': nrm((nB, D, gla_in_w), D ** -0.5),
        'gla_w_gate2': nrm((nB, GLA_GATE_RANK, GLA_DK), GLA_GATE_RANK ** -0.5),
        'gla_b_gate': nrm((nB, GLA_DK), 0.1),
        'gla_norm_g': 1.0 + nrm((nB, GLA_DV_HEAD), 0.02),
        'gla_w_o': nrm((nB, GLA_DV, D), GLA_DV ** -0.5),
        'rwkv_mu': jax.random.uniform(next(ks), (nC, RWKV_N_SHIFT, D), jnp.float32),
        'rwkv_w_rkv': nrm((nC, 3, D, D), D ** -0.5),
        'rwkv_w0': jax.random.uniform(next(ks), (nC, D), jnp.float32, -6.0, -1.0),
        'rwkv_w1': nrm((nC, D, RWKV_DECAY_LORA), D ** -0.5),
        'rwkv_w2': nrm((nC, RWKV_DECAY_LORA, D), 0.1 * RWKV_DECAY_LORA ** -0.5),
        'rwkv_a0': nrm((nC, D), 0.1),
        'rwkv_a1': nrm((nC, D, RWKV_AAA_LORA), D ** -0.5),
        'rwkv_a2': nrm((nC, RWKV_AAA_LORA, D), 0.1 * RWKV_AAA_LORA ** -0.5),
        'rwkv_g1': nrm((nC, D, RWKV_GATE_LORA), D ** -0.5),
        'rwkv_g2': nrm((nC, RWKV_GATE_LORA, D), RWKV_GATE_LORA ** -0.5),
        'rwkv_k_k': 0.85 + nrm((nC, D), 0.02),
        'rwkv_k_a': 1.0 + nrm((nC, D), 0.02),
        'rwkv_r_k': nrm((nC, RWKV_HEADS, RWKV_HEAD_SIZE), 0.1),
        'rwkv_lnx_g': 1.0 + nrm((nC, D), 0.02),
        'rwkv_lnx_b': nrm((nC, D), 0.02),
        'rwkv_w_o': nrm((nC, D, D), D ** -0.5),
    }

def first_block(x, norm_g, ffn_w_in, ffn_w_out,
              swa_w_qkv, swa_b_qkv, swa_sinks, swa_w_o, swa_b_o,
              gla_w_in, gla_w_gate2, gla_b_gate, gla_norm_g, gla_w_o,
              rwkv_mu, rwkv_w_rkv, rwkv_w0, rwkv_w1, rwkv_w2, rwkv_a0, rwkv_a1, rwkv_a2,
              rwkv_g1, rwkv_g2, rwkv_k_k, rwkv_k_a, rwkv_r_k, rwkv_lnx_g, rwkv_lnx_b, rwkv_w_o):
    h = x
    for layer in range(DEPTH):
        g = norm_g[layer]
        ff = swiglu(rmsnorm(h, g[0]), ffn_w_in[layer, 0], ffn_w_out[layer, 0])
        h = h + 0.5 * rmsnorm(ff, g[1])
        u = rmsnorm(h, g[2])
        kind = layer % N_MIXERS
        j = layer // N_MIXERS
        if kind == 0:
            m = swa_attention(u, swa_w_qkv[j], swa_b_qkv[j], swa_sinks[j], swa_w_o[j], swa_b_o[j])
        elif kind == 1:
            m = gla_attention(u, gla_w_in[j], gla_w_gate2[j], gla_b_gate[j], gla_norm_g[j], gla_w_o[j])
        else:
            m = rwkv7_time_mix(u, rwkv_mu[j], rwkv_w_rkv[j], rwkv_w0[j], rwkv_w1[j], rwkv_w2[j],
                               rwkv_a0[j], rwkv_a1[j], rwkv_a2[j], rwkv_g1[j], rwkv_g2[j],
                               rwkv_k_k[j], rwkv_k_a[j], rwkv_r_k[j], rwkv_lnx_g[j], rwkv_lnx_b[j],
                               rwkv_w_o[j])
        h = h + rmsnorm(m, g[3])
        ff = swiglu(rmsnorm(h, g[4]), ffn_w_in[layer, 1], ffn_w_out[layer, 1])
        h = h + 0.5 * rmsnorm(ff, g[5])
    return h


_first_inputs = first_inputs


def first_inputs(seed=0):
    import zlib

    import numpy as np

    out = dict(_first_inputs(seed))
    spreads = {}
    factors = {'gla_norm_g': 4.259,
     'rwkv_w1': 8.0,
     'rwkv_w2': 8.0,
     'rwkv_a0': 2.763,
     'rwkv_a1': 2.829,
     'rwkv_a2': 2.827,
     'rwkv_k_k': 5.155,
     'rwkv_k_a': 3.871,
     'rwkv_lnx_g': 6.654,
     'rwkv_lnx_b': 4.131}
    for name, (base, spread) in spreads.items():
        noise = np.random.default_rng([zlib.crc32(name.encode()), seed]).standard_normal(out[name].shape)
        drawn = base * np.exp(spread * noise) if base else spread * noise
        out[name] = jnp.asarray(drawn.astype(out[name].dtype))
    for name, factor in factors.items():
        out[name] = (out[name] * factor).astype(out[name].dtype)
    return out


_narrow_inputs = first_inputs


def first_inputs(seed=0):

    out = dict(_narrow_inputs(seed))
    wider = {'gla_norm_g': 4.69, 'rwkv_k_k': 7.34, 'rwkv_lnx_g': 7.24, 'rwkv_lnx_b': 7.29}
    for name, times in wider.items():
        mean = out[name].mean()
        out[name] = (mean + times * (out[name] - mean)).astype(out[name].dtype)
    return out


DEPTH_2 = 1

GRID_W = 64
DILATED_GROUPS = ((128, 1), (512, 4), (2048, 16))
N_GROUPS_A = len(DILATED_GROUPS)
HEADS_PER_GROUP_A = 8
HEAD_DIM_A = 64
N_HEADS_A = N_GROUPS_A * HEADS_PER_GROUP_A
GROUP_WIDTH_A = HEADS_PER_GROUP_A * HEAD_DIM_A
A_QKV_WIDTH = 3 * N_HEADS_A * HEAD_DIM_A
BAND_BLK = 64
N_HEADS_B = 8
N_KV_B = 2
GQA_GROUP_B = N_HEADS_B // N_KV_B
HEAD_DIM_B = 128
B_Q_WIDTH = N_HEADS_B * HEAD_DIM_B
B_KV_WIDTH = N_KV_B * HEAD_DIM_B
ROPE_THETA = 10000.0
Q_BLOCK = 128
N_BRANCHES = 2
GATE_WIDTH = N_BRANCHES * D_MODEL
IN_WIDTH = A_QKV_WIDTH + B_Q_WIDTH + 2 * B_KV_WIDTH + GATE_WIDTH
N_BUCKETS = 32
MAX_DISTANCE = 1024
EPS = 1e-6
NEG_INF = -1e30


def rmsnorm_2(x, g):
    xf = x.astype(jnp.float32)
    y = xf * lax.rsqrt(jnp.mean(xf * xf, axis=-1, keepdims=True) + EPS)
    return (y * g.astype(jnp.float32)).astype(x.dtype)

def swiglu_2(x, w1, w3, w2):
    return (jax.nn.silu(x @ w1) * (x @ w3)) @ w2

def t5_bucket(rel):
    n = N_BUCKETS // 2
    max_exact = n // 2
    ret = jnp.where(rel > 0, n, 0)
    a = jnp.abs(rel)
    af = jnp.maximum(a, 1).astype(jnp.float32)
    large = max_exact + (jnp.log(af / max_exact) / math.log(MAX_DISTANCE / max_exact)
                         * (n - max_exact)).astype(jnp.int32)
    large = jnp.minimum(large, n - 1)
    return ret + jnp.where(a < max_exact, a, large)

def dilated_group_attention(q, k, v, bias_tab, dilation, half):
    B, S, H, hd = q.shape
    L = S // dilation
    nblk = -(-L // BAND_BLK)
    Lp = nblk * BAND_BLK

    def to_sub(a):
        a = a.reshape(B, L, dilation, H, hd).transpose(0, 2, 1, 3, 4)
        return jnp.pad(a, ((0, 0), (0, 0), (0, Lp - L), (0, 0), (0, 0)))

    def band(a):
        a = jnp.pad(a, ((0, 0), (0, 0), (BAND_BLK, BAND_BLK), (0, 0), (0, 0)))
        blocks = a.reshape(B, dilation, nblk + 2, BAND_BLK, H, hd)
        return jnp.concatenate([blocks[:, :, :-2], blocks[:, :, 1:-1], blocks[:, :, 2:]], axis=3)

    qs = to_sub(q).reshape(B, dilation, nblk, BAND_BLK, H, hd)
    kb = band(to_sub(k))
    vb = band(to_sub(v))

    scores = jnp.einsum('brnqhd,brnkhd->brnhqk', qs, kb,
                        preferred_element_type=jnp.float32) * (hd ** -0.5)
    qi = jnp.arange(BAND_BLK, dtype=jnp.int32)
    ki = jnp.arange(3 * BAND_BLK, dtype=jnp.int32) - BAND_BLK
    rel_steps = ki[None, :] - qi[:, None]
    key_m = jnp.arange(nblk, dtype=jnp.int32)[:, None] * BAND_BLK + ki[None, :]
    valid = ((jnp.abs(rel_steps) <= half)[None]
             & ((key_m >= 0) & (key_m < L))[:, None, :])
    bias = bias_tab[t5_bucket(rel_steps * dilation)].transpose(2, 0, 1)
    scores = scores + bias.astype(jnp.float32)
    scores = jnp.where(valid[None, None, :, None], scores, NEG_INF)
    lse = jax.nn.logsumexp(scores, axis=-1)
    p = jnp.exp(scores - lse[..., None])
    out = jnp.einsum('brnhqk,brnkhd->brnqhd', p.astype(v.dtype), vb)
    out = out.reshape(B, dilation, Lp, H, hd)[:, :, :L]
    out = out.transpose(0, 2, 1, 3, 4).reshape(B, S, H, hd)
    lse = lse.transpose(0, 1, 2, 4, 3).reshape(B, dilation, Lp, H)[:, :, :L]
    lse = lse.transpose(0, 2, 1, 3).reshape(B, S, H)
    return out, lse

def axial_rope_tables(rows):
    row = jnp.repeat(jnp.arange(rows, dtype=jnp.float32), GRID_W)
    col = jnp.tile(jnp.arange(GRID_W, dtype=jnp.float32), rows)
    n_freq = HEAD_DIM_B // 4
    freq = ROPE_THETA ** (-jnp.arange(n_freq, dtype=jnp.float32) / n_freq)
    ang = jnp.concatenate([row[:, None] * freq, col[:, None] * freq], axis=-1)
    return jnp.cos(ang), jnp.sin(ang)

def apply_rope(x, cos, sin):
    xf = x.astype(jnp.float32).reshape(*x.shape[:-1], x.shape[-1] // 2, 2)
    x0, x1 = xf[..., 0], xf[..., 1]
    c = cos[None, :, None, :]
    s = sin[None, :, None, :]
    out = jnp.stack([x0 * c - x1 * s, x0 * s + x1 * c], axis=-1)
    return out.reshape(x.shape).astype(x.dtype)

def gqa_axial_attention(q, k, v, q_norm, k_norm, cos, sin):
    B, S = q.shape[0], q.shape[1]
    q = apply_rope(rmsnorm_2(q, q_norm), cos, sin)
    k = apply_rope(rmsnorm_2(k, k_norm), cos, sin)
    scale = HEAD_DIM_B ** -0.5
    qblocks = q.reshape(B, S // Q_BLOCK, Q_BLOCK, N_KV_B, GQA_GROUP_B, HEAD_DIM_B).swapaxes(0, 1)

    def attn_block(qb):
        s = jnp.einsum('bqkgd,bskd->bkgqs', qb, k, preferred_element_type=jnp.float32) * scale
        p = jax.nn.softmax(s, axis=-1)
        return jnp.einsum('bkgqs,bskd->bqkgd', p.astype(v.dtype), v)

    ob = lax.map(attn_block, qblocks)
    return ob.swapaxes(0, 1).reshape(B, S, B_Q_WIDTH)

def hybrid_mixer(h, w_in, b_gate, q_norm, k_norm, rel_bias, w_branch_a, w_branch_b, w_out, cos, sin):
    B, S, D = h.shape
    proj = h @ w_in
    o1 = A_QKV_WIDTH
    o2 = o1 + B_Q_WIDTH
    o3 = o2 + B_KV_WIDTH
    o4 = o3 + B_KV_WIDTH
    pa, pq, pk, pv, pg = proj[..., :o1], proj[..., o1:o2], proj[..., o2:o3], proj[..., o3:o4], proj[..., o4:]

    a = pa.reshape(B, S, 3, N_GROUPS_A, HEADS_PER_GROUP_A, HEAD_DIM_A)
    bias_groups = rel_bias.reshape(N_BUCKETS, N_GROUPS_A, HEADS_PER_GROUP_A)
    outs, lses = [], []
    for g, (window, dil) in enumerate(DILATED_GROUPS):
        o, lse = dilated_group_attention(a[:, :, 0, g], a[:, :, 1, g], a[:, :, 2, g],
                                         bias_groups[:, g], dil, window // (2 * dil))
        outs.append(o)
        lses.append(lse)
    wgt = jax.nn.softmax(jnp.stack(lses, axis=0), axis=0)
    o_a = jnp.sum(wgt[..., None] * jnp.stack(outs, axis=0).astype(jnp.float32), axis=0)
    o_a = o_a.astype(h.dtype).reshape(B, S, GROUP_WIDTH_A)

    o_b = gqa_axial_attention(pq.reshape(B, S, N_HEADS_B, HEAD_DIM_B),
                              pk.reshape(B, S, N_KV_B, HEAD_DIM_B),
                              pv.reshape(B, S, N_KV_B, HEAD_DIM_B),
                              q_norm, k_norm, cos, sin)

    gates = jax.nn.sigmoid((pg + b_gate).reshape(B, S, N_BRANCHES, D))
    merged = gates[:, :, 0] * (o_a @ w_branch_a) + gates[:, :, 1] * (o_b @ w_branch_b)
    return merged @ w_out

def second_inputs(seed: int = 0) -> dict:
    key = jax.random.key(seed)
    ks = jax.random.split(key, 24)
    f32 = jnp.float32

    def w(k, shape, fan_in):
        return jax.random.normal(k, shape, f32) * (fan_in ** -0.5)

    def gain(k, shape):
        return 1.0 + 0.05 * jax.random.normal(k, shape, f32)

    L, D = DEPTH_2, D_MODEL
    return {
        'x': jax.random.normal(ks[0], (BATCH, SEQ, D), f32),
        'ffn1_norm': gain(ks[1], (L, D)),
        'ffn1_w1': w(ks[2], (L, D, D_FF), D),
        'ffn1_w3': w(ks[3], (L, D, D_FF), D),
        'ffn1_w2': w(ks[4], (L, D_FF, D), D_FF),
        'mix_norm': gain(ks[5], (L, D)),
        'w_in': w(ks[6], (L, D, IN_WIDTH), D),
        'b_gate': 0.02 * jax.random.normal(ks[7], (L, GATE_WIDTH), f32),
        'q_norm': gain(ks[8], (L, HEAD_DIM_B)),
        'k_norm': gain(ks[9], (L, HEAD_DIM_B)),
        'rel_bias': 0.5 * jax.random.normal(ks[10], (N_BUCKETS, N_HEADS_A), f32),
        'w_branch_a': w(ks[11], (L, GROUP_WIDTH_A, D), GROUP_WIDTH_A),
        'w_branch_b': w(ks[12], (L, B_Q_WIDTH, D), B_Q_WIDTH),
        'w_out': w(ks[13], (L, D, D), D),
        'ffn2_norm': gain(ks[14], (L, D)),
        'ffn2_w1': w(ks[15], (L, D, D_FF), D),
        'ffn2_w3': w(ks[16], (L, D, D_FF), D),
        'ffn2_w2': w(ks[17], (L, D_FF, D), D_FF),
        'final_norm': gain(ks[18], (D,)),
    }

def second_block(x, ffn1_norm, ffn1_w1, ffn1_w3, ffn1_w2, mix_norm, w_in, b_gate, q_norm, k_norm,
              rel_bias, w_branch_a, w_branch_b, w_out, ffn2_norm, ffn2_w1, ffn2_w3, ffn2_w2,
              final_norm):
    S = x.shape[1]
    rows = S // GRID_W
    cos, sin = axial_rope_tables(rows)
    for l in range(DEPTH_2):
        x = x + 0.5 * swiglu_2(rmsnorm_2(x, ffn1_norm[l]), ffn1_w1[l], ffn1_w3[l], ffn1_w2[l])
        h = rmsnorm_2(x, mix_norm[l])
        x = x + hybrid_mixer(h, w_in[l], b_gate[l], q_norm[l], k_norm[l], rel_bias,
                             w_branch_a[l], w_branch_b[l], w_out[l], cos, sin)
        x = x + 0.5 * swiglu_2(rmsnorm_2(x, ffn2_norm[l]), ffn2_w1[l], ffn2_w3[l], ffn2_w2[l])
    return rmsnorm_2(x, final_norm)


def setup_inputs(seed=0):
    out = dict(first_inputs(seed))
    for name, value in second_inputs(seed + 1).items():
        if name != "x":
            out[name + "_2"] = value
    return out


def reference(
    x, norm_g, ffn_w_in, ffn_w_out, swa_w_qkv, swa_b_qkv, swa_sinks, swa_w_o, swa_b_o, gla_w_in,
    gla_w_gate2, gla_b_gate, gla_norm_g, gla_w_o, rwkv_mu, rwkv_w_rkv, rwkv_w0, rwkv_w1,
    rwkv_w2, rwkv_a0, rwkv_a1, rwkv_a2, rwkv_g1, rwkv_g2, rwkv_k_k, rwkv_k_a, rwkv_r_k,
    rwkv_lnx_g, rwkv_lnx_b, rwkv_w_o, ffn1_norm_2, ffn1_w1_2, ffn1_w3_2, ffn1_w2_2, mix_norm_2,
    w_in_2, b_gate_2, q_norm_2, k_norm_2, rel_bias_2, w_branch_a_2, w_branch_b_2, w_out_2,
    ffn2_norm_2, ffn2_w1_2, ffn2_w3_2, ffn2_w2_2, final_norm_2,
):
    x = first_block(
        x, norm_g, ffn_w_in, ffn_w_out, swa_w_qkv, swa_b_qkv, swa_sinks, swa_w_o, swa_b_o,
        gla_w_in, gla_w_gate2, gla_b_gate, gla_norm_g, gla_w_o, rwkv_mu, rwkv_w_rkv, rwkv_w0,
        rwkv_w1, rwkv_w2, rwkv_a0, rwkv_a1, rwkv_a2, rwkv_g1, rwkv_g2, rwkv_k_k, rwkv_k_a,
        rwkv_r_k, rwkv_lnx_g, rwkv_lnx_b, rwkv_w_o,
    )
    return second_block(
        x, ffn1_norm_2, ffn1_w1_2, ffn1_w3_2, ffn1_w2_2, mix_norm_2, w_in_2, b_gate_2, q_norm_2,
        k_norm_2, rel_bias_2, w_branch_a_2, w_branch_b_2, w_out_2, ffn2_norm_2, ffn2_w1_2,
        ffn2_w3_2, ffn2_w2_2, final_norm_2,
    )


_drawn_inputs = setup_inputs


def setup_inputs(seed=0):
    import zlib

    import numpy as np

    out = dict(_drawn_inputs(seed))
    spreads = {}
    factors = {'ffn1_norm_2': 6.814,
     'mix_norm_2': 8.0,
     'b_gate_2': 42.023,
     'q_norm_2': 8.0,
     'k_norm_2': 8.0,
     'rel_bias_2': 4.531,
     'ffn2_norm_2': 7.075}
    for name, (base, spread) in spreads.items():
        noise = np.random.default_rng([zlib.crc32(name.encode()), seed]).standard_normal(out[name].shape)
        drawn = base * np.exp(spread * noise) if base else spread * noise
        out[name] = jnp.asarray(drawn.astype(out[name].dtype))
    for name, factor in factors.items():
        out[name] = (out[name] * factor).astype(out[name].dtype)
    return out
```

```python
import concourse.bass as bass
from concourse import mybir
from contextlib import ExitStack

F32 = mybir.dt.float32
F32R = mybir.dt.float32r
ALU = mybir.AluOpType
ACT = mybir.ActivationFunctionType
AX = mybir.AxisListType.X

P = 128
SEQ = 256
NT = SEQ // P
D = 1024
KB = D // P
D_FF = 2816
FB = D_FF // P
EPS = 1e-6

RAW = 4
SPLIT = 2
IN_W = 2 * KB * P
SLOT = IN_W + D
ARRIVAL = 64
CH = 256
UNROLL = 4
LOOPS = (FB - 2) // UNROLL
MIX = 15528


class Stage:

    def __init__(self, kind, gain=None, norm=False, scale=1.0, bias=None, chunks=(), feature_major=False, dest=None,
                 evac=None, by=None, beside=None, loads=(), gate=None, up=None, down=None, kb=KB, src=None,
                 items=0, max_blocks=0, setup=None, pe=None, act=None, dve=None):
        self.kind, self.loads, self.setup = kind, list(loads), setup
        self.gain, self.norm, self.scale, self.bias = gain, norm, scale, bias
        self.chunks, self.feature_major, self.dest = chunks, feature_major, dest
        self.evac, self.by, self.beside = evac, by, beside
        self.gate, self.up, self.down = gate, up, down
        self.kb, self.src = kb, src
        self.items, self.max_blocks = items, max_blocks
        self.pe, self.act, self.dve = pe, act, dve
        self.units = FB + 1 if kind == "ffn" else len(chunks)


class Env:

    def __init__(self, nc, mix, y, xh, xl, silu, hidden, ident, ones, sq_scratch, out_bank, gate_bank, turn_bank,
                 link, link_act, named):
        self.nc, self.mix, self.y, self.xh, self.xl = nc, mix, y, xh, xl
        self.silu, self.hidden, self.ident, self.ones, self.sq_scratch = silu, hidden, ident, ones, sq_scratch
        self.out_bank, self.gate_bank, self.turn_bank = out_bank, gate_bank, turn_bank
        self.link, self.link_act, self.named = link, link_act, named


class Chunk:

    def __init__(self, kb, n, parts):
        self.kb, self.n, self.parts = kb, n, parts


def columns(w, lo, hi):
    v = w.rearrange("(k p) n -> p k n", p=P)
    return [Chunk(v.shape[1], min(CH, hi - c), [(0, v[:, :, c:min(c + CH, hi)])]) for c in range(lo, hi, CH)]


def spread(row):
    return row.partition_broadcast(P)


def along(ap, n):
    return ap.unsqueeze(2).to_broadcast([ap.shape[0], ap.shape[1], n])


def build(nc, io, out, stages):
    first = []
    u = 0
    for st in stages:
        first.append(u)
        u += st.units
    n_units = u
    evac_at, at = {}, 0
    count = {"pre": 0, "post": 0, "turn": 0, "ffn": 0}
    for s, st in enumerate(stages):
        st.at, st.u0 = s, first[s]
        st.e0 = at
        if st.kind == "proj" and st.dest == "gate":
            at += st.units
        st.nth = count.get(st.kind, 0)
        count[st.kind] = st.nth + 1
    pres = [st for st in stages if st.kind in ("pre", "post")]
    gained = [st for st in stages if st.kind in ("pre", "post") and st.gain is not None]
    for n, st in enumerate(gained):
        st.gain_slot, st.gain_at = n % 2, 16 * (n // 2 + 1)
    items = 0
    for st in stages:
        if st.kind == "attention":
            st.first_item = items
            items += st.items
    turns = 0
    for st in stages:
        if st.kind == "turn":
            st.fill0 = turns
            turns += NT * st.kb // 4

    ctx = ExitStack()
    with ctx:
        def sb(name, shape, dt=F32):
            return ctx.enter_context(nc.sbuf_tensor(name, shape, dt))

        def sem(name):
            return ctx.enter_context(nc.semaphore(name))

        raw = [sb(f"raw{i}", [P, SLOT]) for i in range(RAW)]
        high = [sb(f"high{i}", [P, SLOT], F32R) for i in range(SPLIT)]
        low = [sb(f"low{i}", [P, SLOT], F32R) for i in range(SPLIT)]
        h = sb("h", [P, NT, D])
        y = sb("y", [P, NT, D])
        xh = sb("xh", [P, KB, SEQ], F32R)
        xl = sb("xl", [P, KB, SEQ], F32R)
        gain = [sb(f"gain{i}", [P, D]) for i in range(2)]
        silu = sb("silu", [P, SEQ])
        hidden = sb("hidden", [P, SEQ])
        hid_h = [sb(f"hid_h{i}", [P, SEQ], F32R) for i in range(2)]
        hid_l = [sb(f"hid_l{i}", [P, SEQ], F32R) for i in range(2)]
        ident = sb("ident", [P, P])
        ones = sb("ones", [P, P])
        squares = sb("squares", [P, 2 * NT])
        ms = sb("ms", [P, NT])
        root = sb("root", [P, NT])
        rstd = sb("rstd", [P, NT])
        mix = sb("mix", [P, MIX])
        bank = [ctx.enter_context(nc.psum_tensor(f"bank{i}", [P, 512], F32)) for i in range(8)]
        out_bank, gate_bank, turn_bank = bank[0:4], bank[4:6], bank[6:8]

        arrived = [sem(f"weights_arrived{i}") for i in range(RAW)]
        high_ready = sem("high_ready")
        weights_split = sem("weights_split")
        weights_used = sem("weights_used")
        emptied = sem("emptied")
        silu_ready = sem("silu_ready")
        hidden_ready = sem("hidden_ready")
        gate_up_ready = sem("gate_up_ready")
        gain_loaded = [sem("gain0_loaded"), sem("gain1_loaded")]
        h_loaded = sem("h_loaded")
        consts_loaded = sem("consts_loaded")
        squares_ready = sem("squares_ready")
        root_ready = sem("root_ready")
        meansq_ready = sem("meansq_ready")
        turned = sem("turned")
        turned_high = sem("turned_high")
        turned_low = sem("turned_low")
        dve_link = sem("dve_link")
        act_link = sem("act_link")
        stored = sem("stored")
        done = {e: sem(f"stage_done_{e}") for e in ("pe", "act", "dve")}

        ident_zero = sem("ident_zero")
        ident_ready = sem("ident_ready")

        def next_unit(s):
            u = first[s] + stages[s].units
            return u if u < n_units else None

        def stage_of(u):
            return [st for st in stages if st.units and st.u0 <= u < st.u0 + st.units][0]

        def words(u):
            st = stage_of(u)
            if st.kind == "ffn":
                return IN_W if u == st.u0 else SLOT
            chunk = st.chunks[u - st.u0]
            return chunk.kb * chunk.n

        def barrier(eng, me, s):
            eng.drain().then_inc(done[me], 1)
            for e in ("pe", "act", "dve"):
                if e != me:
                    eng.wait_ge(done[e], s + 1)


        def split_high(act, u, w, turn=0):
            act.wait_ge(arrived[u % RAW], ARRIVAL * (u // RAW + 1) + ARRIVAL * turn)
            if u >= SPLIT:
                act.wait_ge(weights_used, u - SPLIT + 1 + UNROLL * turn)
            nc.scalar.activation(high[u % SPLIT][:, 0:w], raw[u % RAW][:, 0:w], ACT.Copy).then_inc(high_ready, 1)

        def split_low(dve, u, w, turn=0):
            dve.wait_ge(high_ready, u + 1 + UNROLL * turn)
            nc.vector.tensor_tensor(low[u % SPLIT][:, 0:w], raw[u % RAW][:, 0:w],
                                    high[u % SPLIT][:, 0:w].bitcast(F32), ALU.subtract).then_inc(weights_split, 1)

        def load_unit(sp, u, parts, turn=0):
            if u >= RAW or not isinstance(turn, int):
                sp.wait_ge(weights_split, u - RAW + 1 + UNROLL * turn)
            for n, (dst, src) in enumerate(parts):
                last = n == len(parts) - 1
                sp.dma_start(dst, src).then_inc(arrived[u % RAW], ARRIVAL - 16 * (len(parts) - 1) if last else 16)

        def ffn_parts(st, q, at, down_at):
            slot = raw[(st.u0 + q) % RAW]
            parts = []
            if q < FB:
                for n, w in enumerate((st.gate, st.up)):
                    parts.append((slot[:, n * D:(n + 1) * D].rearrange("p (k n) -> p k n", k=KB),
                                  w.rearrange("(k p) n -> p k n", p=P)[:, :, bass.ds(at, P)]))
            if q > 0:
                parts.append((slot[:, IN_W:SLOT], st.down[bass.ds(down_at, P), :]))
            return parts


        def ffn_pe(pe, st):
            def unit(q, turn=0):
                u = st.u0 + q
                H, L = high[u % SPLIT], low[u % SPLIT]
                f = st.nth * FB
                pe.wait_ge(weights_split, u + 1 + UNROLL * turn)
                if q < FB:
                    if f + q >= 2:
                        pe.wait_ge(hidden_ready, f + q - 1 + UNROLL * turn)
                    for n in range(2):
                        for k in range(KB):
                            w = slice((n * KB + k) * P, (n * KB + k + 1) * P)
                            o = gate_bank[q % 2][:, n * SEQ:(n + 1) * SEQ]
                            nc.tensor.matmul(o, H[:, w], xh[:, k, :], start=(k == 0), stop=False)
                            nc.tensor.matmul(o, H[:, w], xl[:, k, :], start=False, stop=False)
                            last = nc.tensor.matmul(o, L[:, w], xh[:, k, :], start=False, stop=(k == KB - 1))
                    last.then_inc(gate_up_ready, 1)
                if q > 0:
                    pe.wait_ge(hidden_ready, f + q + UNROLL * turn)
                    b = (q - 1) % 2
                    for t in range(NT):
                        tok = slice(t * P, (t + 1) * P)
                        for n in range(2):
                            o = out_bank[2 * t + n][:, :]
                            w = slice(IN_W + 512 * n, IN_W + 512 * (n + 1))
                            nc.tensor.matmul(o, hid_h[b][:, tok], H[:, w], start=(q == 1), stop=False)
                            nc.tensor.matmul(o, hid_h[b][:, tok], L[:, w], start=False, stop=False)
                            last = nc.tensor.matmul(o, hid_l[b][:, tok], H[:, w], start=False, stop=(q == FB))
                    last.then_inc(weights_used, 1)
                else:
                    pe.drain().then_inc(weights_used, 1)

            unit(0)
            unit(1)
            with pe.Fori(0, LOOPS) as i:
                for k in range(UNROLL):
                    unit(2 + k, i)
            unit(FB)

        def ffn_act(act, st):
            def unit(q, turn=0):
                if q < FB:
                    split_high(act, st.u0 + q + 1, SLOT, turn)
                    act.wait_ge(gate_up_ready, st.nth * FB + q + 1 + UNROLL * turn)
                    if st.nth * FB + q >= 1:
                        act.wait_ge(hidden_ready, st.nth * FB + q + UNROLL * turn)
                    nc.scalar.activation(silu[:, :], gate_bank[q % 2][:, 0:SEQ], ACT.Silu).then_inc(silu_ready, 1)
                elif next_unit(st.at) is not None:
                    split_high(act, next_unit(st.at), words(next_unit(st.at)))

            unit(0)
            unit(1)
            with act.Fori(0, LOOPS) as i:
                for k in range(UNROLL):
                    unit(2 + k, i)
            unit(FB)

        def ffn_dve(dve, st):
            def unit(q, turn=0):
                if q < FB:
                    split_low(dve, st.u0 + q + 1, SLOT, turn)
                    g = st.nth * FB + q
                    dve.wait_ge(silu_ready, g + 1 + UNROLL * turn)
                    nc.vector.tensor_tensor(hidden[:, :], silu[:, :], gate_bank[q % 2][:, SEQ:2 * SEQ],
                                            ALU.mult).then_inc(hidden_made, 1)
                    dve.wait_ge(hidden_made, g + 1 + UNROLL * turn)
                    if g >= 2:
                        dve.wait_ge(weights_used, st.u0 + q + UNROLL * turn)
                    nc.vector.tensor_copy(hid_h[q % 2][:, :], hidden[:, :]).then_inc(hidden_rounded, 1)
                    dve.wait_ge(hidden_rounded, g + 1 + UNROLL * turn)
                    nc.vector.tensor_tensor(hid_l[q % 2][:, :], hidden[:, :], hid_h[q % 2][:, :].bitcast(F32),
                                            ALU.subtract).then_inc(hidden_ready, 1)
                elif next_unit(st.at) is not None:
                    split_low(dve, next_unit(st.at), words(next_unit(st.at)))

            unit(0)
            unit(1)
            with dve.Fori(0, LOOPS) as i:
                for k in range(UNROLL):
                    unit(2 + k, i)
            unit(FB)

        hidden_made = sem("hidden_made")
        hidden_rounded = sem("hidden_rounded")

        def ffn_sync(sp, st):
            load_unit(sp, st.u0, ffn_parts(st, 0, 0, 0))
            load_unit(sp, st.u0 + 1, ffn_parts(st, 1, P, 0))
            for q in range(2, 2 + UNROLL):
                load_unit(sp, st.u0 + q, ffn_parts(st, q, q * P, (q - 1) * P))
            with sp.Fori(1, LOOPS) as i:
                for k in range(UNROLL):
                    q = 2 + k
                    load_unit(sp, st.u0 + q, ffn_parts(st, q, i * (UNROLL * P) + q * P, i * (UNROLL * P) + (q - 1) * P), i)
            load_unit(sp, st.u0 + FB, ffn_parts(st, FB, 0, (FB - 1) * P))


        def proj_pe(pe, st):
            for c, chunk in enumerate(st.chunks):
                u, kb, n = st.u0 + c, chunk.kb, chunk.n
                H, L = high[u % SPLIT], low[u % SPLIT]
                pe.wait_ge(weights_split, u + 1)
                if st.dest == "gate" and c >= 2:
                    pe.wait_ge(emptied, st.e0 + c - 1)
                groups = []
                if st.feature_major:
                    for f in range(n // P):
                        groups.append((gate_bank[c % 2][:, f * SEQ:(f + 1) * SEQ],
                                       [(W[:, k * n + f * P:k * n + (f + 1) * P], xx[:, k, :])
                                        for k in range(kb) for W, xx in ((H, xh), (H, xl), (L, xh))]))
                else:
                    for t in range(NT):
                        if st.dest == "gate":
                            o = gate_bank[c % 2][:, t * CH:t * CH + n]
                        else:
                            o = out_bank[2 * t + c // 2][:, (c % 2) * CH:(c % 2) * CH + n]
                        groups.append((o, [(xx[:, k, t * P:(t + 1) * P], W[:, k * n:(k + 1) * n])
                                           for k in range(kb) for xx, W in ((xh, H), (xh, L), (xl, H))]))
                for o, terms in groups:
                    for j, (a, b) in enumerate(terms):
                        last = nc.tensor.matmul(o, a, b, start=(j == 0), stop=(j == len(terms) - 1))
                last.then_inc(weights_used, 1)

        def proj_act(act, st):
            for c, chunk in enumerate(st.chunks):
                u = st.u0 + c
                if u + 1 < n_units:
                    split_high(act, u + 1, words(u + 1))
                if st.evac is not None and st.by == "act":
                    act.wait_ge(weights_used, u + 1)
                    st.evac(env, c, gate_bank[c % 2], chunk.n).then_inc(emptied, 1)

        def proj_dve(dve, st):
            if st.beside is not None:
                st.beside(env, dve)
            for c, chunk in enumerate(st.chunks):
                u = st.u0 + c
                if u + 1 < n_units:
                    split_low(dve, u + 1, words(u + 1))
                if st.evac is not None and st.by == "dve":
                    dve.wait_ge(weights_used, u + 1)
                    st.evac(env, c, gate_bank[c % 2], chunk.n).then_inc(emptied, 1)

        def proj_sync(sp, st):
            for c, chunk in enumerate(st.chunks):
                u = st.u0 + c
                slot = raw[u % RAW][:, 0:chunk.kb * chunk.n].rearrange("p (k n) -> p k n", k=chunk.kb)
                load_unit(sp, u, [(slot[:, :, at:at + src.shape[2]], src) for at, src in chunk.parts])


        links = [0]

        def link(dve, ins):
            links[0] += 1
            ins.then_inc(dve_link, 1)
            dve.wait_ge(dve_link, links[0])

        act_links = [0]

        def link_act(act, ins):
            act_links[0] += 1
            ins.then_inc(act_link, 1)
            act.wait_ge(act_link, act_links[0])

        squared, rooted = [0], [0]

        def load_gain(act, st):
            act.dma_start(gain[st.gain_slot][:, :], spread(st.gain)).then_inc(gain_loaded[st.gain_slot], 16)

        def norm_act(act, parts, load_next):
            if load_next:
                load_next()
            for n, part in enumerate(parts):
                if squared[0] + n:
                    act.wait_ge(squares_ready, squared[0] + n)
                nc.scalar.activation(scratch(n, part), part, ACT.Square, accum_out=squares[:, n:n + 1]).then_inc(squares_ready, 1)
            squared[0] += len(parts)
            rooted[0] += 1
            act.wait_ge(meansq_ready, rooted[0])
            nc.scalar.activation(root[:, :], ms[:, :], ACT.Sqrt).then_inc(root_ready, 1)

        sq_out = [y[:, 0, :], y[:, 1, :]]

        def scratch(n, part):
            w = part.shape[-1]
            return sq_scratch[:, 0:w]

        sq_scratch = sb("sq_scratch", [P, D])

        nsq, nroot = [0], [0]

        def norm_dve(dve, n_parts, scale):
            nsq[0] += n_parts
            dve.wait_ge(squares_ready, nsq[0])
            if n_parts == 2 * NT:
                sq = squares[:, :].rearrange("p (t n) -> p t n", t=NT)
                link(dve, nc.vector.tensor_tensor(ms[:, :], sq[:, :, 0], sq[:, :, 1], ALU.add))
                nc.vector.tensor_scalar(ms[:, :], ms[:, :], 1.0 / D, EPS, ALU.mult, ALU.add).then_inc(meansq_ready, 1)
            else:
                nc.vector.tensor_scalar(ms[:, :], squares[:, 0:NT], 1.0 / D, EPS, ALU.mult, ALU.add).then_inc(meansq_ready, 1)
            nroot[0] += 1
            dve.wait_ge(root_ready, nroot[0])
            link(dve, nc.vector.reciprocal(rstd[:, :], root[:, :]))
            if scale != 1.0:
                link(dve, nc.vector.tensor_scalar(rstd[:, :], rstd[:, :], scale, None, ALU.mult))

        def pre_act(act, st):
            norm_act(act, [h[:, t, :] for t in range(NT)], lambda: next_gain(act, st))

        def next_gain(act, st):
            n = gained.index(st) if st in gained else None
            if n is not None and n + 1 < len(gained):
                load_gain(act, gained[n + 1])

        def pre_dve(dve, st):
            norm_dve(dve, NT, 1.0)
            dve.wait_ge(gain_loaded[st.gain_slot], st.gain_at)
            for t in range(NT):
                nc.vector.scalar_tensor_tensor(y[:, t, :], h[:, t, :], rstd[:, t:t + 1], gain[st.gain_slot][:, :],
                                               ALU.mult, ALU.mult)

        def branch_parts(st):
            if st.bias is not None:
                return [y[:, t, n * 512:(n + 1) * 512] for t in range(NT) for n in range(2)]
            return [out_bank[2 * t + n][:, :] for t in range(NT) for n in range(2)]

        biased = sem("biased")
        post_biases = [0, 0]

        def post_act(act, st):
            if st.norm:
                if st.bias is not None:
                    post_biases[0] += 1
                    act.wait_ge(biased, post_biases[0])
                norm_act(act, branch_parts(st), lambda: next_gain(act, st))

        def post_dve(dve, st):
            if st.bias is not None:
                for t in range(NT):
                    for n in range(2):
                        last = nc.vector.tensor_tensor(y[:, t, n * 512:(n + 1) * 512], out_bank[2 * t + n][:, :],
                                                       st.bias[:, n * 512:(n + 1) * 512], ALU.add)
                last.then_inc(biased, 1)
            if st.norm:
                norm_dve(dve, 2 * NT, st.scale)
                dve.wait_ge(gain_loaded[st.gain_slot], st.gain_at)
                for j, part in enumerate(branch_parts(st)):
                    t, n = j // 2, j % 2
                    link(dve, nc.vector.scalar_tensor_tensor(y[:, t, n * 512:(n + 1) * 512], part, rstd[:, t:t + 1],
                                                             gain[st.gain_slot][:, n * 512:(n + 1) * 512],
                                                             ALU.mult, ALU.mult))
                nc.vector.tensor_tensor(h[:, :, :], h[:, :, :], y[:, :, :], ALU.add)
            else:
                for j, part in enumerate(branch_parts(st)):
                    t, n = j // 2, j % 2
                    hp = h[:, t, n * 512:(n + 1) * 512]
                    nc.vector.scalar_tensor_tensor(hp, part, st.scale, hp, ALU.mult, ALU.add)


        def turn_fills(st):
            return [(t, g) for t in range(NT) for g in range(st.kb // 4)]

        def turn_pe(pe, st):
            for x, (t, g) in enumerate(turn_fills(st)):
                f = st.fill0 + x
                if x >= 2:
                    pe.wait_ge(turned_low, f - 1)
                for b in range(4):
                    k = 4 * g + b
                    last = nc.tensor.transpose(turn_bank[x % 2][:, b * P:(b + 1) * P],
                                               (y if st.src is None else st.src(mix))[:, t, k * P:(k + 1) * P],
                                               ident[:, :])
                last.then_inc(turned, 1)

        def turn_act(act, st):
            for x, (t, g) in enumerate(turn_fills(st)):
                act.wait_ge(turned, st.fill0 + x + 1)
                nc.scalar.activation(xh[:, 4 * g:4 * g + 4, t * P:(t + 1) * P],
                                     turn_bank[x % 2][:, :].rearrange("p (k n) -> p k n", k=4), ACT.Copy).then_inc(turned_high, 1)

        def turn_dve(dve, st):
            for x, (t, g) in enumerate(turn_fills(st)):
                dve.wait_ge(turned_high, st.fill0 + x + 1)
                nc.vector.tensor_tensor(xl[:, 4 * g:4 * g + 4, t * P:(t + 1) * P],
                                        turn_bank[x % 2][:, :].rearrange("p (k n) -> p k n", k=4),
                                        xh[:, 4 * g:4 * g + 4, t * P:(t + 1) * P].bitcast(F32), ALU.subtract).then_inc(turned_low, 1)


        att = {n: sem("att_" + n) for n in ("scores", "max", "probs", "turned", "copied", "values", "out")}

        def att_bank(st, i, c):
            return out_bank[2 * (i % 2) + c // 512], c % 512

        def att_pe(pe, st):
            a0, n, NK = st.first_item, st.items, st.max_blocks
            for step in range(n + 2):
                i = step
                if i < n:
                    if a0 + i >= 2:
                        pe.wait_ge(att["max"], a0 + i - 1)
                    for c, q, k in st.item(i).scores:
                        b, c0 = att_bank(st, i, c)
                        last = nc.tensor.matmul(b[:, c0:c0 + k.shape[-1]], q, k, start=True, stop=True)
                    last.then_inc(att["scores"], 1)
                i = step - 1
                if 0 <= i < n:
                    pe.wait_ge(att["probs"], a0 + i + 1)
                    free = a0 + i - (0 if NK > 4 else 1)
                    if free > 0:
                        pe.wait_ge(att["copied"], free)
                    for b in range(len(st.item(i).values)):
                        bank_ = turn_bank[b // 4 if NK > 4 else i % 2]
                        last = nc.tensor.transpose(bank_[:, (b % 4) * P:(b % 4 + 1) * P],
                                                   st.probs(i)[:, b * P:(b + 1) * P], ident[:, :])
                    last.then_inc(att["turned"], 1)
                i = step - 2
                if 0 <= i < n:
                    pe.wait_ge(att["copied"], a0 + i + 1)
                    if a0 + i >= 2:
                        pe.wait_ge(att["out"], a0 + i - 1)
                    vs = st.item(i).values
                    for b, v in enumerate(vs):
                        last = nc.tensor.matmul(gate_bank[i % 2][:, 0:v.shape[-1]], st.turned(i)[:, b * P:(b + 1) * P],
                                                v, start=(b == 0), stop=(b == len(vs) - 1))
                    last.then_inc(att["values"], 1)

        def att_act(act, st):
            a0, n = st.first_item, st.items
            for step in range(n + 1):
                i = step
                if i < n:
                    it = st.item(i)
                    if st.load_bias is not None and i == 0:
                        st.load_bias(act, 0)
                        st.load_bias(act, 1)
                    act.wait_ge(att["max"], a0 + i + 1)
                    if st.load_bias is not None and i + 2 < n:
                        st.load_bias(act, i + 2)
                    if st.sink is not None:
                        nc.scalar.activation(st.sink_e[:, i:i + 1], st.sink(i), ACT.Exp, bias=st.negmax[:, i:i + 1])
                    nc.scalar.activation(st.probs(i)[:, 0:it.keys], st.probs(i)[:, 0:it.keys], ACT.Exp,
                                         bias=st.negmax[:, i:i + 1], scale=st.scale,
                                         accum_out=st.sums[:, i:i + 1]).then_inc(att["probs"], 1)
                i = step - 1
                if 0 <= i < n:
                    act.wait_ge(att["turned"], a0 + i + 1)
                    if a0 + i >= 2:
                        act.wait_ge(att["values"], a0 + i - 1)
                    nb = len(st.item(i).values)
                    for g in range(0, nb, 4):
                        m = min(4, nb - g)
                        bank_ = turn_bank[g // 4 if st.max_blocks > 4 else i % 2]
                        last = nc.scalar.activation(st.turned(i)[:, g * P:(g + m) * P], bank_[:, 0:m * P], ACT.Copy)
                    last.then_inc(att["copied"], 1)

        def att_dve(dve, st):
            a0, n = st.first_item, st.items
            for step in range(n + 2):
                i = step
                if i < n:
                    it = st.item(i)
                    if a0 + i >= 2:
                        dve.wait_ge(att["turned"], a0 + i - 1)
                    if st.before is not None:
                        st.before(dve, i)
                    dve.wait_ge(att["scores"], a0 + i + 1)
                    for c in range(0, it.keys, 512):
                        w = min(512, it.keys - c)
                        b, _ = att_bank(st, i, c)
                        dst = st.probs(i)[:, c:c + w]
                        if it.bias is None:
                            last = nc.vector.tensor_copy(dst, b[:, 0:w])
                        else:
                            last = nc.vector.tensor_tensor(dst, b[:, 0:w], it.bias[:, c:c + w], ALU.add)
                    link(dve, last)
                    nm = st.negmax[:, i:i + 1]
                    ins = nc.vector.tensor_reduce(nm, st.probs(i)[:, 0:it.keys], AX.X, ALU.max, negate=True)
                    if st.scale != 1.0:
                        link(dve, ins)
                        ins = nc.vector.tensor_scalar(nm, nm, st.scale, None, ALU.mult)
                    if st.sink is not None:
                        link(dve, ins)
                        ins = nc.vector.tensor_tensor(nm, nm, st.negsink(i), ALU.min)
                    ins.then_inc(att["max"], 1)
                i = step - 2
                if 0 <= i < n:
                    sm = st.sums[:, i:i + 1]
                    dve.wait_ge(att["values"], a0 + i + 1)
                    if st.sink is not None:
                        link(dve, nc.vector.tensor_tensor(sm, sm, st.sink_e[:, i:i + 1], ALU.add))
                    link(dve, nc.vector.reciprocal(sm, sm))
                    it = st.item(i)
                    nc.vector.tensor_scalar(it.out, gate_bank[i % 2][:, 0:it.out.shape[-1]], sm, None,
                                            ALU.mult).then_inc(att["out"], 1)

        own_sems = {}

        def named(name):
            if name not in own_sems:
                own_sems[name] = sem(name)
            return own_sems[name]

        env = Env(nc, mix, y, xh, xl, silu, hidden, ident, ones, sq_scratch, out_bank, gate_bank, turn_bank,
                  link, link_act, named)
        for st in stages:
            if st.setup is not None:
                st.setup(env, st)
            if st.kind == "post" and st.bias is not None:
                st.bias = st.bias(mix)

        final = y[:, :, :] if stages[-1].kind == "pre" else h[:, :, :]
        block = ctx.enter_context(nc.Block())

        @block.sync
        def _(sp):
            sp.dma_start(h[:, :, :], io["x"][0].rearrange("(t p) d -> p t d", p=P)).then_inc(h_loaded, 16)
            for st in stages:
                if st.kind == "ffn":
                    ffn_sync(sp, st)
                elif st.kind == "proj":
                    proj_sync(sp, st)
            sp.wait_ge(done["dve"], len(stages))
            sp.dma_start(out[0].rearrange("(t p) d -> p t d", p=P), final).then_inc(stored, 16)
            sp.wait_ge(stored, 16)


        @block.gpsimd
        def _(pool):
            nc.gpsimd.memset(ones[:, :], 1.0).then_inc(ident_ready, 1)
            nc.gpsimd.memset(ident[:, :], 0.0).then_inc(ident_zero, 1)
            pool.wait_ge(ident_zero, 1)
            nc.gpsimd.affine_select(out=ident[:, :], in_=ident[:, :], compare_op=ALU.not_equal, fill=1.0,
                                    base=0, pattern=[[-1, P]], channel_multiplier=1).then_inc(ident_ready, 1)

        @block.scalar
        def _(act):
            load_gain(act, gained[0])
            act.wait_ge(h_loaded, 16)
            split_high(act, 0, words(0))
            n_loads = 0
            for s, st in enumerate(stages):
                for dst, src in st.loads:
                    if dst == "halves":
                        dst = lambda mix: sq_scratch[:, 0:7 * P].rearrange("p (n s) -> p n s", n=7)
                    act.dma_start(dst(mix), src, allow_slow_non_contiguous=True).then_inc(consts_loaded, 16)
                {"load": lambda e, st: None, "ffn": ffn_act, "proj": proj_act, "pre": pre_act, "post": post_act, "turn": turn_act, "attention": att_act,
                 "mixer": lambda e, st: st.act(env, e) if st.act else None}[st.kind](act, st)
                if st.loads:
                    n_loads += len(st.loads)
                    act.wait_ge(consts_loaded, 16 * n_loads)
                barrier(act, "act", s)

        @block.vector
        def _(dve):
            dve.wait_ge(h_loaded, 16)
            split_low(dve, 0, words(0))
            for s, st in enumerate(stages):
                {"load": lambda e, st: None, "ffn": ffn_dve, "proj": proj_dve, "pre": pre_dve, "post": post_dve, "turn": turn_dve, "attention": att_dve,
                 "mixer": lambda e, st: st.dve(env, e) if st.dve else None}[st.kind](dve, st)
                barrier(dve, "dve", s)

        @block.tensor
        def _(pe):
            pe.wait_ge(ident_ready, 2)
            for s, st in enumerate(stages):
                if st.kind in ("ffn", "proj", "turn", "attention"):
                    {"ffn": ffn_pe, "proj": proj_pe, "turn": turn_pe, "attention": att_pe}[st.kind](pe, st)
                elif st.kind == "mixer" and st.pe:
                    st.pe(env, pe)
                barrier(pe, "pe", s)



HEADS, KV, HD = 16, 4, 64
WINDOW = 128


class Mix:

    def __init__(self, at=0):
        self.at = at

    def take(self, n, shape=None):
        lo = self.at
        self.at += n
        assert self.at <= MIX, self.at

        def place(mix, part=slice(0, P)):
            ap = mix[part, lo:lo + n]
            if shape is not None:
                ap = ap.rearrange("p (a b) -> p a b", a=shape[0])
            return ap
        return place


class Item:
    def __init__(self, scores, keys, bias, values, out):
        self.scores, self.keys, self.bias, self.values, self.out = scores, keys, bias, values, out


def swa(io, j, pre_gain, post_gain):
    w, b = io["swa_w_qkv"][j], io["swa_b_qkv"][j]
    NQ = HEADS * HD
    m = Mix()
    qf = m.take(HEADS // 2 * SEQ, (HEADS // 2, SEQ))
    kf = m.take(KV * SEQ, (KV, SEQ))
    v = m.take(NT * KV * HD, (NT, KV * HD))
    scores = [m.take(SEQ) for _ in range(2)]
    turned = [m.take(SEQ) for _ in range(2)]
    bq, bk = m.take(HEADS // 2), m.take(KV)
    sinks, negsinks = m.take(HEADS), m.take(HEADS)
    negmax, sums, sink_e = m.take(NT * HEADS), m.take(NT * HEADS), m.take(NT * HEADS)
    mask, bv, bo = m.take(SEQ), m.take(KV * HD), m.take(D)
    loads = [(bq, b[0:NQ].rearrange("(c p) -> p c", p=P)),
             (lambda mix: bk(mix, slice(0, HD)), b[NQ:NQ + KV * HD].rearrange("(c p) -> p c", p=HD)),
             (lambda mix: bk(mix, slice(HD, P)), b[NQ:NQ + KV * HD].rearrange("(c p) -> p c", p=HD)),
             (bv, spread(b[NQ + KV * HD:NQ + 2 * KV * HD])),
             (bo, spread(io["swa_b_o"][j])),
             (sinks, spread(io["swa_sinks"][j])),
             (mask, io["c_window"])]
    wk = w.rearrange("(k p) n -> p k n", p=P)
    k_chunks = [Chunk(KB, CH, [(HD * a, wk[:, :, NQ + HD * g:NQ + HD * (g + 1)])
                               for a, g in enumerate((2 * c, 2 * c, 2 * c + 1, 2 * c + 1))]) for c in range(KV // 2)]

    def evac_q(e, c, bank, n):
        for f in range(2):
            last = e.nc.vector.tensor_scalar(qf(e.mix)[:, 2 * c + f, :], bank[:, f * SEQ:(f + 1) * SEQ],
                                             bq(e.mix)[:, 2 * c + f:2 * c + f + 1], HD ** -0.5, ALU.add, ALU.mult)
        return last

    def evac_k(e, c, bank, n):
        for f in range(2):
            last = e.nc.vector.tensor_scalar(kf(e.mix)[:, 2 * c + f, :], bank[:, f * SEQ:(f + 1) * SEQ],
                                             bk(e.mix)[:, 2 * c + f:2 * c + f + 1], None, ALU.add)
        return last

    def evac_v(e, c, bank, n):
        for t in range(NT):
            last = e.nc.vector.tensor_tensor(v(e.mix)[:, t, :], bank[:, t * CH:t * CH + n], bv(e.mix), ALU.add)
        return last

    def setup(e, st):
        mix = e.mix

        def item(i):
            t, hd = i // HEADS, i % HEADS
            rows = slice(HD * (hd % 2), HD * (hd % 2) + HD)
            g = hd // (HEADS // KV)
            keys = P * (t + 1)
            return Item([(0, qf(mix, rows)[:, hd // 2, t * P:(t + 1) * P], kf(mix, rows)[:, g, 0:keys])], keys,
                        mask(mix)[:, SEQ - keys:SEQ], [v(mix)[:, s, g * HD:(g + 1) * HD] for s in range(t + 1)],
                        e.y[:, t, hd * HD:(hd + 1) * HD])

        def before(dve, i):
            if i == 0:
                e.link(dve, e.nc.vector.tensor_scalar(negsinks(mix), sinks(mix), -1.0, None, ALU.mult))

        st.item, st.before, st.load_bias = item, before, None
        st.probs = lambda i: scores[i % 2](mix)
        st.turned = lambda i: turned[i % 2](mix)
        st.negmax, st.sums, st.sink_e = negmax(mix), sums(mix), sink_e(mix)
        st.sink = lambda i: sinks(mix)[:, i % HEADS:i % HEADS + 1]
        st.negsink = lambda i: negsinks(mix)[:, i % HEADS:i % HEADS + 1]

    stages = [Stage("pre", gain=pre_gain), Stage("turn", kb=KB),
              Stage("proj", chunks=columns(w, 0, NQ), feature_major=True, dest="gate", evac=evac_q, by="dve"),
              Stage("proj", chunks=k_chunks, feature_major=True, dest="gate", evac=evac_k, by="dve"),
              Stage("proj", chunks=columns(w, NQ + KV * HD, NQ + 2 * KV * HD), feature_major=False, dest="gate",
                    evac=evac_v, by="dve"),
              Stage("attention", items=NT * HEADS, max_blocks=NT, scale=1.0, setup=setup),
              Stage("turn", kb=KB),
              Stage("proj", chunks=columns(io["swa_w_o"][j], 0, D), feature_major=False, dest="out", evac=None),
              Stage("post", gain=post_gain, norm=True, scale=1.0, bias=bo)]
    return loads, stages


def step(pe=None, act=None, dve=None):
    return Stage("mixer", pe=pe, act=act, dve=dve)



G_HEADS, G_DK, G_DV, G_RANK = 4, 128, 256, 16
G_TEMP = 16.0
G_EPS = 1e-5
G_LEVELS = [P >> n for n in range(8)]


def gla(io, pre_gain, post_gain):
    w = io["gla_w_in"][0]
    QK, V = G_HEADS * G_DK, G_HEADS * G_DV
    m = Mix()
    qf, kf, b = (m.take(G_HEADS * SEQ, (G_HEADS, SEQ)) for _ in range(3))
    v, gate = m.take(NT * V, (NT, V)), m.take(NT * V, (NT, V))
    z = m.take(G_HEADS * SEQ, (G_HEADS, SEQ))
    weights = z
    far = m.take(G_HEADS * P, (G_HEADS, P))
    decay = [m.take(G_HEADS * SEQ, (G_HEADS, SEQ)) for _ in range(2)]
    ke = [m.take(G_HEADS * SEQ, (G_HEADS, SEQ)) for _ in range(2)]
    masks = m.take(8 * P, (8, P))
    ng, bg, w2 = m.take(G_DV), m.take(G_HEADS), m.take(QK)
    low, low_t, ones = m.take(NT * G_RANK, (NT, G_RANK)), m.take(SEQ), m.take(SEQ)
    sq, mean, rt = m.take(8), m.take(8), m.take(8)
    loads = [(masks, io["c_levels"]), (ng, spread(io["gla_norm_g"][0])),
             (bg, io["gla_b_gate"][0].rearrange("(c p) -> p c", p=P)),
             (lambda mix: w2(mix, slice(0, G_RANK)), io["gla_w_gate2"][0])]

    def evac_feature(dst, scale):
        def evac(e, c, bank, n):
            return e.nc.scalar.activation(dst(e.mix)[:, 2 * c:2 * c + 2, :],
                                          bank[:, :].rearrange("p (f n) -> p f n", f=2), ACT.Copy, scale=scale)
        return evac

    def evac_token(dst, func):
        def evac(e, c, bank, n):
            return e.nc.scalar.activation(dst(e.mix)[:, :, c * CH:c * CH + n],
                                          bank[:, :].rearrange("p (t n) -> p t n", t=NT)[:, :, 0:n], func)
        return evac

    def proj(lo, hi, dst, func=ACT.Copy, feature_major=False, scale=1.0):
        return Stage("proj", chunks=columns(w, lo, hi), feature_major=feature_major, dest="gate", by="act",
                     evac=evac_feature(dst, scale) if feature_major else evac_token(dst, func))

    def low_pe(e, pe):
        for t in range(NT):
            e.nc.tensor.transpose(e.turn_bank[0][0:G_RANK, t * P:(t + 1) * P], low(e.mix)[:, t, :], e.ident[:, :])

    def low_dve(e, dve):
        e.nc.vector.memset(ones(e.mix), 1.0)
        e.nc.vector.tensor_copy(low_t(e.mix, slice(0, G_RANK)), e.turn_bank[0][0:G_RANK, 0:SEQ])

    def z_pe(e, pe):
        for hd in range(G_HEADS):
            e.nc.tensor.matmul(e.out_bank[hd // 2][:, (hd % 2) * SEQ:(hd % 2 + 1) * SEQ],
                               w2(e.mix, slice(0, G_RANK))[:, hd * P:(hd + 1) * P], low_t(e.mix, slice(0, G_RANK)),
                               start=True, stop=True)

    def z_dve(e, dve):
        for hd in range(G_HEADS):
            e.nc.vector.tensor_scalar(z(e.mix)[:, hd, :], e.out_bank[hd // 2][:, (hd % 2) * SEQ:(hd % 2 + 1) * SEQ],
                                      bg(e.mix)[:, hd:hd + 1], None, ALU.add)

    def soft_act(e, act):
        t = decay[0](e.mix)
        e.link_act(act, e.nc.scalar.activation(t, z(e.mix), ACT.Abs))
        e.link_act(act, e.nc.scalar.activation(t, t, ACT.Exp, scale=-1.0))
        e.nc.scalar.activation(t, t, ACT.Ln, bias=1.0)

    def sum_dve(e, dve):
        g = ke[0](e.mix)
        e.link(dve, e.nc.vector.scalar_tensor_tensor(g, z(e.mix), 0.0, decay[0](e.mix), ALU.min, ALU.subtract))
        for hd in range(G_HEADS):
            e.nc.vector.tensor_tensor_scan(b(e.mix)[:, hd, :], ones(e.mix), g[:, hd, :], 0.0, ALU.mult, ALU.add)

    def blocks(ap, size):
        return ap.rearrange("p h (x s) -> p (h x) s", s=size)

    n_levels = len(G_LEVELS)
    QE = lambda e, l: e.y[:, l % 2, :].rearrange("p (h s) -> p h s", h=G_HEADS)

    def level_pe(e, pe):
        for l in range(n_levels + 1):
            pe.wait_ge(e.named("gla_scaled"), min(l + 1, n_levels))
            if l >= 2:
                pe.wait_ge(e.named("gla_added"), l - 1)
            q, k = (QE(e, l), ke[l % 2](e.mix)) if l < n_levels else (qf(e.mix), kf(e.mix))
            for hd in range(G_HEADS):
                for t in range(1 if l == 0 else NT):
                    x = hd if l == 0 else t * G_HEADS + hd
                    i = slice(P, 2 * P) if l == 0 else slice(t * P, (t + 1) * P)
                    last = e.nc.tensor.matmul(e.out_bank[2 * (l % 2) + x // 4][:, (x % 4) * P:(x % 4 + 1) * P],
                                              k[:, hd, t * P:(t + 1) * P], q[:, hd, i], start=True, stop=True)
            last.then_inc(e.named("gla_products"), 1)

    def level_act(e, act):
        for l in range(n_levels):
            act.wait_ge(e.named("gla_distance"), l + 1)
            d = decay[l % 2](e.mix)
            e.link_act(act, e.nc.scalar.activation(d, d, ACT.Abs))
            e.nc.scalar.activation(d, d, ACT.Exp, scale=-1.0 / G_TEMP).then_inc(e.named("gla_decay"), 1)

    def level_dve(e, dve):
        for l in range(-1, n_levels + 2):
            if 0 <= l + 1 < n_levels:
                mm = G_LEVELS[l + 1]
                bv = blocks(b(e.mix), 2 * mm)
                e.nc.vector.tensor_tensor(blocks(decay[(l + 1) % 2](e.mix), 2 * mm), bv,
                                          bv[:, :, mm - 1:mm].to_broadcast([P, bv.shape[1], 2 * mm]),
                                          ALU.subtract).then_inc(e.named("gla_distance"), 1)
            if 0 <= l < n_levels:
                dve.wait_ge(e.named("gla_decay"), l + 1)
                if l >= 2:
                    dve.wait_ge(e.named("gla_products"), l - 1)
                e.nc.vector.tensor_tensor(QE(e, l), qf(e.mix), decay[l % 2](e.mix), ALU.mult)
                e.nc.vector.tensor_tensor(ke[l % 2](e.mix), kf(e.mix), decay[l % 2](e.mix),
                                          ALU.mult).then_inc(e.named("gla_scaled"), 1)
                if l + 2 < n_levels:
                    dve.wait_ge(e.named("gla_scaled"), l + 1)
            if 0 <= l - 1 <= n_levels:
                n = l - 1
                dve.wait_ge(e.named("gla_products"), n + 1)
                if n == 0:
                    e.nc.vector.tensor_copy(far(e.mix), e.out_bank[0][:, :].rearrange("p (h n) -> p h n", h=4)).then_inc(e.named("gla_added"), 1)
                    continue
                sv = weights(e.mix).rearrange("p h (t n) -> p (h t) n", t=NT)
                mk = masks(e.mix)[:, n - 1:n, :].to_broadcast([P, 4, P])
                for part in range(2):
                    bank = e.out_bank[2 * (n % 2) + part][:, :].rearrange("p (h n) -> p h n", h=4)
                    dst = sv[:, 4 * part:4 * part + 4, :]
                    if n == 1:
                        last = e.nc.vector.tensor_tensor(dst, bank, mk, ALU.mult)
                    else:
                        tmp = e.sq_scratch[:, 512 * part:512 * part + 512].rearrange("p (h n) -> p h n", h=4)
                        e.link(dve, e.nc.vector.tensor_tensor(tmp, bank, mk, ALU.mult))
                        last = e.nc.vector.tensor_tensor(dst, dst, tmp, ALU.add)
                last.then_inc(e.named("gla_added"), 1)
                dve.wait_ge(e.named("gla_added"), n + 1)

    def value_pe(e, pe):
        sv = weights(e.mix).rearrange("p h (t n) -> p (h t) n", t=NT)
        for t in range(NT):
            for hd in range(G_HEADS):
                x = t * G_HEADS + hd
                o = e.out_bank[x // 2][:, (x % 2) * G_DV:(x % 2 + 1) * G_DV]
                cols = slice(hd * G_DV, (hd + 1) * G_DV)
                if t == 1:
                    e.nc.tensor.matmul(o, far(e.mix)[:, hd, :], v(e.mix)[:, 0, cols], start=True, stop=False)
                e.nc.tensor.matmul(o, sv[:, x, :], v(e.mix)[:, t, cols], start=(t == 0), stop=True)

    def heads_of(e):
        return [e.out_bank[x // 2][:, (x % 2) * G_DV:(x % 2 + 1) * G_DV] for x in range(NT * G_HEADS)]

    def sq_act(e, act):
        for x, o in enumerate(heads_of(e)):
            e.link_act(act, e.nc.scalar.activation(e.sq_scratch[:, 0:G_DV], o, ACT.Square, accum_out=sq(e.mix)[:, x:x + 1]))

    def mean_dve(e, dve):
        e.nc.vector.tensor_scalar(mean(e.mix), sq(e.mix), 1.0 / G_DV, G_EPS, ALU.mult, ALU.add)

    def root_act(e, act):
        e.nc.scalar.activation(rt(e.mix), mean(e.mix), ACT.Sqrt)

    def out_dve(e, dve):
        e.link(dve, e.nc.vector.reciprocal(rt(e.mix), rt(e.mix)))
        for x, o in enumerate(heads_of(e)):
            t, hd = x // G_HEADS, x % G_HEADS
            last = e.nc.vector.scalar_tensor_tensor(e.y[:, t, hd * G_DV:(hd + 1) * G_DV], o, rt(e.mix)[:, x:x + 1],
                                                    ng(e.mix), ALU.mult, ALU.mult)
        e.link(dve, last)
        e.nc.vector.tensor_tensor(e.y[:, :, :], e.y[:, :, :], gate(e.mix), ALU.mult)

    stages = [Stage("pre", gain=pre_gain), Stage("turn", kb=KB),
              proj(0, QK, qf, feature_major=True, scale=G_DK ** -0.5), proj(QK, 2 * QK, kf, feature_major=True),
              proj(2 * QK, 2 * QK + V, v), proj(2 * QK + V, 2 * QK + 2 * V, gate, ACT.Silu),
              proj(2 * QK + 2 * V, 2 * QK + 2 * V + G_RANK, low),
              step(pe=low_pe), step(dve=low_dve), step(pe=z_pe), step(dve=z_dve), step(act=soft_act), step(dve=sum_dve),
              step(level_pe, level_act, level_dve), step(pe=value_pe), step(act=sq_act), step(dve=mean_dve),
              step(act=root_act), step(dve=out_dve),
              Stage("turn", kb=KB),
              Stage("proj", chunks=columns(io["gla_w_o"][0], 0, D), feature_major=False, dest="out", evac=None),
              Stage("post", gain=post_gain, norm=True, scale=1.0, bias=None)]
    return loads, stages


def level_masks():
    import numpy as np
    j, i = np.arange(P)[:, None], np.arange(P)[None, :]
    out = [((j // (2 * m) == i // (2 * m)) & (j // m < i // m)) for m in G_LEVELS[1:]] + [j == i]
    return np.stack(out, 1).astype(np.float32)



R_HEADS, R_HD = 16, 64
R_PAIRS = R_HEADS // 2
KAPPA = 0.6065306597126334
R_LEVELS = [1 << n for n in range(7)]
LNX_EPS = 64e-5
MID = P // 2 - 1


def rwkv_constants():
    import numpy as np
    f = np.arange(P)
    s, t = f[:, None], f[None, :]
    order = np.stack([s < t, s <= t], 1).astype(np.float32)
    halves = np.stack([(s // (2 * m) == t // (2 * m)) & (s // m < t // m) for m in R_LEVELS], 1).astype(np.float32)
    lower = np.ascontiguousarray(halves[:, 0, :].T)
    same = (s // R_HD == t // R_HD).astype(np.float32)
    sel = (s // R_HD == np.arange(2)[None, :]).astype(np.float32)
    return {"c_order": order, "c_halves": halves, "c_pairs": lower, "c_same": same, "c_sel": sel}


def rwkv(io, pre_gain, post_gain):
    SH = (R_PAIRS, SEQ)
    m = Mix()
    R0, R1, R2, R3, R4 = (m.take(R_PAIRS * SEQ, SH) for _ in range(5))
    uf, sw, em = R0, R0, R0
    dx, af = R1, R1
    rf, kf = R2, R3
    flat = lambda place, lo=0, n=R_PAIRS * SEQ: (lambda mix, part=slice(0, P): place(mix, part).rearrange("p a b -> p (a b)")[:, lo:lo + n])
    tok = lambda place: (lambda mix: place(mix).rearrange("p a b -> p (a b)").rearrange("p (t d) -> p t d", t=NT))
    v = tok(R4)
    result = tok(R3)
    core = m.at
    lora, wa = m.take(D), m.take(SEQ)
    m = Mix(core)
    T1 = m.take(R_PAIRS * SEQ, SH)
    EP = m.take(2 * R_PAIRS * (P + 1), (2 * R_PAIRS, P + 1))
    end = m.at
    m = Mix(core)
    U4 = (4, P)
    TT, AK, RB, RK, MT, Z = (m.take(4 * P, U4) for _ in range(6))
    XX = m.take(8 * P, (8, P))
    assert m.at <= end + 16, (m.at, end)
    m = Mix(max(m.at, end))
    rhs = m.take(2 * R_HD, (2, R_HD))
    order, pairs, same = m.take(2 * P, (2, P)), m.take(P), m.take(P)
    sel = m.take(2)
    mu = m.take(6 * KB, (6, KB))
    w0, a0, k_k, k_a, one_ka, r_k = (m.take(KB) for _ in range(6))
    kcm, nkcm, gamma, tail = m.take(16, (R_PAIRS, NT)), m.take(16, (R_PAIRS, NT)), m.take(8), m.take(8)
    bonus = m.take(NT * R_HEADS, (NT, R_HEADS))
    mean, var = m.take(32), m.take(32)
    lnx_g, lnx_b = flat(R0, 0, D), flat(R0, D, D)
    g2a, g2b = flat(R2, 0, D), flat(R2, D, D)

    def col(a):
        return a.rearrange("(c p) -> p c", p=P)

    loads = [(order, io["c_order"]), (pairs, io["c_pairs"]), (same, io["c_same"]), (sel, io["c_sel"])]
    loads += [((lambda i: lambda mix: mu(mix)[:, i, :])(i), col(io["rwkv_mu"][0, i])) for i in range(6)]
    loads += [(dst, col(io[n][0])) for dst, n in ((w0, "rwkv_w0"), (a0, "rwkv_a0"), (k_k, "rwkv_k_k"), (k_a, "rwkv_k_a"))]
    loads += [(r_k, col(io["rwkv_r_k"][0].rearrange("h n -> (h n)"))),
              (lambda mix: lora(mix, slice(0, R_HD)), io["rwkv_w2"][0]),
              (lambda mix: lora(mix, slice(R_HD, P)), io["rwkv_a2"][0])]

    fills = [[(t, k) for t in range(NT) for k in range(KB)][f:f + 4] for f in range(0, NT * KB, 4)]

    def turn_pe(e, pe):
        for f, blocks in enumerate(fills):
            if f >= 2:
                pe.wait_ge(e.named("u_copied"), f - 1)
            for b, (t, k) in enumerate(blocks):
                last = e.nc.tensor.transpose(e.turn_bank[f % 2][:, b * P:(b + 1) * P], e.y[:, t, k * P:(k + 1) * P], e.ident[:, :])
            last.then_inc(e.named("u_turned"), 1)

    def turn_act(e, act):
        for f, blocks in enumerate(fills):
            act.wait_ge(e.named("u_turned"), f + 1)
            t, k = blocks[0]
            e.nc.scalar.activation(uf(e.mix)[:, k:k + 4, t * P:(t + 1) * P],
                                   e.turn_bank[f % 2][:, :].rearrange("p (k n) -> p k n", k=4), ACT.Copy).then_inc(e.named("u_copied"), 1)

    def mixed(e):
        return e.y[:, :, :].rearrange("p t d -> p (t d)").rearrange("p (k s) -> p k s", k=KB)

    def blend(e, dve, i):
        e.link(dve, e.nc.vector.tensor_tensor(mixed(e), dx(e.mix), along(mu(e.mix)[:, i, :], SEQ), ALU.mult))
        e.nc.vector.tensor_tensor(mixed(e), mixed(e), uf(e.mix), ALU.add)

    def shift_dve(e, dve):
        u, d = uf(e.mix), dx(e.mix)
        e.nc.vector.tensor_tensor(d[:, :, 1:SEQ], u[:, :, 0:SEQ - 1], u[:, :, 1:SEQ], ALU.subtract)
        e.nc.vector.tensor_scalar(one_ka(e.mix), k_a(e.mix), -1.0, 1.0, ALU.mult, ALU.add)
        e.link(dve, e.nc.vector.tensor_scalar(d[:, :, 0:1], u[:, :, 0:1], -1.0, None, ALU.mult))
        blend(e, dve, ORDER[0])

    def high_act(e, act):
        for half in range(2):
            k = slice(4 * half, 4 * half + 4)
            e.nc.scalar.activation(e.xh[:, k, :], mixed(e)[:, k, :], ACT.Copy).then_inc(e.named("blend_high"), 1)

    def low_dve(n):
        def dve_(e, dve):
            for half in range(2):
                k = slice(4 * half, 4 * half + 4)
                dve.wait_ge(e.named("blend_high"), 2 * n + half + 1)
                e.nc.vector.tensor_tensor(e.xl[:, k, :], mixed(e)[:, k, :], e.xh[:, k, :].bitcast(F32), ALU.subtract)
        return dve_

    ORDER = [0, 2, 3, 1, 4, 5]

    def evac_feature(dst):
        def evac(e, c, bank, n):
            return e.nc.scalar.activation(dst(e.mix)[:, 2 * c:2 * c + 2, :], bank[:, :].rearrange("p (f n) -> p f n", f=2), ACT.Copy)
        return evac

    def evac_v(e, c, bank, n):
        return e.nc.scalar.activation(v(e.mix)[:, :, c * CH:(c + 1) * CH], bank[:, :].rearrange("p (t n) -> p t n", t=NT), ACT.Copy)

    def evac_w(e, c, bank, n):
        return e.nc.scalar.activation(wa(e.mix, slice(0, R_HD)), bank[0:R_HD, 0:SEQ], ACT.Tanh)

    def evac_a(e, c, bank, n):
        return e.nc.scalar.activation(wa(e.mix, slice(R_HD, P)), bank[R_HD:P, 0:SEQ], ACT.Copy)

    def evac_g(e, c, bank, n):
        e.nc.scalar.activation(e.silu[:, :], bank[:, 0:SEQ], ACT.Sigmoid)
        return e.nc.scalar.activation(e.hidden[0:32, :], bank[0:32, SEQ:2 * SEQ], ACT.Sigmoid)

    def rows(a):
        return a.rearrange("(k p) n -> p k n", p=P)

    w1, a1, g1 = (rows(io[n][0]) for n in ("rwkv_w1", "rwkv_a1", "rwkv_g1"))
    twice = lambda a: [Chunk(KB, P, [(0, a), (R_HD, a)])]
    GR = 160
    chunks = {0: columns(io["rwkv_w_rkv"][0, 0], 0, D), 2: columns(io["rwkv_w_rkv"][0, 1], 0, D),
              3: columns(io["rwkv_w_rkv"][0, 2], 0, D), 1: twice(w1), 4: twice(a1),
              5: [Chunk(KB, CH, [(0, g1), (GR, g1[:, :, 0:CH - GR])])]}
    evacs = {0: evac_feature(rf), 2: evac_feature(kf), 3: evac_v, 1: evac_w, 4: evac_a, 5: evac_g}

    def beside(n):
        return lambda e, dve: blend(e, dve, ORDER[n + 1]) if n + 1 < len(ORDER) else None

    inputs = []
    for n, i in enumerate(ORDER):
        inputs += [step(act=high_act, dve=low_dve(n)),
                   Stage("proj", chunks=chunks[i], feature_major=(i != 3), dest="gate", by="act", evac=evacs[i],
                         beside=beside(n), loads=[("halves", io["c_halves"])] if n == 0 else [])]

    def lora_pe(part):
        def pe_(e, pe):
            r = slice(0, R_HD) if part == 0 else slice(R_HD, P)
            for c in range(KB):
                e.nc.tensor.matmul(e.out_bank[c // 2][:, (c % 2) * SEQ:(c % 2 + 1) * SEQ],
                                   lora(e.mix, r)[:, c * P:(c + 1) * P], wa(e.mix, r), start=True, stop=True)
        return pe_

    def lora_act(dst, bias):
        def act_(e, act):
            for c in range(KB):
                e.nc.scalar.activation(dst(e.mix)[:, c, :], e.out_bank[c // 2][:, (c % 2) * SEQ:(c % 2 + 1) * SEQ],
                                       ACT.Sigmoid, bias=bias(e.mix)[:, c:c + 1])
        return act_

    A = mixed

    def kk_dve(e, dve):
        e.nc.vector.tensor_tensor(A(e), kf(e.mix), along(k_k(e.mix), SEQ), ALU.mult)

    def kk_act(e, act):
        e.nc.scalar.activation(T1(e.mix), A(e), ACT.Square)

    def kk_pe(e, pe):
        for c in range(KB):
            e.nc.tensor.matmul(e.out_bank[c // 2][:, (c % 2) * SEQ:(c % 2 + 1) * SEQ], same(e.mix), T1(e.mix)[:, c, :],
                               start=True, stop=True)

    def norm_act(e, act):
        for b in range(4):
            e.nc.scalar.activation(T1(e.mix)[:, 2 * b:2 * b + 2, :], e.out_bank[b][:, :].rearrange("p (k s) -> p k s", k=2), ACT.Sqrt)

    def second(e):
        return EP(e.mix).rearrange("p a b -> p (a b)")[:, 0:R_PAIRS * SEQ].rearrange("p (k s) -> p k s", k=KB)

    def prep_dve(e, dve):
        vv, t1, t2, k, r = e.nc.vector, T1(e.mix), second(e), kf(e.mix), rf(e.mix)
        e.link(dve, vv.tensor_scalar(t1, t1, 1e-12, None, ALU.max))
        e.link(dve, vv.reciprocal(t1, t1))
        vv.tensor_tensor(A(e), A(e), t1, ALU.mult)
        for c in range(KB):
            last = vv.tensor_scalar(t2[:, c, :], af(e.mix)[:, c, :], k_a(e.mix)[:, c:c + 1], one_ka(e.mix)[:, c:c + 1],
                                    ALU.mult, ALU.add)
        e.link(dve, last)
        e.link(dve, vv.tensor_tensor(k, k, t2, ALU.mult))
        e.link(dve, vv.tensor_tensor(t2, k, r, ALU.mult))
        for c in range(KB):
            last = vv.tensor_scalar(t2[:, c, :], t2[:, c, :], r_k(e.mix)[:, c:c + 1], None, ALU.mult)
        e.link(dve, vv.tensor_tensor(af(e.mix), af(e.mix), A(e), ALU.mult))

    def bonus_pe(e, pe):
        for t in range(NT):
            for c in range(R_PAIRS):
                e.nc.tensor.matmul(e.gate_bank[0][:, t * R_HEADS + 2 * c:t * R_HEADS + 2 * c + 2],
                                   second(e)[:, c, t * P:(t + 1) * P], sel(e.mix), start=True, stop=True)

    def sum_dve(e, dve):
        vv = e.nc.vector
        for c in range(R_PAIRS):
            for t in range(NT):
                s = slice(t * P, (t + 1) * P)
                last = vv.tensor_tensor_scan(T1(e.mix)[:, c, s], e.ones[:, :], sw(e.mix)[:, c, s], 0.0, ALU.mult, ALU.add)
        e.link(dve, last)
        cm = T1(e.mix).rearrange("p c (t s) -> p c t s", t=NT)[:, :, :, MID]
        vv.tensor_scalar(kcm(e.mix), cm, KAPPA, None, ALU.mult)
        vv.tensor_scalar(nkcm(e.mix), cm, -KAPPA, None, ALU.mult)

    def exp_act(e, act):
        for c in range(R_PAIRS):
            for t in range(NT):
                src = T1(e.mix)[:, c, t * P:(t + 1) * P]
                e.nc.scalar.activation(EP(e.mix)[:, c * NT + t, 1:P + 1], src, ACT.Exp, scale=-KAPPA, bias=kcm(e.mix)[:, c, t:t + 1])
                e.nc.scalar.activation(em(e.mix)[:, c, t * P:(t + 1) * P], src, ACT.Exp, scale=KAPPA, bias=nkcm(e.mix)[:, c, t:t + 1])
        e.nc.scalar.activation(EP(e.mix)[:, :, 0], kcm(e.mix).rearrange("p c t -> p (c t)"), ACT.Exp)
        e.nc.scalar.activation(tail(e.mix), nkcm(e.mix)[:, :, 1], ACT.Exp)

    def bonus_dve(e, dve):
        e.nc.vector.tensor_copy(bonus(e.mix), e.gate_bank[0][:, 0:NT * R_HEADS].rearrange("p (t h) -> p t h", t=NT))

    def scale_dve(e, dve):
        vv = e.nc.vector
        ct = lambda ap: ap.rearrange("p c (t s) -> p (c t) s", t=NT)
        vv.tensor_tensor(gamma(e.mix), EP(e.mix).rearrange("p (c t) s -> p c t s", t=NT)[:, :, 0, P], tail(e.mix), ALU.mult)
        vv.tensor_tensor(af(e.mix), af(e.mix), em(e.mix), ALU.mult)
        vv.tensor_tensor(kf(e.mix), kf(e.mix), em(e.mix), ALU.mult)
        vv.scalar_tensor_tensor(ct(A(e)), ct(A(e)), -1.0, EP(e.mix)[:, :, 0:P], ALU.mult, ALU.mult)
        vv.tensor_tensor(ct(rf(e.mix)), ct(rf(e.mix)), EP(e.mix)[:, :, 1:P + 1], ALU.mult)

    NL = len(R_LEVELS) - 1

    def core_pe(e, pe):
        t_ = e.nc.tensor
        mix = e.mix
        S = e.named
        for c in range(R_PAIRS):
            rows_ = [slice(R_HD * q, R_HD * q + R_HD) for q in range(2)]
            cols_ = [slice(t * P, (t + 1) * P) for t in range(NT)]
            F = lambda place, q, t: place(mix, rows_[q])[:, c, cols_[t]]
            At = lambda q, t: e.y[rows_[q], :, :].rearrange("p t d -> p (t d)").rearrange("p (k s) -> p k s", k=KB)[:, c, cols_[t]]
            if c > 0:
                pe.wait_ge(S("rw_stored"), c)
            for q in range(2):
                for t in range(NT):
                    lo, hi = slice(t * P, (t + 1) * P), slice((2 + t) * P, (3 + t) * P)
                    t_.matmul(e.gate_bank[q][:, lo], At(q, t), F(af, q, t), start=True, stop=True)
                    t_.matmul(e.out_bank[2 * q][:, lo], F(af, q, t), At(q, t), start=True, stop=True)
                    t_.matmul(e.out_bank[2 * q][:, hi], F(kf, q, t), At(q, t), start=True, stop=True)
                    t_.matmul(e.out_bank[2 * q + 1][:, lo], F(af, q, t), F(rf, q, t), start=True, stop=True)
                    last = t_.matmul(e.out_bank[2 * q + 1][:, hi], F(kf, q, t), F(rf, q, t), start=True, stop=True)
            last.then_inc(S("rw_grams"), 1)
            for n in range(NL):
                for q in range(2):
                    pe.wait_ge(S("rw_joined"), (c * (NL + 1) + n) * 2 + q + 1)
                    for t in range(NT):
                        u = 2 * q + t
                        last = t_.matmul(e.gate_bank[q][:, t * P:(t + 1) * P], MT(mix)[:, u, :], XX(mix)[:, 2 * u, :], start=True, stop=True)
                    last.then_inc(S("rw_mx"), 1)
                for q in range(2):
                    pe.wait_ge(S("rw_mx_copied"), (c * NL + n) * 2 + q + 1)
                    for t in range(NT):
                        u = 2 * q + t
                        b = e.turn_bank[q]
                        if n < NL - 1:
                            t_.matmul(b[:, 2 * t * P:(2 * t + 1) * P], XX(mix)[:, 2 * u + 1, :], Z(mix)[:, u, :], start=True, stop=True)
                        last = t_.matmul(b[:, (2 * t + 1) * P:(2 * t + 2) * P], Z(mix)[:, u, :], XX(mix)[:, 2 * u + 1, :], start=True, stop=True)
                    last.then_inc(S("rw_xmx"), 1)
            pe.wait_ge(S("rw_joined"), (c * (NL + 1) + NL) * 2 + 2)
            t_.transpose(e.gate_bank[0][:, 0:P], af(mix)[:, c, 0:P], e.ident[:, :])
            t_.transpose(e.gate_bank[0][:, P:2 * P], kf(mix)[:, c, 0:P], e.ident[:, :]).then_inc(S("rw_bk"), 1)
            for t in range(NT):
                V = lambda q: v(mix)[:, t, c * P + R_HD * q:c * P + R_HD * q + R_HD]
                H = lambda q: slice(R_HD * q, R_HD * q + R_HD)
                if t == 1:
                    pe.wait_ge(S("rw_state_ready"), c + 1)
                for q in range(2):
                    o = (e.gate_bank[1], e.turn_bank[0])[q][:, 0:R_HD]
                    last = t_.matmul(o, AK(mix)[:, 2 * q + t, :], V(q), start=True, stop=(t == 0))
                    if t == 1:
                        last = t_.matmul(o, At(q, t), state(e, q), start=False, stop=True)
                last.then_inc(S("rw_rhs"), 1)
                pe.wait_ge(S("rw_rhs_copied"), NT * c + t + 1)
                for q in range(2):
                    last = t_.matmul(e.turn_bank[1][:, H(q)], XX(mix)[:, 2 * (2 * q + t) + 1, :], rhs(mix)[:, q, :], start=True, stop=True)
                last.then_inc(S("rw_u"), 1)
                pe.wait_ge(S("rw_u_copied"), NT * c + t + 1)
                if t == 0:
                    pe.wait_ge(S("rw_bk_copied"), c + 1)
                    for q in range(2):
                        o = e.gate_bank[0][H(q), 2 * P:2 * P + R_HD]
                        t_.matmul(o, BT(e)[:, H(q)], rhs(mix)[:, q, :], start=True, stop=False)
                        last = t_.matmul(o, KT(e)[:, H(q)], V(q), start=False, stop=True)
                    last.then_inc(S("rw_state"), 1)
                for q in range(2):
                    o = e.out_bank[2 * q + t][:, 0:R_HD]
                    t_.matmul(o, RB(mix)[:, 2 * q + t, :], rhs(mix)[:, q, :], start=True, stop=False)
                    last = t_.matmul(o, RK(mix)[:, 2 * q + t, :], V(q), start=False, stop=(t == 0))
                    if t == 1:
                        last = t_.matmul(o, F(rf, q, t), state(e, q), start=False, stop=True)
                last.then_inc(S("rw_y"), 1)

    BT = lambda e: Z(e.mix)[:, 0, :]
    KT = lambda e: Z(e.mix)[:, 1, :]

    def state(e, q):
        return Z(e.mix, slice(R_HD * q, R_HD * q + R_HD))[:, 2, 0:R_HD]

    def core_act(e, act):
        mix, S = e.mix, e.named
        for c in range(R_PAIRS):
            for n in range(NL):
                for q in range(2):
                    act.wait_ge(S("rw_mx"), (c * NL + n) * 2 + q + 1)
                    e.nc.scalar.activation(Z(mix)[:, 2 * q:2 * q + 2, :], e.gate_bank[q][:, 0:2 * P].rearrange("p (t s) -> p t s", t=2),
                                           ACT.Copy).then_inc(S("rw_mx_copied"), 1)
            act.wait_ge(S("rw_bk"), c + 1)
            e.nc.scalar.activation(Z(mix)[:, 0:2, :], e.gate_bank[0][:, 0:2 * P].rearrange("p (t s) -> p t s", t=2),
                                   ACT.Copy).then_inc(S("rw_bk_copied"), 1)
            for t in range(NT):
                act.wait_ge(S("rw_rhs"), NT * c + t + 1)
                if t == 1:
                    act.wait_ge(S("rw_y"), NT * c + 1)
                e.nc.scalar.activation(rhs(mix)[:, 0, :], e.gate_bank[1][:, 0:R_HD], ACT.Copy)
                e.nc.scalar.activation(rhs(mix)[:, 1, :], e.turn_bank[0][:, 0:R_HD], ACT.Copy).then_inc(S("rw_rhs_copied"), 1)
                act.wait_ge(S("rw_u"), NT * c + t + 1)
                e.nc.scalar.activation(rhs(mix), e.turn_bank[1][:, 0:P].rearrange("p (q d) -> p q d", q=2), ACT.Copy).then_inc(S("rw_u_copied"), 1)

    def core_dve(e, dve):
        mix, S, vv = e.mix, e.named, e.nc.vector
        for c in range(R_PAIRS):
            dve.wait_ge(S("rw_grams"), c + 1)
            sm = order(mix)[:, 0:1, :].to_broadcast([P, 2, P])
            im = order(mix)[:, 1:2, :].to_broadcast([P, 2, P])
            gram = lambda q, b, part: e.out_bank[2 * q + b][:, part * 2 * P:(part + 1) * 2 * P].rearrange("p (t s) -> p t s", t=2)
            for q in range(2):
                last = vv.tensor_tensor(TT(mix)[:, 2 * q:2 * q + 2, :], gram(q, 0, 0), sm, ALU.mult)
            e.link(dve, last)
            xx = XX(mix).rearrange("p (u two) s -> p u two s", two=2)
            level = lambda n: halves(e)[:, n:n + 1, :].to_broadcast([P, 2, P])
            idb = e.ident[:, :].unsqueeze(1).to_broadcast([P, 2, P])
            low_ = pairs(mix).unsqueeze(1).to_broadcast([P, 2, P])
            for q in range(2):
                us = slice(2 * q, 2 * q + 2)
                e.link(dve, vv.tensor_tensor(xx[:, us, 0, :], e.gate_bank[q][:, 0:2 * P].rearrange("p (t s) -> p t s", t=2), low_, ALU.mult))
                e.link(dve, vv.tensor_tensor(xx[:, us, 1, :], TT(mix)[:, us, :], level(0), ALU.mult))
                vv.tensor_tensor(xx[:, us, 0, :], xx[:, us, 0, :], idb, ALU.add)
                vv.tensor_tensor(xx[:, us, 1, :], xx[:, us, 1, :], idb, ALU.add)
                vv.tensor_tensor(MT(mix)[:, us, :], TT(mix)[:, us, :], level(1), ALU.mult).then_inc(S("rw_joined"), 1)
            for q in range(2):
                us = slice(2 * q, 2 * q + 2)
                vv.tensor_tensor(AK(mix)[:, us, :], gram(q, 0, 1), sm, ALU.mult)
                vv.tensor_tensor(RB(mix)[:, us, :], gram(q, 1, 0), im, ALU.mult)
                vv.tensor_tensor(RK(mix)[:, us, :], gram(q, 1, 1), im, ALU.mult)
            for n in range(NL):
                for q in range(2):
                    us = slice(2 * q, 2 * q + 2)
                    dve.wait_ge(S("rw_xmx"), (c * NL + n) * 2 + q + 1)
                    tb = e.turn_bank[q][:, :].rearrange("p (u two s) -> p u two s", u=2, two=2)
                    if n < NL - 1:
                        x2 = XX(mix)[:, 4 * q:4 * q + 4, :]
                        vv.tensor_tensor(x2, x2, e.turn_bank[q][:, :].rearrange("p (u s) -> p u s", u=4), ALU.add)
                        vv.tensor_tensor(MT(mix)[:, us, :], TT(mix)[:, us, :], level(n + 2), ALU.mult).then_inc(S("rw_joined"), 1)
                    else:
                        vv.tensor_tensor(xx[:, us, 1, :], xx[:, us, 1, :], tb[:, :, 1, :], ALU.add).then_inc(S("rw_joined"), 1)
            dve.wait_ge(S("rw_state"), c + 1)
            vv.tensor_scalar(Z(mix)[:, 2, 0:R_HD], e.gate_bank[0][:, 2 * P:2 * P + R_HD], gamma(mix)[:, c:c + 1], None,
                             ALU.mult).then_inc(S("rw_state_ready"), 1)
            dve.wait_ge(S("rw_y"), NT * (c + 1))
            for t in range(NT):
                for q in range(2):
                    last = vv.tensor_copy(A(e)[:, c, t * P + q * R_HD:t * P + (q + 1) * R_HD], e.out_bank[2 * q + t][:, 0:R_HD])
            last.then_inc(S("rw_stored"), 1)

    def g_pe(e, pe):
        for t in range(NT):
            for n in range(2):
                o, s = e.out_bank[2 * t + n][:, :], slice(512 * n, 512 * (n + 1))
                e.nc.tensor.matmul(o, e.silu[:, t * P:(t + 1) * P], g2a(e.mix)[:, s], start=True, stop=False)
                e.nc.tensor.matmul(o, e.hidden[0:32, t * P:(t + 1) * P], g2b(e.mix, slice(0, 32))[:, s], start=False, stop=True)

    def groups(e):
        return A(e).rearrange("p c s -> p (c s)").rearrange("p (g d) -> p g d", d=R_HD)

    def mean_dve(e, dve):
        vv, y_ = e.nc.vector, groups(e)
        e.link(dve, vv.tensor_reduce(mean(e.mix), y_, AX.X, ALU.add))
        e.link(dve, vv.tensor_scalar(mean(e.mix), mean(e.mix), 1.0 / R_HD, None, ALU.mult))
        e.link(dve, vv.tensor_tensor(y_, y_, along(mean(e.mix), R_HD), ALU.subtract))
        sq = T1(e.mix).rearrange("p c s -> p (c s)").rearrange("p (g d) -> p g d", d=R_HD)
        e.link(dve, vv.tensor_tensor(sq, y_, y_, ALU.mult))
        e.link(dve, vv.tensor_reduce(var(e.mix), sq, AX.X, ALU.add))
        vv.tensor_scalar(var(e.mix), var(e.mix), 1.0 / R_HD, LNX_EPS, ALU.mult, ALU.add)

    def root_act(e, act):
        e.nc.scalar.activation(var(e.mix), var(e.mix), ACT.Sqrt)

    def gate_dve(e, dve):
        vv, y_ = e.nc.vector, groups(e)
        e.link(dve, vv.reciprocal(var(e.mix), var(e.mix)))
        e.link(dve, vv.tensor_tensor(y_, y_, along(var(e.mix), R_HD), ALU.mult))
        for t in range(NT):
            yt = A(e).rearrange("p c (t s) -> p c t s", t=NT)[:, :, t, :]
            wide = lambda ap: ap.rearrange("p (c s) -> p c s", s=P)
            out_ = result(e.mix)[:, t, :]
            heads = lambda ap: ap.rearrange("p (h d) -> p h d", d=R_HD)
            e.link(dve, vv.tensor_tensor(yt, yt, wide(lnx_g(e.mix)), ALU.mult))
            e.link(dve, vv.tensor_tensor(yt, yt, wide(lnx_b(e.mix)), ALU.add))
            e.link(dve, vv.tensor_tensor(heads(out_), heads(v(e.mix)[:, t, :]), along(bonus(e.mix)[:, t, :], R_HD), ALU.mult))
            e.link(dve, vv.tensor_tensor(wide(out_), wide(out_), yt, ALU.add))
            for n in range(2):
                o = result(e.mix)[:, t, 512 * n:512 * (n + 1)]
                vv.tensor_tensor(o, o, e.out_bank[2 * t + n][:, :], ALU.mult)

    def halves(e):
        return e.sq_scratch[:, 0:7 * P].rearrange("p (n s) -> p n s", n=7)

    def core_step():
        s = step(core_pe, core_act, core_dve)
        s.loads = [(lnx_g, spread(io["rwkv_lnx_g"][0])), (lnx_b, spread(io["rwkv_lnx_b"][0]))]
        return s

    def after_step():
        s = step(dve=mean_dve)
        s.loads = [(g2a, io["rwkv_g2"][0, 0:P, :]), (lambda mix: g2b(mix, slice(0, 32)), io["rwkv_g2"][0, P:GR, :])]
        return s

    stages = [Stage("pre", gain=pre_gain), step(turn_pe, turn_act), step(dve=shift_dve)] + inputs + [
              step(pe=lora_pe(0)), step(act=lora_act(sw, w0)), step(pe=lora_pe(1)), step(act=lora_act(af, a0)),
              step(dve=kk_dve), step(act=kk_act), step(pe=kk_pe), step(act=norm_act), step(dve=prep_dve),
              step(pe=bonus_pe, dve=sum_dve), step(act=exp_act, dve=bonus_dve), step(dve=scale_dve),
              core_step(), after_step(), step(pe=g_pe, act=root_act), step(dve=gate_dve),
              Stage("turn", kb=KB, src=result),
              Stage("proj", chunks=columns(io["rwkv_w_o"][0], 0, D), feature_major=False, dest="out", evac=None),
              Stage("post", gain=post_gain, norm=True, scale=1.0, bias=None)]
    return loads, stages



GRID_W = 64
DILATED = ((128, 1), (512, 4), (2048, 16))
A_GROUPS, A_PER = len(DILATED), 8
A_HEADS = A_GROUPS * A_PER
A_HD = 64
B_HEADS, B_KV, B_HD = 8, 2, 128
B_ROT = B_HEADS + B_KV
BUCKETS, MAX_DISTANCE = 32, 1024
THETA = 10000.0


def hybrid_constants():
    import math
    import numpy as np
    rel = np.arange(2 * SEQ) - (SEQ - 1)
    n = BUCKETS // 2
    exact = n // 2
    a = np.abs(rel)
    large = exact + (np.log(np.maximum(a, 1).astype(np.float32) / np.float32(exact))
                     / np.float32(math.log(MAX_DISTANCE / exact)) * np.float32(n - exact)).astype(np.int32)
    bucket = np.where(rel > 0, n, 0) + np.where(a < exact, a, np.minimum(large, n - 1))
    onehot = (np.arange(BUCKETS)[:, None] == bucket[None, :]).astype(np.float32)
    out = np.zeros((A_GROUPS, 2 * SEQ), np.float32)
    for g, (window, dil) in enumerate(DILATED):
        out[g] = np.where((rel % dil == 0) & (a // dil <= window // (2 * dil)), 0.0, -1e30)
    group = (np.arange(A_GROUPS)[:, None] == np.arange(A_HEADS)[None, :] // A_PER).astype(np.float32)
    row, col = np.arange(SEQ) // GRID_W, np.arange(SEQ) % GRID_W
    nf = B_HD // 4
    freq = np.float32(THETA) ** (-np.arange(nf, dtype=np.float32) / np.float32(nf))
    ang = np.concatenate([row[:, None].astype(np.float32) * freq, col[:, None].astype(np.float32) * freq], -1)
    table = np.stack([np.cos(ang), np.sin(ang)], 1).reshape(NT, P, 2, B_HD // 2).transpose(1, 0, 2, 3)
    return {"c_onehot": onehot, "c_outside": out, "c_group": group,
            "c_rope": np.ascontiguousarray(table.reshape(P, NT * 2, B_HD // 2)).astype(np.float32)}


def hybrid(io):
    w = io["w_in_2"][0]
    A_QK = A_HEADS * A_HD
    o1 = 3 * A_QK
    o2 = o1 + B_ROT * B_HD
    o3 = o2 + B_KV * B_HD
    m = Mix()
    qf, kf = (m.take(A_HEADS // 2 * SEQ, (A_HEADS // 2, SEQ)) for _ in range(2))
    v = m.take(NT * A_QK, (NT, A_QK))
    A_KEYS = A_GROUPS * SEQ
    bias = [m.take(A_KEYS) for _ in range(2)]
    scores = [m.take(A_KEYS) for _ in range(2)]
    turned = [m.take(A_KEYS) for _ in range(2)]
    negmax, sums = m.take(NT * A_PER), m.take(NT * A_PER)
    onehot, outside, table, relb, group = bias[0], bias[1], scores[0], scores[1], turned[0]
    rope = Mix(MIX - NT * B_HD).take(NT * 2 * B_HD // 2, (NT * 2, B_HD // 2))
    rowsB, rowsG = slice(0, BUCKETS), slice(0, A_GROUPS)
    loads = [(lambda mix: onehot(mix, rowsB)[:, 0:2 * SEQ], io["c_onehot"]),
             (lambda mix: outside(mix, rowsG)[:, 0:2 * SEQ], io["c_outside"]),
             (lambda mix: relb(mix, rowsB)[:, 0:A_HEADS], io["rel_bias_2"]),
             (lambda mix: group(mix, rowsG)[:, 0:A_HEADS], io["c_group"]),
             (rope, io["c_rope"])]

    def table_pe(e, pe):
        o = e.out_bank[0][0:A_HEADS, :]
        e.nc.tensor.matmul(o, relb(e.mix, rowsB)[:, 0:A_HEADS], onehot(e.mix, rowsB)[:, 0:2 * SEQ], start=True, stop=False)
        e.nc.tensor.matmul(o, group(e.mix, rowsG)[:, 0:A_HEADS], outside(e.mix, rowsG)[:, 0:2 * SEQ], start=False, stop=True)

    def table_act(e, act):
        rows = table(e.mix, slice(0, A_HEADS))[:, 0:2 * SEQ]
        e.link_act(act, e.nc.scalar.activation(rows, e.out_bank[0][0:A_HEADS, :], ACT.Copy))
        act.dma_start(io["t_bias"], rows.unsqueeze(1).to_broadcast([A_HEADS, P, 2 * SEQ])).then_inc(e.named("table_stored"), 16)

    def evac_feature(dst, scale):
        def evac(e, c, bank, n):
            return e.nc.scalar.activation(dst(e.mix)[:, 2 * c:2 * c + 2, :],
                                          bank[:, :].rearrange("p (f n) -> p f n", f=2), ACT.Copy, scale=scale)
        return evac

    def evac_token(dst, at=0):
        def evac(e, c, bank, n):
            return e.nc.scalar.activation(dst(e.mix)[:, :, c * CH:c * CH + n],
                                          bank[:, :].rearrange("p (t n) -> p t n", t=NT)[:, :, 0:n], ACT.Copy)
        return evac

    def proj(lo, hi, evac, feature_major=False, by="act", loads=()):
        return Stage("proj", chunks=columns(w, lo, hi), feature_major=feature_major, dest="gate", by=by, evac=evac,
                     loads=list(loads))

    def setup_a(e, st):
        mix = e.mix

        def item(i):
            t, j = i // A_PER, i % A_PER
            rows = slice(A_HD * (j % 2), A_HD * (j % 2) + A_HD)
            sc, vs = [], []
            for g in range(A_GROUPS):
                tile = (g * A_PER + j) // 2
                sc.append((g * SEQ, qf(mix, rows)[:, tile, t * P:(t + 1) * P], kf(mix, rows)[:, tile, :]))
                cols = slice((g * A_PER + j) * A_HD, (g * A_PER + j + 1) * A_HD)
                vs += [v(mix)[:, s, cols] for s in range(NT)]
            return Item(sc, A_KEYS, bias[i % 2](mix), vs, e.y[:, t, j * A_HD:(j + 1) * A_HD])

        def load_bias(act, i):
            t, j = i // A_PER, i % A_PER
            tb = io["t_bias"]
            if i == 0:
                act.wait_ge(e.named("table_stored"), 16)
            src = bass.AP(tb.tensor, tb.offset + j * P * 2 * SEQ + SEQ - 1 - t * P,
                          [[2 * SEQ - 1, P], [A_PER * P * 2 * SEQ, A_GROUPS], [1, SEQ]])
            act.dma_start(bias[i % 2](mix).rearrange("p (g s) -> p g s", g=A_GROUPS), src).then_inc(
                e.named(f"bias{i % 2}_loaded"), 16)

        def before(dve, i):
            dve.wait_ge(e.named(f"bias{i % 2}_loaded"), 16 * (i // 2 + 1))

        st.item, st.load_bias, st.before = item, load_bias, before
        st.probs = lambda i: scores[i % 2](mix)
        st.turned = lambda i: turned[i % 2](mix)
        st.negmax, st.sums, st.sink = negmax(mix), sums(mix), None

    m = Mix()
    qk = m.take(NT * B_ROT * B_HD, (NT, B_ROT * B_HD))
    ob = m_ob = lambda mix: qk(mix)[:, :, 0:B_HEADS * B_HD]
    vb = m.take(NT * B_KV * B_HD, (NT, B_KV * B_HD))
    gates = m.take(NT * 2 * D, (NT, 2 * D))
    bg = m.take(2 * D)
    qkf = m.take(B_ROT * SEQ, (B_ROT, SEQ))
    scores_b = [m.take(SEQ) for _ in range(2)]
    turned_b = [m.take(SEQ) for _ in range(2)]
    negmax_b, sums_b = m.take(NT * B_HEADS), m.take(NT * B_HEADS)
    sq, mean, rt = (m.take(NT * B_ROT) for _ in range(3))
    gains = m.take(B_ROT * B_HD, (B_ROT, B_HD))
    assert m.at <= MIX - NT * B_HD

    def rows_of(g, n):
        return bass.AP(g.tensor, g.offset, [[0, P], [0, n], [1, B_HD]])

    loads_b = [(bg, spread(io["b_gate_2"][0])),
               (lambda mix: gains(mix)[:, 0:B_HEADS, :], rows_of(io["q_norm_2"][0], B_HEADS)),
               (lambda mix: gains(mix)[:, B_HEADS:B_ROT, :], rows_of(io["k_norm_2"][0], B_KV))]

    def heads_of(e):
        return qk(e.mix).rearrange("p t (h d) -> p (t h) d", d=B_HD)

    def norm_dve(e, dve):
        x = heads_of(e)
        tmp = qkf(e.mix).rearrange("p h (a d) -> p (h a) d", d=B_HD)
        e.link(dve, e.nc.vector.tensor_tensor(tmp, x, x, ALU.mult))
        e.link(dve, e.nc.vector.tensor_reduce(sq(e.mix), tmp, AX.X, ALU.add))
        e.nc.vector.tensor_scalar(mean(e.mix), sq(e.mix), 1.0 / B_HD, EPS, ALU.mult, ALU.add)

    def root_act(e, act):
        e.nc.scalar.activation(rt(e.mix), mean(e.mix), ACT.Sqrt)

    def rope_dve(e, dve):
        v_, x = e.nc.vector, heads_of(e)
        e.link(dve, v_.reciprocal(rt(e.mix), rt(e.mix)))
        e.link(dve, v_.tensor_tensor(x, x, along(rt(e.mix), B_HD), ALU.mult))
        H2 = B_HD // 2
        for t in range(NT):
            xt = x[:, t * B_ROT:(t + 1) * B_ROT, :]
            e.link(dve, v_.tensor_tensor(xt, xt, gains(e.mix), ALU.mult))
            pair = xt.rearrange("p h (f two) -> p h f two", two=2)
            x0, x1 = pair[:, :, :, 0], pair[:, :, :, 1]
            c = rope(e.mix)[:, 2 * t:2 * t + 1, :].to_broadcast([P, B_ROT, H2])
            s = rope(e.mix)[:, 2 * t + 1:2 * t + 2, :].to_broadcast([P, B_ROT, H2])
            tmp = qkf(e.mix).rearrange("p h s -> p (h s)")
            p4 = [tmp[:, n * B_ROT * H2:(n + 1) * B_ROT * H2].rearrange("p (h f) -> p h f", h=B_ROT) for n in range(4)]
            v_.tensor_tensor(p4[0], x0, c, ALU.mult)
            v_.tensor_tensor(p4[1], x1, s, ALU.mult)
            v_.tensor_tensor(p4[2], x0, s, ALU.mult)
            e.link(dve, v_.tensor_tensor(p4[3], x1, c, ALU.mult))
            v_.tensor_tensor(x0, p4[0], p4[1], ALU.subtract)
            e.link(dve, v_.tensor_tensor(x1, p4[2], p4[3], ALU.add))

    fills = [[(t, hd) for t in range(NT) for hd in range(B_ROT)][f:f + 4] for f in range(0, NT * B_ROT, 4)]

    def turn_pe(e, pe):
        for f, blocks in enumerate(fills):
            if f >= 2:
                pe.wait_ge(e.named("rope_copied"), f - 1)
            for b, (t, hd) in enumerate(blocks):
                last = e.nc.tensor.transpose(e.turn_bank[f % 2][:, b * P:(b + 1) * P],
                                             qk(e.mix)[:, t, hd * B_HD:(hd + 1) * B_HD], e.ident[:, :])
            last.then_inc(e.named("rope_turned"), 1)

    def turn_act(e, act):
        for f, blocks in enumerate(fills):
            act.wait_ge(e.named("rope_turned"), f + 1)
            for b, (t, hd) in enumerate(blocks):
                last = e.nc.scalar.activation(qkf(e.mix)[:, hd, t * P:(t + 1) * P],
                                              e.turn_bank[f % 2][:, b * P:(b + 1) * P], ACT.Copy)
            last.then_inc(e.named("rope_copied"), 1)

    def setup_b(e, st):
        mix = e.mix

        def item(i):
            t, hd = i // B_HEADS, i % B_HEADS
            g = hd // (B_HEADS // B_KV)
            return Item([(0, qkf(mix)[:, hd, t * P:(t + 1) * P], qkf(mix)[:, B_HEADS + g, :])], SEQ, None,
                        [vb(mix)[:, s, g * B_HD:(g + 1) * B_HD] for s in range(NT)],
                        ob(mix)[:, t, hd * B_HD:(hd + 1) * B_HD])

        st.item, st.load_bias, st.before = item, None, None
        st.probs = lambda i: scores_b[i % 2](mix)
        st.turned = lambda i: turned_b[i % 2](mix)
        st.negmax, st.sums, st.sink = negmax_b(mix), sums_b(mix), None

    def evac_gates(e, c, bank, n):
        return e.nc.vector.tensor_tensor(gates(e.mix)[:, :, c * CH:(c + 1) * CH],
                                         bank[:, :].rearrange("p (t n) -> p t n", t=NT),
                                         bg(e.mix)[:, c * CH:(c + 1) * CH].unsqueeze(1).to_broadcast([P, NT, CH]), ALU.add)

    def gate_act(e, act):
        for t in range(NT):
            e.nc.scalar.activation(gates(e.mix)[:, t, :], gates(e.mix)[:, t, :], ACT.Sigmoid)

    def merge(branch):
        def dve_(e, dve):
            for t in range(NT):
                for n in range(2):
                    gt = gates(e.mix)[:, t, branch * D + n * 512:branch * D + (n + 1) * 512]
                    dst = e.y[:, t, n * 512:(n + 1) * 512] if branch == 0 else gt
                    last = e.nc.vector.tensor_tensor(dst, gt, e.out_bank[2 * t + n][:, :], ALU.mult)
            if branch == 1:
                e.link(dve, last)
                e.nc.vector.tensor_tensor(e.y[:, :, :], e.y[:, :, :], gates(e.mix)[:, :, D:2 * D], ALU.add)
        return dve_

    def back(name):
        return Stage("proj", chunks=columns(io[name][0], 0, D), feature_major=False, dest="out", evac=None)

    stages = [step(pe=table_pe), step(act=table_act),
              Stage("pre", gain=io["mix_norm_2"][0]), Stage("turn", kb=KB),
              proj(0, A_QK, evac_feature(qf, A_HD ** -0.5), feature_major=True),
              proj(A_QK, 2 * A_QK, evac_feature(kf, 1.0), feature_major=True), proj(2 * A_QK, o1, evac_token(v)),
              Stage("attention", items=NT * A_PER, max_blocks=NT * A_GROUPS, scale=1.0, setup=setup_a),
              proj(o1, o2, evac_token(qk), loads=loads_b), proj(o2, o3, evac_token(vb)),
              proj(o3, o3 + 2 * D, evac_gates, by="dve"), step(act=gate_act),
              step(dve=norm_dve), step(act=root_act), step(dve=rope_dve), step(pe=turn_pe, act=turn_act),
              Stage("attention", items=NT * B_HEADS, max_blocks=NT, scale=B_HD ** -0.5, setup=setup_b),
              Stage("turn", kb=A_PER * A_HD // P), back("w_branch_a_2"), step(dve=merge(0)),
              Stage("turn", kb=KB, src=ob), back("w_branch_b_2"), step(dve=merge(1)),
              Stage("turn", kb=KB), back("w_out_2"),
              Stage("post", gain=None, norm=False, scale=1.0, bias=None)]
    return loads, stages


def network(io, only=None):
    st = []

    def ffn(gate, up, down, loads=()):
        return Stage("ffn", gate=gate, up=up, down=down, loads=list(loads))

    def first_ffn(l, i, loads=()):
        g, w = io["norm_g"][l], io["ffn_w_in"][l, i]
        return [Stage("pre", gain=g[4 * i]), Stage("turn", kb=KB),
                ffn(w[:, 0:D_FF], w[:, D_FF:2 * D_FF], io["ffn_w_out"][l, i], loads),
                Stage("post", gain=g[4 * i + 1], norm=True, scale=0.5, bias=None)]

    def second_ffn(n, loads=()):
        w = [io[f"ffn{n}_w{i}_2"][0] for i in (1, 3, 2)]
        return [Stage("pre", gain=io[f"ffn{n}_norm_2"][0]), Stage("turn", kb=KB), ffn(*w, loads),
                Stage("post", gain=None, norm=False, scale=0.5, bias=None)]

    for layer in only if only is not None else [0, 1, 2, 3, 4]:
        if isinstance(layer, tuple):
            part, layer = layer
        else:
            part = "all"
        if layer < 4:
            g = io["norm_g"][layer]
            loads, mixer = (lambda: swa(io, 0, g[2], g[3]), lambda: gla(io, g[2], g[3]),
                            lambda: rwkv(io, g[2], g[3]), lambda: swa(io, 1, g[2], g[3]))[layer]()
            before, after, tail = [], [], []
            if part != "mixer":
                before, after = first_ffn(layer, 0, loads), first_ffn(layer, 1)
        else:
            loads, mixer = hybrid(io)
            before, after = ([], []) if part == "mixer" else (second_ffn(1, loads), second_ffn(2))
            tail = [Stage("pre", gain=io["final_norm_2"])]
        if part == "mixer":
            before, after = [Stage("load", loads=loads)], []
        if part == "none":
            before, after = [], []
        st += before + mixer + after + tail
    return st


def constants():
    import numpy as np
    q, k = np.arange(P)[:, None] + P, np.arange(2 * P)[None, :]
    window = np.where((q - k >= 0) & (q - k < WINDOW), 0.0, -1e30).astype(np.float32)
    return {"c_window": window, "c_levels": level_masks(), **rwkv_constants(), **hybrid_constants()}


_OUTS = [((1, SEQ, D), "float32")]


def kernel(**inputs):
    import numpy as _np
    import concourse.bacc as _bacc
    from concourse import mybir as _mybir
    from concourse.bass_utils import run_bass_kernel_spmd as _run

    nc = _bacc.Bacc("TRN2", target_bir_lowering=False, num_devices=1)
    arrays, io = {}, {}
    inputs.update(constants())
    for name in inputs:
        a = _np.ascontiguousarray(inputs[name])
        arrays[f"in_{name}_dram"] = a
        io[name] = nc.dram_tensor(f"in_{name}_dram", a.shape, _mybir.dt.from_np(a.dtype), kind="ExternalInput").ap()
    out = nc.dram_tensor("out_0_dram", _OUTS[0][0], F32, kind="ExternalOutput").ap()
    io["t_bias"] = nc.dram_tensor("t_bias", (A_HEADS, P, 2 * SEQ), F32, kind="Internal").ap()
    build(nc, io, out, network(io))
    r = _run(nc, [arrays], core_ids=[0])
    return r.results[0]["out_0_dram"]
```

```python
import concourse.bass as bass
from concourse import mybir
from contextlib import ExitStack

F32 = mybir.dt.float32
F32R = mybir.dt.float32r
ALU = mybir.AluOpType
ACT = mybir.ActivationFunctionType
AX = mybir.AxisListType.X

P = 128
SEQ = 256
NT = SEQ // P
D = 1024
KB = D // P
D_FF = 2816
FB = D_FF // P
EPS = 1e-6

RAW = 4
SPLIT = 2
IN_W = 2 * KB * P
SLOT = IN_W + D
ARRIVAL = 64
CH = 256
UNROLL = 4
LOOPS = (FB - 2) // UNROLL
MIX = 15528


class Stage:

    def __init__(self, kind, gain=None, norm=False, scale=1.0, bias=None, chunks=(), feature_major=False, dest=None,
                 evac=None, by=None, beside=None, loads=(), gate=None, up=None, down=None, kb=KB, src=None,
                 items=0, max_blocks=0, setup=None, post=None, pre=None, turn=False, pe=None, act=None, dve=None):
        self.kind, self.loads, self.setup = kind, list(loads), setup
        self.gain, self.norm, self.scale, self.bias = gain, norm, scale, bias
        self.chunks, self.feature_major, self.dest = chunks, feature_major, dest
        self.evac, self.by, self.beside = evac, by, beside
        self.gate, self.up, self.down = gate, up, down
        self.post, self.pre, self.turn = post, pre, turn
        self.kb, self.src = kb, src
        self.items, self.max_blocks = items, max_blocks
        self.pe, self.act, self.dve = pe, act, dve
        self.units = FB + 1 if kind == "ffn" else len(chunks)


class Env:

    def __init__(self, nc, mix, y, xh, xl, silu, hidden, ident, ones, sq_scratch, out_bank, gate_bank, turn_bank,
                 link, link_act, named):
        self.nc, self.mix, self.y, self.xh, self.xl = nc, mix, y, xh, xl
        self.silu, self.hidden, self.ident, self.ones, self.sq_scratch = silu, hidden, ident, ones, sq_scratch
        self.out_bank, self.gate_bank, self.turn_bank = out_bank, gate_bank, turn_bank
        self.link, self.link_act, self.named = link, link_act, named


class Chunk:

    def __init__(self, kb, n, parts):
        self.kb, self.n, self.parts = kb, n, parts


def columns(w, lo, hi):
    v = w.rearrange("(k p) n -> p k n", p=P)
    return [Chunk(v.shape[1], min(CH, hi - c), [(0, v[:, :, c:min(c + CH, hi)])]) for c in range(lo, hi, CH)]


def spread(row):
    return row.partition_broadcast(P)


def along(ap, n):
    return ap.unsqueeze(2).to_broadcast([ap.shape[0], ap.shape[1], n])


def build(nc, io, out, stages):
    first = []
    u = 0
    for st in stages:
        first.append(u)
        u += st.units
    n_units = u
    evac_at, at = {}, 0
    count = {}
    for s, st in enumerate(stages):
        st.at, st.u0 = s, first[s]
        st.e0 = at
        if st.kind == "proj" and st.dest == "gate":
            at += st.units
        st.nth = count.get(st.kind, 0)
        count[st.kind] = st.nth + 1
    crossings = [st for st in stages if st.kind == "cross"]
    tiles = {"post": 0, "pre": 0}
    gains = [0, 0]
    for st in crossings:
        st.post_gained = st.post is not None and st.post.norm
        gains[0] += st.post_gained
        gains[1] += st.pre is not None
        st.gains = tuple(gains)
        st.roots0 = tiles["post"] + tiles["pre"]
        tiles["post"] += NT * st.post_gained
        st.pre0 = tiles["pre"]
        tiles["pre"] += NT * (st.pre is not None)
    items = 0
    for st in stages:
        if st.kind == "attention":
            st.first_item = items
            items += st.items
    turns = 0
    for st in stages:
        if st.kind == "turn" or (st.kind == "cross" and st.turn):
            st.fill0 = turns
            turns += NT * st.kb // 4

    ctx = ExitStack()
    with ctx:
        def sb(name, shape, dt=F32):
            return ctx.enter_context(nc.sbuf_tensor(name, shape, dt))

        def sem(name):
            return ctx.enter_context(nc.semaphore(name))

        raw = [sb(f"raw{i}", [P, SLOT]) for i in range(RAW)]
        high = [sb(f"high{i}", [P, SLOT], F32R) for i in range(SPLIT)]
        low = [sb(f"low{i}", [P, SLOT], F32R) for i in range(SPLIT)]
        h = sb("h", [P, NT, D])
        y = sb("y", [P, NT, D])
        xh = sb("xh", [P, KB, SEQ], F32R)
        xl = sb("xl", [P, KB, SEQ], F32R)
        gain = [sb(f"gain{i}", [P, D]) for i in range(2)]
        silu = sb("silu", [P, SEQ])
        hidden = sb("hidden", [P, SEQ])
        hid_h = [sb(f"hid_h{i}", [P, SEQ], F32R) for i in range(2)]
        hid_l = [sb(f"hid_l{i}", [P, SEQ], F32R) for i in range(2)]
        ident = sb("ident", [P, P])
        ones = sb("ones", [P, P])
        squares = sb("squares", [P, 2 * NT])
        root = sb("root", [P, 2 * NT])
        rstd = sb("rstd", [P, 2 * NT])
        idle = sb("idle", [P, 1])
        sq_scratch = sb("sq_scratch", [P, D])
        ln_eps = sb("ln_eps", [P, 2])
        mix = sb("mix", [P, MIX])
        out_banks = ctx.enter_context(nc.psum_tensor("out_banks", [P, 4 * 512], F32))
        out_bank = [out_banks[:, b * 512:(b + 1) * 512] for b in range(4)]
        gate_bank = [ctx.enter_context(nc.psum_tensor(f"gate_bank{i}", [P, 512], F32)) for i in range(2)]
        turn_bank = [ctx.enter_context(nc.psum_tensor(f"turn_bank{i}", [P, 512], F32)) for i in range(2)]

        arrived = [sem(f"weights_arrived{i}") for i in range(RAW)]
        high_ready = sem("high_ready")
        weights_split = sem("weights_split")
        weights_used = sem("weights_used")
        emptied = sem("emptied")
        silu_ready = sem("silu_ready")
        hidden_ready = sem("hidden_ready")
        gate_up_ready = sem("gate_up_ready")
        gain_loaded = [sem("gain0_loaded"), sem("gain1_loaded")]
        h_loaded = sem("h_loaded")
        consts_loaded = sem("consts_loaded")
        biased = sem("biased")
        tile_free = sem("tile_free")
        branch_read = sem("branch_read")
        root_ready = sem("root_ready")
        h_ready = sem("h_ready")
        y_ready = sem("y_ready")
        turned = sem("turned")
        turned_high = sem("turned_high")
        turned_low = sem("turned_low")
        dve_link = sem("dve_link")
        act_link = sem("act_link")
        stored = sem("stored")
        done = {e: sem(f"stage_done_{e}") for e in ("pe", "act", "dve")}

        ident_zero = sem("ident_zero")
        ident_ready = sem("ident_ready")

        def next_unit(s):
            u = first[s] + stages[s].units
            return u if u < n_units else None

        def stage_of(u):
            return [st for st in stages if st.units and st.u0 <= u < st.u0 + st.units][0]

        def words(u):
            st = stage_of(u)
            if st.kind == "ffn":
                return IN_W if u == st.u0 else SLOT
            chunk = st.chunks[u - st.u0]
            return chunk.kb * chunk.n

        def barrier(eng, me, s):
            eng.drain().then_inc(done[me], 1)
            for e in ("pe", "act", "dve"):
                if e != me:
                    eng.wait_ge(done[e], s + 1)


        def split_high(act, u, w, turn=0):
            act.wait_ge(arrived[u % RAW], ARRIVAL * (u // RAW + 1) + ARRIVAL * turn)
            if u >= SPLIT:
                act.wait_ge(weights_used, u - SPLIT + 1 + UNROLL * turn)
            nc.scalar.activation(high[u % SPLIT][:, 0:w], raw[u % RAW][:, 0:w], ACT.Copy).then_inc(high_ready, 1)

        def split_low(dve, u, w, turn=0):
            dve.wait_ge(high_ready, u + 1 + UNROLL * turn)
            nc.vector.tensor_tensor(low[u % SPLIT][:, 0:w], raw[u % RAW][:, 0:w],
                                    high[u % SPLIT][:, 0:w].bitcast(F32), ALU.subtract).then_inc(weights_split, 1)

        def load_unit(sp, u, parts, turn=0):
            if u >= RAW or not isinstance(turn, int):
                sp.wait_ge(weights_split, u - RAW + 1 + UNROLL * turn)
            for n, (dst, src) in enumerate(parts):
                last = n == len(parts) - 1
                sp.dma_start(dst, src).then_inc(arrived[u % RAW], ARRIVAL - 16 * (len(parts) - 1) if last else 16)

        def ffn_parts(st, q, at, down_at):
            slot = raw[(st.u0 + q) % RAW]
            parts = []
            if q < FB:
                for n, w in enumerate((st.gate, st.up)):
                    parts.append((slot[:, n * D:(n + 1) * D].rearrange("p (k n) -> p k n", k=KB),
                                  w.rearrange("(k p) n -> p k n", p=P)[:, :, bass.ds(at, P)]))
            if q > 0:
                parts.append((slot[:, IN_W:SLOT], st.down[bass.ds(down_at, P), :]))
            return parts


        def ffn_pe(pe, st):
            def unit(q, turn=0):
                u = st.u0 + q
                H, L = high[u % SPLIT], low[u % SPLIT]
                f = st.nth * FB
                pe.wait_ge(weights_split, u + 1 + UNROLL * turn)
                if q < FB:
                    if f + q >= 2:
                        pe.wait_ge(hidden_ready, f + q - 1 + UNROLL * turn)
                    for n in range(2):
                        for k in range(KB):
                            w = slice((n * KB + k) * P, (n * KB + k + 1) * P)
                            o = gate_bank[q % 2][:, n * SEQ:(n + 1) * SEQ]
                            nc.tensor.matmul(o, H[:, w], xh[:, k, :], start=(k == 0), stop=False)
                            nc.tensor.matmul(o, H[:, w], xl[:, k, :], start=False, stop=False)
                            last = nc.tensor.matmul(o, L[:, w], xh[:, k, :], start=False, stop=(k == KB - 1))
                    last.then_inc(gate_up_ready, 1)
                if q > 0:
                    pe.wait_ge(hidden_ready, f + q + UNROLL * turn)
                    b = (q - 1) % 2
                    for t in range(NT):
                        tok = slice(t * P, (t + 1) * P)
                        for n in range(2):
                            o = out_bank[2 * t + n][:, :]
                            w = slice(IN_W + 512 * n, IN_W + 512 * (n + 1))
                            nc.tensor.matmul(o, hid_h[b][:, tok], H[:, w], start=(q == 1), stop=False)
                            nc.tensor.matmul(o, hid_h[b][:, tok], L[:, w], start=False, stop=False)
                            last = nc.tensor.matmul(o, hid_l[b][:, tok], H[:, w], start=False, stop=(q == FB))
                    last.then_inc(weights_used, 1)
                else:
                    pe.drain().then_inc(weights_used, 1)

            unit(0)
            unit(1)
            with pe.Fori(0, LOOPS) as i:
                for k in range(UNROLL):
                    unit(2 + k, i)
            unit(FB)

        def ffn_act(act, st):
            def unit(q, turn=0):
                if q < FB:
                    split_high(act, st.u0 + q + 1, SLOT, turn)
                    act.wait_ge(gate_up_ready, st.nth * FB + q + 1 + UNROLL * turn)
                    if st.nth * FB + q >= 1:
                        act.wait_ge(hidden_ready, st.nth * FB + q + UNROLL * turn)
                    nc.scalar.activation(silu[:, :], gate_bank[q % 2][:, 0:SEQ], ACT.Silu).then_inc(silu_ready, 1)
                else:
                    if next_unit(st.at) is not None:
                        split_high(act, next_unit(st.at), words(next_unit(st.at)))
                    nc.scalar.activation(idle[:, :], ones[:, 0:1], ACT.Sqrt)

            unit(0)
            unit(1)
            with act.Fori(0, LOOPS) as i:
                for k in range(UNROLL):
                    unit(2 + k, i)
            unit(FB)

        def ffn_dve(dve, st):
            def unit(q, turn=0):
                if q < FB:
                    split_low(dve, st.u0 + q + 1, SLOT, turn)
                    g = st.nth * FB + q
                    dve.wait_ge(silu_ready, g + 1 + UNROLL * turn)
                    nc.vector.tensor_tensor(hidden[:, :], silu[:, :], gate_bank[q % 2][:, SEQ:2 * SEQ],
                                            ALU.mult).then_inc(hidden_made, 1)
                    dve.wait_ge(hidden_made, g + 1 + UNROLL * turn)
                    if g >= 2:
                        dve.wait_ge(weights_used, st.u0 + q + UNROLL * turn)
                    nc.vector.tensor_copy(hid_h[q % 2][:, :], hidden[:, :]).then_inc(hidden_rounded, 1)
                    dve.wait_ge(hidden_rounded, g + 1 + UNROLL * turn)
                    nc.vector.tensor_tensor(hid_l[q % 2][:, :], hidden[:, :], hid_h[q % 2][:, :].bitcast(F32),
                                            ALU.subtract).then_inc(hidden_ready, 1)
                elif next_unit(st.at) is not None:
                    split_low(dve, next_unit(st.at), words(next_unit(st.at)))

            unit(0)
            unit(1)
            with dve.Fori(0, LOOPS) as i:
                for k in range(UNROLL):
                    unit(2 + k, i)
            unit(FB)

        hidden_made = sem("hidden_made")
        hidden_rounded = sem("hidden_rounded")

        def ffn_sync(sp, st):
            load_unit(sp, st.u0, ffn_parts(st, 0, 0, 0))
            load_unit(sp, st.u0 + 1, ffn_parts(st, 1, P, 0))
            for q in range(2, 2 + UNROLL):
                load_unit(sp, st.u0 + q, ffn_parts(st, q, q * P, (q - 1) * P))
            with sp.Fori(1, LOOPS) as i:
                for k in range(UNROLL):
                    q = 2 + k
                    load_unit(sp, st.u0 + q, ffn_parts(st, q, i * (UNROLL * P) + q * P, i * (UNROLL * P) + (q - 1) * P), i)
            load_unit(sp, st.u0 + FB, ffn_parts(st, FB, 0, (FB - 1) * P))


        def proj_pe(pe, st):
            for c, chunk in enumerate(st.chunks):
                u, kb, n = st.u0 + c, chunk.kb, chunk.n
                H, L = high[u % SPLIT], low[u % SPLIT]
                pe.wait_ge(weights_split, u + 1)
                if st.dest == "gate" and c >= 2:
                    pe.wait_ge(emptied, st.e0 + c - 1)
                groups = []
                if st.feature_major:
                    for f in range(n // P):
                        groups.append((gate_bank[c % 2][:, f * SEQ:(f + 1) * SEQ],
                                       [(W[:, k * n + f * P:k * n + (f + 1) * P], xx[:, k, :])
                                        for k in range(kb) for W, xx in ((H, xh), (H, xl), (L, xh))]))
                else:
                    for t in range(NT):
                        if st.dest == "gate":
                            o = gate_bank[c % 2][:, t * CH:t * CH + n]
                        else:
                            o = out_bank[2 * t + c // 2][:, (c % 2) * CH:(c % 2) * CH + n]
                        groups.append((o, [(xx[:, k, t * P:(t + 1) * P], W[:, k * n:(k + 1) * n])
                                           for k in range(kb) for xx, W in ((xh, H), (xh, L), (xl, H))]))
                for o, terms in groups:
                    for j, (a, b) in enumerate(terms):
                        last = nc.tensor.matmul(o, a, b, start=(j == 0), stop=(j == len(terms) - 1))
                last.then_inc(weights_used, 1)

        def proj_act(act, st):
            for c, chunk in enumerate(st.chunks):
                u = st.u0 + c
                if u + 1 < n_units:
                    split_high(act, u + 1, words(u + 1))
                if st.dest == "out" and c == len(st.chunks) - 1:
                    nc.scalar.activation(idle[:, :], ones[:, 0:1], ACT.Sqrt)
                if st.evac is not None and st.by == "act":
                    act.wait_ge(weights_used, u + 1)
                    st.evac(env, c, gate_bank[c % 2], chunk.n).then_inc(emptied, 1)

        def proj_dve(dve, st):
            if st.beside is not None:
                st.beside(env, dve)
            for c, chunk in enumerate(st.chunks):
                u = st.u0 + c
                if u + 1 < n_units:
                    split_low(dve, u + 1, words(u + 1))
                if st.evac is not None and st.by == "dve":
                    dve.wait_ge(weights_used, u + 1)
                    st.evac(env, c, gate_bank[c % 2], chunk.n).then_inc(emptied, 1)

        def proj_sync(sp, st):
            for c, chunk in enumerate(st.chunks):
                u = st.u0 + c
                slot = raw[u % RAW][:, 0:chunk.kb * chunk.n].rearrange("p (k n) -> p k n", k=chunk.kb)
                load_unit(sp, u, [(slot[:, :, at:at + src.shape[2]], src) for at, src in chunk.parts])


        links = [0]

        def link(dve, ins):
            links[0] += 1
            ins.then_inc(dve_link, 1)
            dve.wait_ge(dve_link, links[0])

        act_links = [0]

        def link_act(act, ins):
            act_links[0] += 1
            ins.then_inc(act_link, 1)
            act.wait_ge(act_link, act_links[0])

        def load_gains(act, st):
            for slot, part in enumerate((st.post if st.post_gained else None, st.pre)):
                if part is not None:
                    act.dma_start(gain[slot][:, :], spread(part.gain)).then_inc(gain_loaded[slot], 16)

        def root_of(act, src, slot, scale):
            link_act(act, nc.scalar.activation(sq_scratch[:, :], src, ACT.Square, accum_out=squares[:, slot:slot + 1]))
            nc.scalar.activation(root[:, slot:slot + 1], squares[:, slot:slot + 1], ACT.Sqrt, scale=scale * scale / D,
                                 bias=ln_eps[:, int(scale) - 1:int(scale)]).then_inc(root_ready, 1)

        def cross_act(act, st):
            post, pre = st.post, st.pre
            if st.post_gained:
                for t in range(NT):
                    if post.bias is not None:
                        biases[0] += 1
                        act.wait_ge(biased, biases[0])
                    elif t == 1:
                        free_turns[0] += 1
                        act.wait_ge(tile_free, free_turns[0])
                    root_of(act, y[:, t, :] if post.bias is not None else out_banks[:, t * D:(t + 1) * D], t, 1 / post.scale)
                    if post.bias is not None:
                        act.drain().then_inc(branch_read, 1)
            if pre is not None:
                for t in range(NT):
                    if post is not None:
                        act.wait_ge(h_ready, posts_before(st) + t + 1)
                    root_of(act, h[:, t, :], NT + t, 1)
            if st.turn:
                turn_act(act, st)

        def posts_before(st):
            return NT * len([x for x in crossings if x.post is not None and x.at < st.at])

        biases = [0]
        free_turns = [0]
        bias_read = [0]

        def cross_dve(dve, st):
            post, pre = st.post, st.pre
            v_ = nc.vector
            roots = st.roots0
            if st.post_gained:
                dve.wait_ge(gain_loaded[0], 16 * st.gains[0])
                for t in range(NT):
                    if post.bias is not None:
                        v_.tensor_tensor(y[:, t, :], out_banks[:, t * D:(t + 1) * D], post.bias, ALU.add).then_inc(biased, 1)
                for t in (range(NT) if post.bias is not None else (1, 0)):
                    if post.bias is not None:
                        bias_read[0] += 1
                        dve.wait_ge(branch_read, bias_read[0])
                        last = v_.tensor_tensor(y[:, t, :], y[:, t, :], gain[0][:, :], ALU.mult)
                    else:
                        if t == 0:
                            dve.wait_ge(root_ready, roots + 1)
                        last = v_.tensor_tensor(y[:, t, :], out_banks[:, t * D:(t + 1) * D], gain[0][:, :], ALU.mult)
                        if t == 1:
                            last.then_inc(tile_free, 1)
                link(dve, last)

            def residual(t):
                if post is None:
                    return
                if st.post_gained:
                    dve.wait_ge(root_ready, roots + t + 1)
                    link(dve, v_.reciprocal(rstd[:, t:t + 1], root[:, t:t + 1]))
                    ins = v_.scalar_tensor_tensor(h[:, t, :], y[:, t, :], rstd[:, t:t + 1], h[:, t, :], ALU.mult, ALU.add)
                else:
                    ins = v_.scalar_tensor_tensor(h[:, t, :], out_banks[:, t * D:(t + 1) * D], post.scale, h[:, t, :], ALU.mult, ALU.add)
                ins.then_inc(h_ready, 1)
                dve.wait_ge(h_ready, posts_before(st) + t + 1)

            def gained(t):
                link(dve, v_.tensor_tensor(y[:, t, :], h[:, t, :], gain[1][:, :], ALU.mult))

            def normed(t):
                s = NT + t
                dve.wait_ge(root_ready, roots + NT * st.post_gained + t + 1)
                link(dve, v_.reciprocal(rstd[:, s:s + 1], root[:, s:s + 1]))
                v_.tensor_scalar(y[:, t, :], y[:, t, :], rstd[:, s:s + 1], None, ALU.mult).then_inc(y_ready, 1)

            residual(0)
            if pre is None:
                residual(1)
                return
            dve.wait_ge(gain_loaded[1], 16 * st.gains[1])
            gained(0)
            residual(1)
            normed(0)
            gained(1)
            normed(1)
            if st.turn:
                turn_dve(dve, st)


        def turn_fills(st):
            return [(t, g) for t in range(NT) for g in range(st.kb // 4)]

        def turn_pe(pe, st):
            for x, (t, g) in enumerate(turn_fills(st)):
                f = st.fill0 + x
                if st.kind == "cross":
                    pe.wait_ge(y_ready, st.pre0 + t + 1)
                if x >= 2:
                    pe.wait_ge(turned_low, f - 1)
                for b in range(4):
                    k = 4 * g + b
                    last = nc.tensor.transpose(turn_bank[x % 2][:, b * P:(b + 1) * P],
                                               (y if st.src is None else st.src(mix))[:, t, k * P:(k + 1) * P],
                                               ident[:, :])
                last.then_inc(turned, 1)

        def turn_act(act, st):
            for x, (t, g) in enumerate(turn_fills(st)):
                act.wait_ge(turned, st.fill0 + x + 1)
                nc.scalar.activation(xh[:, 4 * g:4 * g + 4, t * P:(t + 1) * P],
                                     turn_bank[x % 2][:, :].rearrange("p (k n) -> p k n", k=4), ACT.Copy).then_inc(turned_high, 1)

        def turn_dve(dve, st):
            for x, (t, g) in enumerate(turn_fills(st)):
                dve.wait_ge(turned_high, st.fill0 + x + 1)
                nc.vector.tensor_tensor(xl[:, 4 * g:4 * g + 4, t * P:(t + 1) * P],
                                        turn_bank[x % 2][:, :].rearrange("p (k n) -> p k n", k=4),
                                        xh[:, 4 * g:4 * g + 4, t * P:(t + 1) * P].bitcast(F32), ALU.subtract).then_inc(turned_low, 1)


        att = {n: sem("att_" + n) for n in ("scores", "max", "probs", "turned", "copied", "values", "out")}

        def att_bank(st, i, c):
            return out_bank[2 * (i % 2) + c // 512], c % 512

        def att_pe(pe, st):
            a0, n, NK = st.first_item, st.items, st.max_blocks
            for step in range(n + 2):
                i = step
                if i < n:
                    if a0 + i >= 2:
                        pe.wait_ge(att["max"], a0 + i - 1)
                    for c, q, k in st.item(i).scores:
                        b, c0 = att_bank(st, i, c)
                        last = nc.tensor.matmul(b[:, c0:c0 + k.shape[-1]], q, k, start=True, stop=True)
                    last.then_inc(att["scores"], 1)
                i = step - 1
                if 0 <= i < n:
                    pe.wait_ge(att["probs"], a0 + i + 1)
                    free = a0 + i - (0 if NK > 4 else 1)
                    if free > 0:
                        pe.wait_ge(att["copied"], free)
                    for b in range(len(st.item(i).values)):
                        bank_ = turn_bank[b // 4 if NK > 4 else i % 2]
                        last = nc.tensor.transpose(bank_[:, (b % 4) * P:(b % 4 + 1) * P],
                                                   st.probs(i)[:, b * P:(b + 1) * P], ident[:, :])
                    last.then_inc(att["turned"], 1)
                i = step - 2
                if 0 <= i < n:
                    pe.wait_ge(att["copied"], a0 + i + 1)
                    if a0 + i >= 2:
                        pe.wait_ge(att["out"], a0 + i - 1)
                    vs = st.item(i).values
                    for b, v in enumerate(vs):
                        last = nc.tensor.matmul(gate_bank[i % 2][:, 0:v.shape[-1]], st.turned(i)[:, b * P:(b + 1) * P],
                                                v, start=(b == 0), stop=(b == len(vs) - 1))
                    last.then_inc(att["values"], 1)

        def att_act(act, st):
            a0, n = st.first_item, st.items
            for step in range(n + 1):
                i = step
                if i < n:
                    it = st.item(i)
                    if st.load_bias is not None and i == 0:
                        st.load_bias(act, 0)
                        st.load_bias(act, 1)
                    act.wait_ge(att["max"], a0 + i + 1)
                    if st.load_bias is not None and i + 2 < n:
                        st.load_bias(act, i + 2)
                    if st.sink is not None:
                        nc.scalar.activation(st.sink_e[:, i:i + 1], st.sink(i), ACT.Exp, bias=st.negmax[:, i:i + 1])
                    nc.scalar.activation(st.probs(i)[:, 0:it.keys], st.probs(i)[:, 0:it.keys], ACT.Exp,
                                         bias=st.negmax[:, i:i + 1], scale=st.scale,
                                         accum_out=st.sums[:, i:i + 1]).then_inc(att["probs"], 1)
                i = step - 1
                if 0 <= i < n:
                    act.wait_ge(att["turned"], a0 + i + 1)
                    if a0 + i >= 2:
                        act.wait_ge(att["values"], a0 + i - 1)
                    nb = len(st.item(i).values)
                    for g in range(0, nb, 4):
                        m = min(4, nb - g)
                        bank_ = turn_bank[g // 4 if st.max_blocks > 4 else i % 2]
                        last = nc.scalar.activation(st.turned(i)[:, g * P:(g + m) * P], bank_[:, 0:m * P], ACT.Copy)
                    last.then_inc(att["copied"], 1)

        def att_dve(dve, st):
            a0, n = st.first_item, st.items
            for step in range(n + 2):
                i = step
                if i < n:
                    it = st.item(i)
                    if a0 + i >= 2:
                        dve.wait_ge(att["turned"], a0 + i - 1)
                    if st.before is not None:
                        st.before(dve, i)
                    dve.wait_ge(att["scores"], a0 + i + 1)
                    for c in range(0, it.keys, 512):
                        w = min(512, it.keys - c)
                        b, _ = att_bank(st, i, c)
                        dst = st.probs(i)[:, c:c + w]
                        if it.bias is None:
                            last = nc.vector.tensor_copy(dst, b[:, 0:w])
                        else:
                            last = nc.vector.tensor_tensor(dst, b[:, 0:w], it.bias[:, c:c + w], ALU.add)
                    link(dve, last)
                    nm = st.negmax[:, i:i + 1]
                    ins = nc.vector.tensor_reduce(nm, st.probs(i)[:, 0:it.keys], AX.X, ALU.max, negate=True)
                    if st.scale != 1.0:
                        link(dve, ins)
                        ins = nc.vector.tensor_scalar(nm, nm, st.scale, None, ALU.mult)
                    if st.sink is not None:
                        link(dve, ins)
                        ins = nc.vector.tensor_tensor(nm, nm, st.negsink(i), ALU.min)
                    ins.then_inc(att["max"], 1)
                i = step - 2
                if 0 <= i < n:
                    sm = st.sums[:, i:i + 1]
                    dve.wait_ge(att["values"], a0 + i + 1)
                    if st.sink is not None:
                        link(dve, nc.vector.tensor_tensor(sm, sm, st.sink_e[:, i:i + 1], ALU.add))
                    link(dve, nc.vector.reciprocal(sm, sm))
                    it = st.item(i)
                    nc.vector.tensor_scalar(it.out, gate_bank[i % 2][:, 0:it.out.shape[-1]], sm, None,
                                            ALU.mult).then_inc(att["out"], 1)

        own_sems = {}

        def named(name):
            if name not in own_sems:
                own_sems[name] = sem(name)
            return own_sems[name]

        env = Env(nc, mix, y, xh, xl, silu, hidden, ident, ones, sq_scratch, out_bank, gate_bank, turn_bank,
                  link, link_act, named)
        for st in stages:
            if st.setup is not None:
                st.setup(env, st)
            if st.kind == "cross" and st.post is not None and st.post.bias is not None:
                st.post.bias = st.post.bias(mix)

        final = y[:, :, :] if stages[-1].pre is not None else h[:, :, :]
        block = ctx.enter_context(nc.Block())

        @block.sync
        def _(sp):
            sp.dma_start(h[:, :, :], io["x"][0].rearrange("(t p) d -> p t d", p=P)).then_inc(h_loaded, 16)
            for st in stages:
                if st.kind == "ffn":
                    ffn_sync(sp, st)
                elif st.kind == "proj":
                    proj_sync(sp, st)
            sp.wait_ge(done["dve"], len(stages))
            sp.dma_start(out[0].rearrange("(t p) d -> p t d", p=P), final).then_inc(stored, 16)
            sp.wait_ge(stored, 16)


        @block.gpsimd
        def _(pool):
            nc.gpsimd.memset(ones[:, :], 1.0).then_inc(ident_ready, 1)
            nc.gpsimd.memset(ln_eps[:, 0:1], EPS).then_inc(ident_ready, 1)
            nc.gpsimd.memset(ln_eps[:, 1:2], 4 * EPS).then_inc(ident_ready, 1)
            nc.gpsimd.memset(ident[:, :], 0.0).then_inc(ident_zero, 1)
            pool.wait_ge(ident_zero, 1)
            nc.gpsimd.affine_select(out=ident[:, :], in_=ident[:, :], compare_op=ALU.not_equal, fill=1.0,
                                    base=0, pattern=[[-1, P]], channel_multiplier=1).then_inc(ident_ready, 1)

        @block.scalar
        def _(act):
            load_gains(act, crossings[0])
            act.wait_ge(ident_ready, 4)
            act.wait_ge(h_loaded, 16)
            split_high(act, 0, words(0))
            n_loads = 0
            for s, st in enumerate(stages):
                if s and stages[s - 1].kind == "cross" and stages[s - 1] is not crossings[-1]:
                    load_gains(act, crossings[crossings.index(stages[s - 1]) + 1])
                for dst, src in st.loads:
                    if dst == "halves":
                        dst = lambda mix: sq_scratch[:, 0:7 * P].rearrange("p (n s) -> p n s", n=7)
                    act.dma_start(dst(mix), src, allow_slow_non_contiguous=True).then_inc(consts_loaded, 16)
                {"load": lambda e, st: None, "ffn": ffn_act, "proj": proj_act, "cross": cross_act, "turn": turn_act, "attention": att_act,
                 "mixer": lambda e, st: st.act(env, e) if st.act else None}[st.kind](act, st)
                if st.loads:
                    n_loads += len(st.loads)
                    act.wait_ge(consts_loaded, 16 * n_loads)
                barrier(act, "act", s)

        @block.vector
        def _(dve):
            dve.wait_ge(h_loaded, 16)
            split_low(dve, 0, words(0))
            for s, st in enumerate(stages):
                {"load": lambda e, st: None, "ffn": ffn_dve, "proj": proj_dve, "cross": cross_dve, "turn": turn_dve, "attention": att_dve,
                 "mixer": lambda e, st: st.dve(env, e) if st.dve else None}[st.kind](dve, st)
                barrier(dve, "dve", s)

        @block.tensor
        def _(pe):
            pe.wait_ge(ident_ready, 4)
            for s, st in enumerate(stages):
                if st.kind in ("ffn", "proj", "turn", "attention"):
                    {"ffn": ffn_pe, "proj": proj_pe, "turn": turn_pe, "attention": att_pe}[st.kind](pe, st)
                elif st.kind == "cross" and st.turn:
                    turn_pe(pe, st)
                elif st.kind == "mixer" and st.pe:
                    st.pe(env, pe)
                barrier(pe, "pe", s)



HEADS, KV, HD = 16, 4, 64
WINDOW = 128


class Mix:

    def __init__(self, at=0):
        self.at = at

    def take(self, n, shape=None):
        lo = self.at
        self.at += n
        assert self.at <= MIX, self.at

        def place(mix, part=slice(0, P)):
            ap = mix[part, lo:lo + n]
            if shape is not None:
                ap = ap.rearrange("p (a b) -> p a b", a=shape[0])
            return ap
        return place


class Item:
    def __init__(self, scores, keys, bias, values, out):
        self.scores, self.keys, self.bias, self.values, self.out = scores, keys, bias, values, out


def swa(io, j, pre_gain, post_gain):
    w, b = io["swa_w_qkv"][j], io["swa_b_qkv"][j]
    NQ = HEADS * HD
    m = Mix()
    qf = m.take(HEADS // 2 * SEQ, (HEADS // 2, SEQ))
    kf = m.take(KV * SEQ, (KV, SEQ))
    v = m.take(NT * KV * HD, (NT, KV * HD))
    scores = [m.take(SEQ) for _ in range(2)]
    turned = [m.take(SEQ) for _ in range(2)]
    bq, bk = m.take(HEADS // 2), m.take(KV)
    sinks, negsinks = m.take(HEADS), m.take(HEADS)
    negmax, sums, sink_e = m.take(NT * HEADS), m.take(NT * HEADS), m.take(NT * HEADS)
    mask, bv, bo = m.take(SEQ), m.take(KV * HD), m.take(D)
    loads = [(bq, b[0:NQ].rearrange("(c p) -> p c", p=P)),
             (lambda mix: bk(mix, slice(0, HD)), b[NQ:NQ + KV * HD].rearrange("(c p) -> p c", p=HD)),
             (lambda mix: bk(mix, slice(HD, P)), b[NQ:NQ + KV * HD].rearrange("(c p) -> p c", p=HD)),
             (bv, spread(b[NQ + KV * HD:NQ + 2 * KV * HD])),
             (bo, spread(io["swa_b_o"][j])),
             (sinks, spread(io["swa_sinks"][j])),
             (mask, io["c_window"])]
    wk = w.rearrange("(k p) n -> p k n", p=P)
    k_chunks = [Chunk(KB, CH, [(HD * a, wk[:, :, NQ + HD * g:NQ + HD * (g + 1)])
                               for a, g in enumerate((2 * c, 2 * c, 2 * c + 1, 2 * c + 1))]) for c in range(KV // 2)]

    def evac_q(e, c, bank, n):
        for f in range(2):
            last = e.nc.vector.tensor_scalar(qf(e.mix)[:, 2 * c + f, :], bank[:, f * SEQ:(f + 1) * SEQ],
                                             bq(e.mix)[:, 2 * c + f:2 * c + f + 1], HD ** -0.5, ALU.add, ALU.mult)
        return last

    def evac_k(e, c, bank, n):
        for f in range(2):
            last = e.nc.vector.tensor_scalar(kf(e.mix)[:, 2 * c + f, :], bank[:, f * SEQ:(f + 1) * SEQ],
                                             bk(e.mix)[:, 2 * c + f:2 * c + f + 1], None, ALU.add)
        return last

    def evac_v(e, c, bank, n):
        for t in range(NT):
            last = e.nc.vector.tensor_tensor(v(e.mix)[:, t, :], bank[:, t * CH:t * CH + n], bv(e.mix), ALU.add)
        return last

    def setup(e, st):
        mix = e.mix

        def item(i):
            t, hd = i // HEADS, i % HEADS
            rows = slice(HD * (hd % 2), HD * (hd % 2) + HD)
            g = hd // (HEADS // KV)
            keys = P * (t + 1)
            return Item([(0, qf(mix, rows)[:, hd // 2, t * P:(t + 1) * P], kf(mix, rows)[:, g, 0:keys])], keys,
                        mask(mix)[:, SEQ - keys:SEQ], [v(mix)[:, s, g * HD:(g + 1) * HD] for s in range(t + 1)],
                        e.y[:, t, hd * HD:(hd + 1) * HD])

        def before(dve, i):
            if i == 0:
                e.link(dve, e.nc.vector.tensor_scalar(negsinks(mix), sinks(mix), -1.0, None, ALU.mult))

        st.item, st.before, st.load_bias = item, before, None
        st.probs = lambda i: scores[i % 2](mix)
        st.turned = lambda i: turned[i % 2](mix)
        st.negmax, st.sums, st.sink_e = negmax(mix), sums(mix), sink_e(mix)
        st.sink = lambda i: sinks(mix)[:, i % HEADS:i % HEADS + 1]
        st.negsink = lambda i: negsinks(mix)[:, i % HEADS:i % HEADS + 1]

    stages = [Stage("pre", gain=pre_gain), Stage("turn", kb=KB),
              Stage("proj", chunks=columns(w, 0, NQ), feature_major=True, dest="gate", evac=evac_q, by="dve"),
              Stage("proj", chunks=k_chunks, feature_major=True, dest="gate", evac=evac_k, by="dve"),
              Stage("proj", chunks=columns(w, NQ + KV * HD, NQ + 2 * KV * HD), feature_major=False, dest="gate",
                    evac=evac_v, by="dve"),
              Stage("attention", items=NT * HEADS, max_blocks=NT, scale=1.0, setup=setup),
              Stage("turn", kb=KB),
              Stage("proj", chunks=columns(io["swa_w_o"][j], 0, D), feature_major=False, dest="out", evac=None),
              Stage("post", gain=post_gain, norm=True, scale=1.0, bias=bo)]
    return loads, stages


def step(pe=None, act=None, dve=None):
    return Stage("mixer", pe=pe, act=act, dve=dve)



G_HEADS, G_DK, G_DV, G_RANK = 4, 128, 256, 16
G_TEMP = 16.0
G_EPS = 1e-5
G_LEVELS = [P >> n for n in range(8)]


def gla(io, pre_gain, post_gain):
    w = io["gla_w_in"][0]
    QK, V = G_HEADS * G_DK, G_HEADS * G_DV
    m = Mix()
    qf, kf, b = (m.take(G_HEADS * SEQ, (G_HEADS, SEQ)) for _ in range(3))
    v, gate = m.take(NT * V, (NT, V)), m.take(NT * V, (NT, V))
    z = m.take(G_HEADS * SEQ, (G_HEADS, SEQ))
    weights = z
    far = m.take(G_HEADS * P, (G_HEADS, P))
    decay = [m.take(G_HEADS * SEQ, (G_HEADS, SEQ)) for _ in range(2)]
    ke = [m.take(G_HEADS * SEQ, (G_HEADS, SEQ)) for _ in range(2)]
    masks = m.take(8 * P, (8, P))
    ng, bg, w2 = m.take(G_DV), m.take(G_HEADS), m.take(QK)
    low, low_t, ones = m.take(NT * G_RANK, (NT, G_RANK)), m.take(SEQ), m.take(SEQ)
    sq, mean, rt = m.take(8), m.take(8), m.take(8)
    loads = [(masks, io["c_levels"]), (ng, spread(io["gla_norm_g"][0])),
             (bg, io["gla_b_gate"][0].rearrange("(c p) -> p c", p=P)),
             (lambda mix: w2(mix, slice(0, G_RANK)), io["gla_w_gate2"][0])]

    def evac_feature(dst, scale):
        def evac(e, c, bank, n):
            return e.nc.scalar.activation(dst(e.mix)[:, 2 * c:2 * c + 2, :],
                                          bank[:, :].rearrange("p (f n) -> p f n", f=2), ACT.Copy, scale=scale)
        return evac

    def evac_token(dst, func):
        def evac(e, c, bank, n):
            return e.nc.scalar.activation(dst(e.mix)[:, :, c * CH:c * CH + n],
                                          bank[:, :].rearrange("p (t n) -> p t n", t=NT)[:, :, 0:n], func)
        return evac

    def proj(lo, hi, dst, func=ACT.Copy, feature_major=False, scale=1.0):
        return Stage("proj", chunks=columns(w, lo, hi), feature_major=feature_major, dest="gate", by="act",
                     evac=evac_feature(dst, scale) if feature_major else evac_token(dst, func))

    def low_pe(e, pe):
        for t in range(NT):
            e.nc.tensor.transpose(e.turn_bank[0][0:G_RANK, t * P:(t + 1) * P], low(e.mix)[:, t, :], e.ident[:, :])

    def low_dve(e, dve):
        e.nc.vector.memset(ones(e.mix), 1.0)
        e.nc.vector.tensor_copy(low_t(e.mix, slice(0, G_RANK)), e.turn_bank[0][0:G_RANK, 0:SEQ])

    def z_pe(e, pe):
        for hd in range(G_HEADS):
            e.nc.tensor.matmul(e.out_bank[hd // 2][:, (hd % 2) * SEQ:(hd % 2 + 1) * SEQ],
                               w2(e.mix, slice(0, G_RANK))[:, hd * P:(hd + 1) * P], low_t(e.mix, slice(0, G_RANK)),
                               start=True, stop=True)

    def z_dve(e, dve):
        for hd in range(G_HEADS):
            e.nc.vector.tensor_scalar(z(e.mix)[:, hd, :], e.out_bank[hd // 2][:, (hd % 2) * SEQ:(hd % 2 + 1) * SEQ],
                                      bg(e.mix)[:, hd:hd + 1], None, ALU.add)

    def soft_act(e, act):
        t = decay[0](e.mix)
        e.link_act(act, e.nc.scalar.activation(t, z(e.mix), ACT.Abs))
        e.link_act(act, e.nc.scalar.activation(t, t, ACT.Exp, scale=-1.0))
        e.nc.scalar.activation(t, t, ACT.Ln, bias=1.0)

    def sum_dve(e, dve):
        g = ke[0](e.mix)
        e.link(dve, e.nc.vector.scalar_tensor_tensor(g, z(e.mix), 0.0, decay[0](e.mix), ALU.min, ALU.subtract))
        for hd in range(G_HEADS):
            e.nc.vector.tensor_tensor_scan(b(e.mix)[:, hd, :], ones(e.mix), g[:, hd, :], 0.0, ALU.mult, ALU.add)

    def blocks(ap, size):
        return ap.rearrange("p h (x s) -> p (h x) s", s=size)

    n_levels = len(G_LEVELS)
    QE = lambda e, l: e.y[:, l % 2, :].rearrange("p (h s) -> p h s", h=G_HEADS)

    def level_pe(e, pe):
        for l in range(n_levels + 1):
            pe.wait_ge(e.named("gla_scaled"), min(l + 1, n_levels))
            if l >= 2:
                pe.wait_ge(e.named("gla_added"), l - 1)
            q, k = (QE(e, l), ke[l % 2](e.mix)) if l < n_levels else (qf(e.mix), kf(e.mix))
            for hd in range(G_HEADS):
                for t in range(1 if l == 0 else NT):
                    x = hd if l == 0 else t * G_HEADS + hd
                    i = slice(P, 2 * P) if l == 0 else slice(t * P, (t + 1) * P)
                    last = e.nc.tensor.matmul(e.out_bank[2 * (l % 2) + x // 4][:, (x % 4) * P:(x % 4 + 1) * P],
                                              k[:, hd, t * P:(t + 1) * P], q[:, hd, i], start=True, stop=True)
            last.then_inc(e.named("gla_products"), 1)

    def level_act(e, act):
        for l in range(n_levels):
            act.wait_ge(e.named("gla_distance"), l + 1)
            d = decay[l % 2](e.mix)
            e.link_act(act, e.nc.scalar.activation(d, d, ACT.Abs))
            e.nc.scalar.activation(d, d, ACT.Exp, scale=-1.0 / G_TEMP).then_inc(e.named("gla_decay"), 1)

    def level_dve(e, dve):
        for l in range(-1, n_levels + 2):
            if 0 <= l + 1 < n_levels:
                mm = G_LEVELS[l + 1]
                bv = blocks(b(e.mix), 2 * mm)
                e.nc.vector.tensor_tensor(blocks(decay[(l + 1) % 2](e.mix), 2 * mm), bv,
                                          bv[:, :, mm - 1:mm].to_broadcast([P, bv.shape[1], 2 * mm]),
                                          ALU.subtract).then_inc(e.named("gla_distance"), 1)
            if 0 <= l < n_levels:
                dve.wait_ge(e.named("gla_decay"), l + 1)
                if l >= 2:
                    dve.wait_ge(e.named("gla_products"), l - 1)
                e.nc.vector.tensor_tensor(QE(e, l), qf(e.mix), decay[l % 2](e.mix), ALU.mult)
                e.nc.vector.tensor_tensor(ke[l % 2](e.mix), kf(e.mix), decay[l % 2](e.mix),
                                          ALU.mult).then_inc(e.named("gla_scaled"), 1)
                if l + 2 < n_levels:
                    dve.wait_ge(e.named("gla_scaled"), l + 1)
            if 0 <= l - 1 <= n_levels:
                n = l - 1
                dve.wait_ge(e.named("gla_products"), n + 1)
                if n == 0:
                    e.nc.vector.tensor_copy(far(e.mix), e.out_bank[0][:, :].rearrange("p (h n) -> p h n", h=4)).then_inc(e.named("gla_added"), 1)
                    continue
                sv = weights(e.mix).rearrange("p h (t n) -> p (h t) n", t=NT)
                mk = masks(e.mix)[:, n - 1:n, :].to_broadcast([P, 4, P])
                for part in range(2):
                    bank = e.out_bank[2 * (n % 2) + part][:, :].rearrange("p (h n) -> p h n", h=4)
                    dst = sv[:, 4 * part:4 * part + 4, :]
                    if n == 1:
                        last = e.nc.vector.tensor_tensor(dst, bank, mk, ALU.mult)
                    else:
                        tmp = e.sq_scratch[:, 512 * part:512 * part + 512].rearrange("p (h n) -> p h n", h=4)
                        e.link(dve, e.nc.vector.tensor_tensor(tmp, bank, mk, ALU.mult))
                        last = e.nc.vector.tensor_tensor(dst, dst, tmp, ALU.add)
                last.then_inc(e.named("gla_added"), 1)
                dve.wait_ge(e.named("gla_added"), n + 1)

    def value_pe(e, pe):
        sv = weights(e.mix).rearrange("p h (t n) -> p (h t) n", t=NT)
        for t in range(NT):
            for hd in range(G_HEADS):
                x = t * G_HEADS + hd
                o = e.out_bank[x // 2][:, (x % 2) * G_DV:(x % 2 + 1) * G_DV]
                cols = slice(hd * G_DV, (hd + 1) * G_DV)
                if t == 1:
                    e.nc.tensor.matmul(o, far(e.mix)[:, hd, :], v(e.mix)[:, 0, cols], start=True, stop=False)
                e.nc.tensor.matmul(o, sv[:, x, :], v(e.mix)[:, t, cols], start=(t == 0), stop=True)

    def heads_of(e):
        return [e.out_bank[x // 2][:, (x % 2) * G_DV:(x % 2 + 1) * G_DV] for x in range(NT * G_HEADS)]

    def sq_act(e, act):
        for x, o in enumerate(heads_of(e)):
            e.link_act(act, e.nc.scalar.activation(e.sq_scratch[:, 0:G_DV], o, ACT.Square, accum_out=sq(e.mix)[:, x:x + 1]))

    def mean_dve(e, dve):
        e.nc.vector.tensor_scalar(mean(e.mix), sq(e.mix), 1.0 / G_DV, G_EPS, ALU.mult, ALU.add)

    def root_act(e, act):
        e.nc.scalar.activation(rt(e.mix), mean(e.mix), ACT.Sqrt)

    def out_dve(e, dve):
        e.link(dve, e.nc.vector.reciprocal(rt(e.mix), rt(e.mix)))
        for x, o in enumerate(heads_of(e)):
            t, hd = x // G_HEADS, x % G_HEADS
            last = e.nc.vector.scalar_tensor_tensor(e.y[:, t, hd * G_DV:(hd + 1) * G_DV], o, rt(e.mix)[:, x:x + 1],
                                                    ng(e.mix), ALU.mult, ALU.mult)
        e.link(dve, last)
        e.nc.vector.tensor_tensor(e.y[:, :, :], e.y[:, :, :], gate(e.mix), ALU.mult)

    stages = [Stage("pre", gain=pre_gain), Stage("turn", kb=KB),
              proj(0, QK, qf, feature_major=True, scale=G_DK ** -0.5), proj(QK, 2 * QK, kf, feature_major=True),
              proj(2 * QK, 2 * QK + V, v), proj(2 * QK + V, 2 * QK + 2 * V, gate, ACT.Silu),
              proj(2 * QK + 2 * V, 2 * QK + 2 * V + G_RANK, low),
              step(pe=low_pe), step(dve=low_dve), step(pe=z_pe), step(dve=z_dve), step(act=soft_act), step(dve=sum_dve),
              step(level_pe, level_act, level_dve), step(pe=value_pe), step(act=sq_act), step(dve=mean_dve),
              step(act=root_act), step(dve=out_dve),
              Stage("turn", kb=KB),
              Stage("proj", chunks=columns(io["gla_w_o"][0], 0, D), feature_major=False, dest="out", evac=None),
              Stage("post", gain=post_gain, norm=True, scale=1.0, bias=None)]
    return loads, stages


def level_masks():
    import numpy as np
    j, i = np.arange(P)[:, None], np.arange(P)[None, :]
    out = [((j // (2 * m) == i // (2 * m)) & (j // m < i // m)) for m in G_LEVELS[1:]] + [j == i]
    return np.stack(out, 1).astype(np.float32)



R_HEADS, R_HD = 16, 64
R_PAIRS = R_HEADS // 2
KAPPA = 0.6065306597126334
R_LEVELS = [1 << n for n in range(7)]
LNX_EPS = 64e-5
MID = P // 2 - 1


def rwkv_constants():
    import numpy as np
    f = np.arange(P)
    s, t = f[:, None], f[None, :]
    order = np.stack([s < t, s <= t], 1).astype(np.float32)
    halves = np.stack([(s // (2 * m) == t // (2 * m)) & (s // m < t // m) for m in R_LEVELS], 1).astype(np.float32)
    lower = np.ascontiguousarray(halves[:, 0, :].T)
    same = (s // R_HD == t // R_HD).astype(np.float32)
    sel = (s // R_HD == np.arange(2)[None, :]).astype(np.float32)
    return {"c_order": order, "c_halves": halves, "c_pairs": lower, "c_same": same, "c_sel": sel}


def rwkv(io, pre_gain, post_gain):
    SH = (R_PAIRS, SEQ)
    m = Mix()
    R0, R1, R2, R3, R4 = (m.take(R_PAIRS * SEQ, SH) for _ in range(5))
    uf, sw, em = R0, R0, R0
    dx, af = R1, R1
    rf, kf = R2, R3
    flat = lambda place, lo=0, n=R_PAIRS * SEQ: (lambda mix, part=slice(0, P): place(mix, part).rearrange("p a b -> p (a b)")[:, lo:lo + n])
    tok = lambda place: (lambda mix: place(mix).rearrange("p a b -> p (a b)").rearrange("p (t d) -> p t d", t=NT))
    v = tok(R4)
    result = tok(R3)
    core = m.at
    lora, wa = m.take(D), m.take(SEQ)
    m = Mix(core)
    T1 = m.take(R_PAIRS * SEQ, SH)
    EP = m.take(2 * R_PAIRS * (P + 1), (2 * R_PAIRS, P + 1))
    end = m.at
    m = Mix(core)
    U4 = (4, P)
    TT, MT, Z = (m.take(4 * P, U4) for _ in range(3))
    XX = m.take(8 * P, (8, P))
    grams0 = [m.take(4 * P, U4) for _ in range(3)]
    assert m.at <= end, (m.at, end)
    m1 = Mix(0)
    grams1 = [m1.take(4 * P, U4) for _ in range(3)]
    XT = m1.take(4 * P, U4)
    AK, RB, RK = ((lambda n: lambda mix, c: (grams0, grams1)[c % 2][n](mix))(n) for n in range(3))
    m = Mix(max(m.at, end))
    rhs = m.take(2 * R_HD, (2, R_HD))
    order, pairs, same = m.take(2 * P, (2, P)), m.take(P), m.take(P)
    sel = m.take(2)
    mu = m.take(6 * KB, (6, KB))
    w0, a0, k_k, k_a, one_ka, r_k = (m.take(KB) for _ in range(6))
    kcm, nkcm, gamma, tail = m.take(16, (R_PAIRS, NT)), m.take(16, (R_PAIRS, NT)), m.take(8), m.take(8)
    bonus = m.take(NT * R_HEADS, (NT, R_HEADS))
    mean, var = m.take(32), m.take(32)
    bk = m.take(2 * P, (2, P))
    lnx_g, lnx_b = flat(R0, 0, D), flat(R0, D, D)
    g2a, g2b = flat(R2, 0, D), flat(R2, D, D)

    def col(a):
        return a.rearrange("(c p) -> p c", p=P)

    loads = [(order, io["c_order"]), (pairs, io["c_pairs"]), (same, io["c_same"]), (sel, io["c_sel"])]
    loads += [((lambda i: lambda mix: mu(mix)[:, i, :])(i), col(io["rwkv_mu"][0, i])) for i in range(6)]
    loads += [(dst, col(io[n][0])) for dst, n in ((w0, "rwkv_w0"), (a0, "rwkv_a0"), (k_k, "rwkv_k_k"), (k_a, "rwkv_k_a"))]
    loads += [(r_k, col(io["rwkv_r_k"][0].rearrange("h n -> (h n)"))),
              (lambda mix: lora(mix, slice(0, R_HD)), io["rwkv_w2"][0]),
              (lambda mix: lora(mix, slice(R_HD, P)), io["rwkv_a2"][0])]

    fills = [[(t, k) for t in range(NT) for k in range(KB)][f:f + 4] for f in range(0, NT * KB, 4)]

    def turn_pe(e, pe):
        for f, blocks in enumerate(fills):
            if f >= 2:
                pe.wait_ge(e.named("u_copied"), f - 1)
            for b, (t, k) in enumerate(blocks):
                last = e.nc.tensor.transpose(e.turn_bank[f % 2][:, b * P:(b + 1) * P], e.y[:, t, k * P:(k + 1) * P], e.ident[:, :])
            last.then_inc(e.named("u_turned"), 1)

    def turn_act(e, act):
        for f, blocks in enumerate(fills):
            act.wait_ge(e.named("u_turned"), f + 1)
            t, k = blocks[0]
            e.nc.scalar.activation(uf(e.mix)[:, k:k + 4, t * P:(t + 1) * P],
                                   e.turn_bank[f % 2][:, :].rearrange("p (k n) -> p k n", k=4), ACT.Copy).then_inc(e.named("u_copied"), 1)

    def mixed(e):
        return e.y[:, :, :].rearrange("p t d -> p (t d)").rearrange("p (k s) -> p k s", k=KB)

    def blend(e, dve, i):
        e.link(dve, e.nc.vector.tensor_tensor(mixed(e), dx(e.mix), along(mu(e.mix)[:, i, :], SEQ), ALU.mult))
        e.nc.vector.tensor_tensor(mixed(e), mixed(e), uf(e.mix), ALU.add)

    def shift_dve(e, dve):
        u, d = uf(e.mix), dx(e.mix)
        e.nc.vector.tensor_tensor(d[:, :, 1:SEQ], u[:, :, 0:SEQ - 1], u[:, :, 1:SEQ], ALU.subtract)
        e.nc.vector.tensor_scalar(one_ka(e.mix), k_a(e.mix), -1.0, 1.0, ALU.mult, ALU.add)
        e.link(dve, e.nc.vector.tensor_scalar(d[:, :, 0:1], u[:, :, 0:1], -1.0, None, ALU.mult))
        blend(e, dve, ORDER[0])

    def high_act(e, act):
        for half in range(2):
            k = slice(4 * half, 4 * half + 4)
            e.nc.scalar.activation(e.xh[:, k, :], mixed(e)[:, k, :], ACT.Copy).then_inc(e.named("blend_high"), 1)

    def low_dve(n):
        def dve_(e, dve):
            for half in range(2):
                k = slice(4 * half, 4 * half + 4)
                dve.wait_ge(e.named("blend_high"), 2 * n + half + 1)
                e.nc.vector.tensor_tensor(e.xl[:, k, :], mixed(e)[:, k, :], e.xh[:, k, :].bitcast(F32), ALU.subtract)
        return dve_

    ORDER = [0, 2, 3, 1, 4, 5]

    def evac_feature(dst):
        def evac(e, c, bank, n):
            return e.nc.scalar.activation(dst(e.mix)[:, 2 * c:2 * c + 2, :], bank[:, :].rearrange("p (f n) -> p f n", f=2), ACT.Copy)
        return evac

    def evac_v(e, c, bank, n):
        return e.nc.scalar.activation(v(e.mix)[:, :, c * CH:(c + 1) * CH], bank[:, :].rearrange("p (t n) -> p t n", t=NT), ACT.Copy)

    def evac_w(e, c, bank, n):
        return e.nc.scalar.activation(wa(e.mix, slice(0, R_HD)), bank[0:R_HD, 0:SEQ], ACT.Tanh)

    def evac_a(e, c, bank, n):
        return e.nc.scalar.activation(wa(e.mix, slice(R_HD, P)), bank[R_HD:P, 0:SEQ], ACT.Copy)

    def evac_g(e, c, bank, n):
        e.nc.scalar.activation(e.silu[:, :], bank[:, 0:SEQ], ACT.Sigmoid)
        return e.nc.scalar.activation(e.hidden[0:32, :], bank[0:32, SEQ:2 * SEQ], ACT.Sigmoid)

    def rows(a):
        return a.rearrange("(k p) n -> p k n", p=P)

    w1, a1, g1 = (rows(io[n][0]) for n in ("rwkv_w1", "rwkv_a1", "rwkv_g1"))
    twice = lambda a: [Chunk(KB, P, [(0, a), (R_HD, a)])]
    GR = 160
    chunks = {0: columns(io["rwkv_w_rkv"][0, 0], 0, D), 2: columns(io["rwkv_w_rkv"][0, 1], 0, D),
              3: columns(io["rwkv_w_rkv"][0, 2], 0, D), 1: twice(w1), 4: twice(a1),
              5: [Chunk(KB, CH, [(0, g1), (GR, g1[:, :, 0:CH - GR])])]}
    evacs = {0: evac_feature(rf), 2: evac_feature(kf), 3: evac_v, 1: evac_w, 4: evac_a, 5: evac_g}

    def beside(n):
        return lambda e, dve: blend(e, dve, ORDER[n + 1]) if n + 1 < len(ORDER) else None

    inputs = []
    for n, i in enumerate(ORDER):
        inputs += [step(act=high_act, dve=low_dve(n)),
                   Stage("proj", chunks=chunks[i], feature_major=(i != 3), dest="gate", by="act", evac=evacs[i],
                         beside=beside(n), loads=[("halves", io["c_halves"])] if n == 0 else [])]

    def lora_pe(part):
        def pe_(e, pe):
            r = slice(0, R_HD) if part == 0 else slice(R_HD, P)
            for c in range(KB):
                e.nc.tensor.matmul(e.out_bank[c // 2][:, (c % 2) * SEQ:(c % 2 + 1) * SEQ],
                                   lora(e.mix, r)[:, c * P:(c + 1) * P], wa(e.mix, r), start=True, stop=True)
        return pe_

    def lora_act(dst, bias):
        def act_(e, act):
            for c in range(KB):
                e.nc.scalar.activation(dst(e.mix)[:, c, :], e.out_bank[c // 2][:, (c % 2) * SEQ:(c % 2 + 1) * SEQ],
                                       ACT.Sigmoid, bias=bias(e.mix)[:, c:c + 1])
        return act_

    A = mixed

    def kk_dve(e, dve):
        e.nc.vector.tensor_tensor(A(e), kf(e.mix), along(k_k(e.mix), SEQ), ALU.mult)

    def kk_act(e, act):
        e.nc.scalar.activation(T1(e.mix), A(e), ACT.Square)

    def kk_pe(e, pe):
        for c in range(KB):
            e.nc.tensor.matmul(e.out_bank[c // 2][:, (c % 2) * SEQ:(c % 2 + 1) * SEQ], same(e.mix), T1(e.mix)[:, c, :],
                               start=True, stop=True)

    def norm_act(e, act):
        for b in range(4):
            e.nc.scalar.activation(T1(e.mix)[:, 2 * b:2 * b + 2, :], e.out_bank[b][:, :].rearrange("p (k s) -> p k s", k=2), ACT.Sqrt)

    def second(e):
        return EP(e.mix).rearrange("p a b -> p (a b)")[:, 0:R_PAIRS * SEQ].rearrange("p (k s) -> p k s", k=KB)

    def prep_dve(e, dve):
        vv, t1, t2, k, r = e.nc.vector, T1(e.mix), second(e), kf(e.mix), rf(e.mix)
        e.link(dve, vv.tensor_scalar(t1, t1, 1e-12, None, ALU.max))
        e.link(dve, vv.reciprocal(t1, t1))
        vv.tensor_tensor(A(e), A(e), t1, ALU.mult)
        for c in range(KB):
            last = vv.tensor_scalar(t2[:, c, :], af(e.mix)[:, c, :], k_a(e.mix)[:, c:c + 1], one_ka(e.mix)[:, c:c + 1],
                                    ALU.mult, ALU.add)
        e.link(dve, last)
        e.link(dve, vv.tensor_tensor(k, k, t2, ALU.mult))
        e.link(dve, vv.tensor_tensor(t2, k, r, ALU.mult))
        for c in range(KB):
            last = vv.tensor_scalar(t2[:, c, :], t2[:, c, :], r_k(e.mix)[:, c:c + 1], None, ALU.mult)
        e.link(dve, vv.tensor_tensor(af(e.mix), af(e.mix), A(e), ALU.mult))

    def bonus_pe(e, pe):
        for t in range(NT):
            for c in range(R_PAIRS):
                e.nc.tensor.matmul(e.gate_bank[0][:, t * R_HEADS + 2 * c:t * R_HEADS + 2 * c + 2],
                                   second(e)[:, c, t * P:(t + 1) * P], sel(e.mix), start=True, stop=True)

    def sum_dve(e, dve):
        vv = e.nc.vector
        for c in range(R_PAIRS):
            for t in range(NT):
                s = slice(t * P, (t + 1) * P)
                last = vv.tensor_tensor_scan(T1(e.mix)[:, c, s], e.ones[:, :], sw(e.mix)[:, c, s], 0.0, ALU.mult, ALU.add)
        e.link(dve, last)
        cm = T1(e.mix).rearrange("p c (t s) -> p c t s", t=NT)[:, :, :, MID]
        vv.tensor_scalar(kcm(e.mix), cm, KAPPA, None, ALU.mult)
        vv.tensor_scalar(nkcm(e.mix), cm, -KAPPA, None, ALU.mult)

    def exp_act(e, act):
        for c in range(R_PAIRS):
            for t in range(NT):
                src = T1(e.mix)[:, c, t * P:(t + 1) * P]
                e.nc.scalar.activation(EP(e.mix)[:, c * NT + t, 1:P + 1], src, ACT.Exp, scale=-KAPPA, bias=kcm(e.mix)[:, c, t:t + 1])
                e.nc.scalar.activation(em(e.mix)[:, c, t * P:(t + 1) * P], src, ACT.Exp, scale=KAPPA, bias=nkcm(e.mix)[:, c, t:t + 1])
        e.nc.scalar.activation(EP(e.mix)[:, :, 0], kcm(e.mix).rearrange("p c t -> p (c t)"), ACT.Exp)
        e.nc.scalar.activation(tail(e.mix), nkcm(e.mix)[:, :, 1], ACT.Exp)

    def bonus_dve(e, dve):
        e.nc.vector.tensor_copy(bonus(e.mix), e.gate_bank[0][:, 0:NT * R_HEADS].rearrange("p (t h) -> p t h", t=NT))

    def scale_dve(e, dve):
        vv = e.nc.vector
        ct = lambda ap: ap.rearrange("p c (t s) -> p (c t) s", t=NT)
        vv.tensor_tensor(gamma(e.mix), EP(e.mix).rearrange("p (c t) s -> p c t s", t=NT)[:, :, 0, P], tail(e.mix), ALU.mult)
        vv.tensor_tensor(af(e.mix), af(e.mix), em(e.mix), ALU.mult)
        vv.tensor_tensor(kf(e.mix), kf(e.mix), em(e.mix), ALU.mult)
        vv.scalar_tensor_tensor(ct(A(e)), ct(A(e)), -1.0, EP(e.mix)[:, :, 0:P], ALU.mult, ALU.mult)
        vv.tensor_tensor(ct(rf(e.mix)), ct(rf(e.mix)), EP(e.mix)[:, :, 1:P + 1], ALU.mult)

    NL = len(R_LEVELS) - 1

    def state(e, q):
        return same(e.mix, slice(R_HD * q, R_HD * q + R_HD))[:, 0:R_HD]

    def core_pe(e, pe):
        t_, mix, S = e.nc.tensor, e.mix, e.named
        rows_ = [slice(R_HD * q, R_HD * q + R_HD) for q in range(2)]

        def F(place, c, q, t):
            return place(mix, rows_[q])[:, c, t * P:(t + 1) * P]

        def At(c, q, t):
            flat_ = e.y[rows_[q], :, :].rearrange("p t d -> p (t d)")
            return flat_[:, c * SEQ + t * P:c * SEQ + (t + 1) * P]

        def factors(c):
            if c >= 2:
                pe.wait_ge(S("rw_stored"), NT * (c - 1))
            for q in range(2):
                for t in range(NT):
                    lo, hi = slice(t * P, (t + 1) * P), slice((2 + t) * P, (3 + t) * P)
                    A_, B_, K_, R_ = At(c, q, t), F(af, c, q, t), F(kf, c, q, t), F(rf, c, q, t)
                    t_.matmul(e.gate_bank[q][:, lo], A_, B_, start=True, stop=True)
                    t_.matmul(e.out_bank[2 * q][:, lo], B_, A_, start=True, stop=True)
                    t_.matmul(e.out_bank[2 * q][:, hi], K_, A_, start=True, stop=True)
                    t_.matmul(e.out_bank[2 * q + 1][:, lo], B_, R_, start=True, stop=True)
                    last = t_.matmul(e.out_bank[2 * q + 1][:, hi], K_, R_, start=True, stop=True)
            last.then_inc(S("rw_grams"), 1)

        def mx(c, n):
            for q in range(2):
                pe.wait_ge(S("rw_joined"), (c * (NL + 1) + n) * 2 + q + 1)
                for t in range(NT):
                    u = 2 * q + t
                    last = t_.matmul(e.gate_bank[q][:, t * P:(t + 1) * P], MT(mix)[:, u, :], XX(mix)[:, 2 * u, :],
                                     start=True, stop=True)
                last.then_inc(S("rw_mx"), 1)

        def xmx(c, n):
            for q in range(2):
                pe.wait_ge(S("rw_mx_copied"), (c * NL + n) * 2 + q + 1)
                for t in range(NT):
                    u = 2 * q + t
                    if n < NL - 1:
                        t_.matmul(e.turn_bank[q][:, 2 * t * P:(2 * t + 1) * P], XX(mix)[:, 2 * u + 1, :], Z(mix)[:, u, :],
                                  start=True, stop=True)
                    last = t_.matmul(e.turn_bank[q][:, (2 * t + 1) * P:(2 * t + 2) * P], Z(mix)[:, u, :],
                                     XX(mix)[:, 2 * u + 1, :], start=True, stop=True)
                last.then_inc(S("rw_xmx"), 1)

        def right_side(c, t):
            if t == 0:
                pe.wait_ge(S("rw_masked"), min(c + 2, R_PAIRS))
                if c > 0:
                    pe.wait_ge(S("rw_stored"), NT * c)
                t_.transpose(e.out_bank[3][:, P:2 * P], af(mix)[:, c, 0:P], e.ident[:, :])
                t_.transpose(e.out_bank[3][:, 2 * P:3 * P], kf(mix)[:, c, 0:P], e.ident[:, :]).then_inc(S("rw_bk"), 1)
            else:
                pe.wait_ge(S("rw_state_ready"), c + 1)
                pe.wait_ge(S("rw_stored"), NT * c + 1)
            for q in range(2):
                o = e.out_bank[q][:, 0:R_HD]
                last = t_.matmul(o, AK(mix, c)[:, 2 * q + t, :], V(c, q, t), start=True, stop=(t == 0))
                if t == 1:
                    last = t_.matmul(o, At(c, q, t), state(e, q), start=False, stop=True)
            last.then_inc(S("rw_rhs"), 1)

        def V(c, q, t):
            return v(mix)[:, t, c * P + R_HD * q:c * P + R_HD * q + R_HD]

        def solve(c, t):
            if t == 0:
                pe.wait_ge(S("rw_joined"), (c * (NL + 1) + NL) * 2 + 2)
            pe.wait_ge(S("rw_rhs_copied"), NT * c + t + 1)
            for q in range(2):
                last = t_.matmul(e.out_bank[2][:, q * R_HD:(q + 1) * R_HD], XT(mix)[:, 2 * q + t, :], rhs(mix)[:, q, :],
                                 start=True, stop=True)
            last.then_inc(S("rw_u"), 1)

        def output(c, t):
            pe.wait_ge(S("rw_u_copied"), NT * c + t + 1)
            if t == 0:
                pe.wait_ge(S("rw_bk_copied"), c + 1)
                for q in range(2):
                    cols = slice(q * R_HD, (q + 1) * R_HD)
                    o = e.out_bank[3][cols, 0:R_HD]
                    t_.matmul(o, bk(mix)[:, 0, cols], rhs(mix)[:, q, :], start=True, stop=False)
                    last = t_.matmul(o, bk(mix)[:, 1, cols], V(c, q, 0), start=False, stop=True)
                last.then_inc(S("rw_state"), 1)
            for q in range(2):
                o = e.out_bank[q][:, R_HD:2 * R_HD]
                t_.matmul(o, RB(mix, c)[:, 2 * q + t, :], rhs(mix)[:, q, :], start=True, stop=False)
                last = t_.matmul(o, RK(mix, c)[:, 2 * q + t, :], V(c, q, t), start=False, stop=(t == 0))
                if t == 1:
                    last = t_.matmul(o, F(rf, c, q, t), state(e, q), start=False, stop=True)
            last.then_inc(S("rw_y"), 1)

        factors(0)
        for c in range(R_PAIRS + 1):
            for n in range(NL):
                if c < R_PAIRS:
                    mx(c, n)
                if c > 0:
                    (right_side, solve, output)[n % 3](c - 1, n // 3)
                if c < R_PAIRS:
                    xmx(c, n)
            if c + 1 < R_PAIRS:
                factors(c + 1)

    def core_act(e, act):
        mix, S, copy = e.mix, e.named, e.nc.scalar.activation

        def hop(c, n):
            t = n // 3
            if n % 3 == 0:
                if t == 0:
                    act.wait_ge(S("rw_bk"), c + 1)
                    copy(bk(mix), e.out_bank[3][:, P:3 * P].rearrange("p (t s) -> p t s", t=2), ACT.Copy).then_inc(S("rw_bk_copied"), 1)
                act.wait_ge(S("rw_rhs"), NT * c + t + 1)
                if NT * c + t > 0:
                    act.wait_ge(S("rw_y"), NT * c + t)
                copy(rhs(mix)[:, 0, :], e.out_bank[0][:, 0:R_HD], ACT.Copy)
                copy(rhs(mix)[:, 1, :], e.out_bank[1][:, 0:R_HD], ACT.Copy).then_inc(S("rw_rhs_copied"), 1)
            elif n % 3 == 1:
                act.wait_ge(S("rw_u"), NT * c + t + 1)
                copy(rhs(mix), e.out_bank[2][:, 0:P].rearrange("p (q d) -> p q d", q=2), ACT.Copy).then_inc(S("rw_u_copied"), 1)
            else:
                act.wait_ge(S("rw_y"), NT * c + t + 1)
                for q in range(2):
                    last = copy(A(e)[:, c, t * P + q * R_HD:t * P + (q + 1) * R_HD], e.out_bank[q][:, R_HD:2 * R_HD], ACT.Copy)
                last.then_inc(S("rw_stored"), 1)

        for c in range(R_PAIRS + 1):
            for n in range(NL):
                for q in range(2 if c < R_PAIRS else 0):
                    act.wait_ge(S("rw_mx"), (c * NL + n) * 2 + q + 1)
                    copy(Z(mix)[:, 2 * q:2 * q + 2, :], e.gate_bank[q][:, 0:2 * P].rearrange("p (t s) -> p t s", t=2),
                         ACT.Copy).then_inc(S("rw_mx_copied"), 1)
                if c > 0:
                    hop(c - 1, n)

    def core_dve(e, dve):
        mix, S, vv = e.mix, e.named, e.nc.vector
        sm = order(mix)[:, 0:1, :].to_broadcast([P, 2, P])
        im = order(mix)[:, 1:2, :].to_broadcast([P, 2, P])
        idb = e.ident[:, :].unsqueeze(1).to_broadcast([P, 2, P])
        low_ = pairs(mix).unsqueeze(1).to_broadcast([P, 2, P])

        def level(n):
            return halves(e)[:, n:n + 1, :].to_broadcast([P, 2, P])

        def gram(q, b, part):
            return e.out_bank[2 * q + b][:, part * 2 * P:(part + 1) * 2 * P].rearrange("p (t s) -> p t s", t=2)

        for c in range(R_PAIRS + 1):
            if c < R_PAIRS:
                dve.wait_ge(S("rw_grams"), c + 1)
                for q in range(2):
                    last = vv.tensor_tensor(TT(mix)[:, 2 * q:2 * q + 2, :], gram(q, 0, 0), sm, ALU.mult)
                e.link(dve, last)
                xx = XX(mix).rearrange("p (u two) s -> p u two s", two=2)
                for q in range(2):
                    us = slice(2 * q, 2 * q + 2)
                    vv.tensor_tensor(xx[:, us, 0, :], e.gate_bank[q][:, 0:2 * P].rearrange("p (t s) -> p t s", t=2), low_, ALU.mult)
                    last = vv.tensor_tensor(xx[:, us, 1, :], TT(mix)[:, us, :], level(0), ALU.mult)
                e.link(dve, last)
                for q in range(2):
                    us = slice(2 * q, 2 * q + 2)
                    vv.tensor_tensor(xx[:, us, 0, :], xx[:, us, 0, :], idb, ALU.add)
                    vv.tensor_tensor(xx[:, us, 1, :], xx[:, us, 1, :], idb, ALU.add)
                    vv.tensor_tensor(MT(mix)[:, us, :], TT(mix)[:, us, :], level(1), ALU.mult).then_inc(S("rw_joined"), 1)
                if c >= 2:
                    dve.wait_ge(S("rw_y"), NT * (c - 1))
                for q in range(2):
                    us = slice(2 * q, 2 * q + 2)
                    vv.tensor_tensor(AK(mix, c)[:, us, :], gram(q, 0, 1), sm, ALU.mult)
                    vv.tensor_tensor(RB(mix, c)[:, us, :], gram(q, 1, 0), im, ALU.mult)
                    last = vv.tensor_tensor(RK(mix, c)[:, us, :], gram(q, 1, 1), im, ALU.mult)
                last.then_inc(S("rw_masked"), 1)
            for n in range(NL):
                if n == 2 and c > 0:
                    dve.wait_ge(S("rw_state"), c)
                    vv.tensor_scalar(same(mix)[:, 0:R_HD], e.out_bank[3][:, 0:R_HD], gamma(mix)[:, c - 1:c], None,
                                     ALU.mult).then_inc(S("rw_state_ready"), 1)
                for q in range(2 if c < R_PAIRS else 0):
                    us = slice(2 * q, 2 * q + 2)
                    dve.wait_ge(S("rw_xmx"), (c * NL + n) * 2 + q + 1)
                    if n < NL - 1:
                        x2 = XX(mix)[:, 4 * q:4 * q + 4, :]
                        vv.tensor_tensor(x2, x2, e.turn_bank[q][:, :].rearrange("p (u s) -> p u s", u=4), ALU.add)
                        vv.tensor_tensor(MT(mix)[:, us, :], TT(mix)[:, us, :], level(n + 2), ALU.mult).then_inc(S("rw_joined"), 1)
                    else:
                        if c > 0 and q == 0:
                            dve.wait_ge(S("rw_u"), NT * c)
                        tb = e.turn_bank[q][:, :].rearrange("p (u two s) -> p u two s", u=2, two=2)
                        vv.tensor_tensor(XT(mix)[:, us, :], xx[:, us, 1, :], tb[:, :, 1, :], ALU.add).then_inc(S("rw_joined"), 1)

    def g_pe(e, pe):
        for t in range(NT):
            for n in range(2):
                o, s = e.out_bank[2 * t + n][:, :], slice(512 * n, 512 * (n + 1))
                e.nc.tensor.matmul(o, e.silu[:, t * P:(t + 1) * P], g2a(e.mix)[:, s], start=True, stop=False)
                e.nc.tensor.matmul(o, e.hidden[0:32, t * P:(t + 1) * P], g2b(e.mix, slice(0, 32))[:, s], start=False, stop=True)

    def groups(e):
        return A(e).rearrange("p c s -> p (c s)").rearrange("p (g d) -> p g d", d=R_HD)

    def mean_dve(e, dve):
        vv, y_ = e.nc.vector, groups(e)
        e.link(dve, vv.tensor_reduce(mean(e.mix), y_, AX.X, ALU.add))
        e.link(dve, vv.tensor_scalar(mean(e.mix), mean(e.mix), 1.0 / R_HD, None, ALU.mult))
        e.link(dve, vv.tensor_tensor(y_, y_, along(mean(e.mix), R_HD), ALU.subtract))
        sq = T1(e.mix).rearrange("p c s -> p (c s)").rearrange("p (g d) -> p g d", d=R_HD)
        e.link(dve, vv.tensor_tensor(sq, y_, y_, ALU.mult))
        e.link(dve, vv.tensor_reduce(var(e.mix), sq, AX.X, ALU.add))
        vv.tensor_scalar(var(e.mix), var(e.mix), 1.0 / R_HD, LNX_EPS, ALU.mult, ALU.add)

    def root_act(e, act):
        e.nc.scalar.activation(var(e.mix), var(e.mix), ACT.Sqrt)

    def gate_dve(e, dve):
        vv, y_ = e.nc.vector, groups(e)
        e.link(dve, vv.reciprocal(var(e.mix), var(e.mix)))
        e.link(dve, vv.tensor_tensor(y_, y_, along(var(e.mix), R_HD), ALU.mult))
        for t in range(NT):
            yt = A(e).rearrange("p c (t s) -> p c t s", t=NT)[:, :, t, :]
            wide = lambda ap: ap.rearrange("p (c s) -> p c s", s=P)
            out_ = result(e.mix)[:, t, :]
            heads = lambda ap: ap.rearrange("p (h d) -> p h d", d=R_HD)
            e.link(dve, vv.tensor_tensor(yt, yt, wide(lnx_g(e.mix)), ALU.mult))
            e.link(dve, vv.tensor_tensor(yt, yt, wide(lnx_b(e.mix)), ALU.add))
            e.link(dve, vv.tensor_tensor(heads(out_), heads(v(e.mix)[:, t, :]), along(bonus(e.mix)[:, t, :], R_HD), ALU.mult))
            e.link(dve, vv.tensor_tensor(wide(out_), wide(out_), yt, ALU.add))
            for n in range(2):
                o = result(e.mix)[:, t, 512 * n:512 * (n + 1)]
                vv.tensor_tensor(o, o, e.out_bank[2 * t + n][:, :], ALU.mult)

    def halves(e):
        return e.sq_scratch[:, 0:7 * P].rearrange("p (n s) -> p n s", n=7)

    def after_step():
        s = step(dve=mean_dve)
        s.loads = [(g2a, io["rwkv_g2"][0, 0:P, :]), (lambda mix: g2b(mix, slice(0, 32)), io["rwkv_g2"][0, P:GR, :]),
                   (lnx_g, spread(io["rwkv_lnx_g"][0])), (lnx_b, spread(io["rwkv_lnx_b"][0]))]
        return s

    stages = [Stage("pre", gain=pre_gain), step(turn_pe, turn_act), step(dve=shift_dve)] + inputs + [
              step(pe=lora_pe(0)), step(act=lora_act(sw, w0)), step(pe=lora_pe(1)), step(act=lora_act(af, a0)),
              step(dve=kk_dve), step(act=kk_act), step(pe=kk_pe), step(act=norm_act), step(dve=prep_dve),
              step(pe=bonus_pe, dve=sum_dve), step(act=exp_act, dve=bonus_dve), step(dve=scale_dve),
              step(core_pe, core_act, core_dve), after_step(), step(pe=g_pe, act=root_act), step(dve=gate_dve),
              Stage("turn", kb=KB, src=result),
              Stage("proj", chunks=columns(io["rwkv_w_o"][0], 0, D), feature_major=False, dest="out", evac=None),
              Stage("post", gain=post_gain, norm=True, scale=1.0, bias=None)]
    return loads, stages



GRID_W = 64
DILATED = ((128, 1), (512, 4), (2048, 16))
A_GROUPS, A_PER = len(DILATED), 8
A_HEADS = A_GROUPS * A_PER
A_HD = 64
B_HEADS, B_KV, B_HD = 8, 2, 128
B_ROT = B_HEADS + B_KV
BUCKETS, MAX_DISTANCE = 32, 1024
THETA = 10000.0


def hybrid_constants():
    import math
    import numpy as np
    rel = np.arange(2 * SEQ) - (SEQ - 1)
    n = BUCKETS // 2
    exact = n // 2
    a = np.abs(rel)
    large = exact + (np.log(np.maximum(a, 1).astype(np.float32) / np.float32(exact))
                     / np.float32(math.log(MAX_DISTANCE / exact)) * np.float32(n - exact)).astype(np.int32)
    bucket = np.where(rel > 0, n, 0) + np.where(a < exact, a, np.minimum(large, n - 1))
    onehot = (np.arange(BUCKETS)[:, None] == bucket[None, :]).astype(np.float32)
    out = np.zeros((A_GROUPS, 2 * SEQ), np.float32)
    for g, (window, dil) in enumerate(DILATED):
        out[g] = np.where((rel % dil == 0) & (a // dil <= window // (2 * dil)), 0.0, -1e30)
    group = (np.arange(A_GROUPS)[:, None] == np.arange(A_HEADS)[None, :] // A_PER).astype(np.float32)
    row, col = np.arange(SEQ) // GRID_W, np.arange(SEQ) % GRID_W
    nf = B_HD // 4
    freq = np.float32(THETA) ** (-np.arange(nf, dtype=np.float32) / np.float32(nf))
    ang = np.concatenate([row[:, None].astype(np.float32) * freq, col[:, None].astype(np.float32) * freq], -1)
    table = np.stack([np.cos(ang), np.sin(ang)], 1).reshape(NT, P, 2, B_HD // 2).transpose(1, 0, 2, 3)
    return {"c_onehot": onehot, "c_outside": out, "c_group": group,
            "c_rope": np.ascontiguousarray(table.reshape(P, NT * 2, B_HD // 2)).astype(np.float32)}


def hybrid(io):
    w = io["w_in_2"][0]
    A_QK = A_HEADS * A_HD
    o1 = 3 * A_QK
    o2 = o1 + B_ROT * B_HD
    o3 = o2 + B_KV * B_HD
    m = Mix()
    qf, kf = (m.take(A_HEADS // 2 * SEQ, (A_HEADS // 2, SEQ)) for _ in range(2))
    v = m.take(NT * A_QK, (NT, A_QK))
    A_KEYS = A_GROUPS * SEQ
    bias = [m.take(A_KEYS) for _ in range(2)]
    scores = [m.take(A_KEYS) for _ in range(2)]
    turned = [m.take(A_KEYS) for _ in range(2)]
    negmax, sums = m.take(NT * A_PER), m.take(NT * A_PER)
    onehot, outside, table, relb, group = bias[0], bias[1], scores[0], scores[1], turned[0]
    rope = Mix(MIX - NT * B_HD).take(NT * 2 * B_HD // 2, (NT * 2, B_HD // 2))
    rowsB, rowsG = slice(0, BUCKETS), slice(0, A_GROUPS)
    loads = [(lambda mix: onehot(mix, rowsB)[:, 0:2 * SEQ], io["c_onehot"]),
             (lambda mix: outside(mix, rowsG)[:, 0:2 * SEQ], io["c_outside"]),
             (lambda mix: relb(mix, rowsB)[:, 0:A_HEADS], io["rel_bias_2"]),
             (lambda mix: group(mix, rowsG)[:, 0:A_HEADS], io["c_group"]),
             (rope, io["c_rope"])]

    def table_pe(e, pe):
        o = e.out_bank[0][0:A_HEADS, :]
        e.nc.tensor.matmul(o, relb(e.mix, rowsB)[:, 0:A_HEADS], onehot(e.mix, rowsB)[:, 0:2 * SEQ], start=True, stop=False)
        e.nc.tensor.matmul(o, group(e.mix, rowsG)[:, 0:A_HEADS], outside(e.mix, rowsG)[:, 0:2 * SEQ], start=False, stop=True)

    def table_act(e, act):
        rows = table(e.mix, slice(0, A_HEADS))[:, 0:2 * SEQ]
        e.link_act(act, e.nc.scalar.activation(rows, e.out_bank[0][0:A_HEADS, :], ACT.Copy))
        act.dma_start(io["t_bias"], rows.unsqueeze(1).to_broadcast([A_HEADS, P, 2 * SEQ])).then_inc(e.named("table_stored"), 16)

    def evac_feature(dst, scale):
        def evac(e, c, bank, n):
            return e.nc.scalar.activation(dst(e.mix)[:, 2 * c:2 * c + 2, :],
                                          bank[:, :].rearrange("p (f n) -> p f n", f=2), ACT.Copy, scale=scale)
        return evac

    def evac_token(dst, at=0):
        def evac(e, c, bank, n):
            return e.nc.scalar.activation(dst(e.mix)[:, :, c * CH:c * CH + n],
                                          bank[:, :].rearrange("p (t n) -> p t n", t=NT)[:, :, 0:n], ACT.Copy)
        return evac

    def proj(lo, hi, evac, feature_major=False, by="act", loads=()):
        return Stage("proj", chunks=columns(w, lo, hi), feature_major=feature_major, dest="gate", by=by, evac=evac,
                     loads=list(loads))

    def setup_a(e, st):
        mix = e.mix

        def item(i):
            t, j = i // A_PER, i % A_PER
            rows = slice(A_HD * (j % 2), A_HD * (j % 2) + A_HD)
            sc, vs = [], []
            for g in range(A_GROUPS):
                tile = (g * A_PER + j) // 2
                sc.append((g * SEQ, qf(mix, rows)[:, tile, t * P:(t + 1) * P], kf(mix, rows)[:, tile, :]))
                cols = slice((g * A_PER + j) * A_HD, (g * A_PER + j + 1) * A_HD)
                vs += [v(mix)[:, s, cols] for s in range(NT)]
            return Item(sc, A_KEYS, bias[i % 2](mix), vs, e.y[:, t, j * A_HD:(j + 1) * A_HD])

        def load_bias(act, i):
            t, j = i // A_PER, i % A_PER
            tb = io["t_bias"]
            if i == 0:
                act.wait_ge(e.named("table_stored"), 16)
            src = bass.AP(tb.tensor, tb.offset + j * P * 2 * SEQ + SEQ - 1 - t * P,
                          [[2 * SEQ - 1, P], [A_PER * P * 2 * SEQ, A_GROUPS], [1, SEQ]])
            act.dma_start(bias[i % 2](mix).rearrange("p (g s) -> p g s", g=A_GROUPS), src).then_inc(
                e.named(f"bias{i % 2}_loaded"), 16)

        def before(dve, i):
            dve.wait_ge(e.named(f"bias{i % 2}_loaded"), 16 * (i // 2 + 1))

        st.item, st.load_bias, st.before = item, load_bias, before
        st.probs = lambda i: scores[i % 2](mix)
        st.turned = lambda i: turned[i % 2](mix)
        st.negmax, st.sums, st.sink = negmax(mix), sums(mix), None

    m = Mix()
    qk = m.take(NT * B_ROT * B_HD, (NT, B_ROT * B_HD))
    ob = m_ob = lambda mix: qk(mix)[:, :, 0:B_HEADS * B_HD]
    vb = m.take(NT * B_KV * B_HD, (NT, B_KV * B_HD))
    gates = m.take(NT * 2 * D, (NT, 2 * D))
    bg = m.take(2 * D)
    qkf = m.take(B_ROT * SEQ, (B_ROT, SEQ))
    scores_b = [m.take(SEQ) for _ in range(2)]
    turned_b = [m.take(SEQ) for _ in range(2)]
    negmax_b, sums_b = m.take(NT * B_HEADS), m.take(NT * B_HEADS)
    sq, mean, rt = (m.take(NT * B_ROT) for _ in range(3))
    gains = m.take(B_ROT * B_HD, (B_ROT, B_HD))
    assert m.at <= MIX - NT * B_HD

    def rows_of(g, n):
        return bass.AP(g.tensor, g.offset, [[0, P], [0, n], [1, B_HD]])

    loads_b = [(bg, spread(io["b_gate_2"][0])),
               (lambda mix: gains(mix)[:, 0:B_HEADS, :], rows_of(io["q_norm_2"][0], B_HEADS)),
               (lambda mix: gains(mix)[:, B_HEADS:B_ROT, :], rows_of(io["k_norm_2"][0], B_KV))]

    def heads_of(e):
        return qk(e.mix).rearrange("p t (h d) -> p (t h) d", d=B_HD)

    def norm_dve(e, dve):
        x = heads_of(e)
        tmp = qkf(e.mix).rearrange("p h (a d) -> p (h a) d", d=B_HD)
        e.link(dve, e.nc.vector.tensor_tensor(tmp, x, x, ALU.mult))
        e.link(dve, e.nc.vector.tensor_reduce(sq(e.mix), tmp, AX.X, ALU.add))
        e.nc.vector.tensor_scalar(mean(e.mix), sq(e.mix), 1.0 / B_HD, EPS, ALU.mult, ALU.add)

    def root_act(e, act):
        e.nc.scalar.activation(rt(e.mix), mean(e.mix), ACT.Sqrt)

    def rope_dve(e, dve):
        v_, x = e.nc.vector, heads_of(e)
        e.link(dve, v_.reciprocal(rt(e.mix), rt(e.mix)))
        e.link(dve, v_.tensor_tensor(x, x, along(rt(e.mix), B_HD), ALU.mult))
        H2 = B_HD // 2
        for t in range(NT):
            xt = x[:, t * B_ROT:(t + 1) * B_ROT, :]
            e.link(dve, v_.tensor_tensor(xt, xt, gains(e.mix), ALU.mult))
            pair = xt.rearrange("p h (f two) -> p h f two", two=2)
            x0, x1 = pair[:, :, :, 0], pair[:, :, :, 1]
            c = rope(e.mix)[:, 2 * t:2 * t + 1, :].to_broadcast([P, B_ROT, H2])
            s = rope(e.mix)[:, 2 * t + 1:2 * t + 2, :].to_broadcast([P, B_ROT, H2])
            tmp = qkf(e.mix).rearrange("p h s -> p (h s)")
            p4 = [tmp[:, n * B_ROT * H2:(n + 1) * B_ROT * H2].rearrange("p (h f) -> p h f", h=B_ROT) for n in range(4)]
            v_.tensor_tensor(p4[0], x0, c, ALU.mult)
            v_.tensor_tensor(p4[1], x1, s, ALU.mult)
            v_.tensor_tensor(p4[2], x0, s, ALU.mult)
            e.link(dve, v_.tensor_tensor(p4[3], x1, c, ALU.mult))
            v_.tensor_tensor(x0, p4[0], p4[1], ALU.subtract)
            e.link(dve, v_.tensor_tensor(x1, p4[2], p4[3], ALU.add))

    fills = [[(t, hd) for t in range(NT) for hd in range(B_ROT)][f:f + 4] for f in range(0, NT * B_ROT, 4)]

    def turn_pe(e, pe):
        for f, blocks in enumerate(fills):
            if f >= 2:
                pe.wait_ge(e.named("rope_copied"), f - 1)
            for b, (t, hd) in enumerate(blocks):
                last = e.nc.tensor.transpose(e.turn_bank[f % 2][:, b * P:(b + 1) * P],
                                             qk(e.mix)[:, t, hd * B_HD:(hd + 1) * B_HD], e.ident[:, :])
            last.then_inc(e.named("rope_turned"), 1)

    def turn_act(e, act):
        for f, blocks in enumerate(fills):
            act.wait_ge(e.named("rope_turned"), f + 1)
            for b, (t, hd) in enumerate(blocks):
                last = e.nc.scalar.activation(qkf(e.mix)[:, hd, t * P:(t + 1) * P],
                                              e.turn_bank[f % 2][:, b * P:(b + 1) * P], ACT.Copy)
            last.then_inc(e.named("rope_copied"), 1)

    def setup_b(e, st):
        mix = e.mix

        def item(i):
            t, hd = i // B_HEADS, i % B_HEADS
            g = hd // (B_HEADS // B_KV)
            return Item([(0, qkf(mix)[:, hd, t * P:(t + 1) * P], qkf(mix)[:, B_HEADS + g, :])], SEQ, None,
                        [vb(mix)[:, s, g * B_HD:(g + 1) * B_HD] for s in range(NT)],
                        ob(mix)[:, t, hd * B_HD:(hd + 1) * B_HD])

        st.item, st.load_bias, st.before = item, None, None
        st.probs = lambda i: scores_b[i % 2](mix)
        st.turned = lambda i: turned_b[i % 2](mix)
        st.negmax, st.sums, st.sink = negmax_b(mix), sums_b(mix), None

    def evac_gates(e, c, bank, n):
        return e.nc.vector.tensor_tensor(gates(e.mix)[:, :, c * CH:(c + 1) * CH],
                                         bank[:, :].rearrange("p (t n) -> p t n", t=NT),
                                         bg(e.mix)[:, c * CH:(c + 1) * CH].unsqueeze(1).to_broadcast([P, NT, CH]), ALU.add)

    def gate_act(e, act):
        for t in range(NT):
            e.nc.scalar.activation(gates(e.mix)[:, t, :], gates(e.mix)[:, t, :], ACT.Sigmoid)

    def merge(branch):
        def dve_(e, dve):
            for t in range(NT):
                for n in range(2):
                    gt = gates(e.mix)[:, t, branch * D + n * 512:branch * D + (n + 1) * 512]
                    dst = e.y[:, t, n * 512:(n + 1) * 512] if branch == 0 else gt
                    last = e.nc.vector.tensor_tensor(dst, gt, e.out_bank[2 * t + n][:, :], ALU.mult)
            if branch == 1:
                e.link(dve, last)
                e.nc.vector.tensor_tensor(e.y[:, :, :], e.y[:, :, :], gates(e.mix)[:, :, D:2 * D], ALU.add)
        return dve_

    def back(name):
        return Stage("proj", chunks=columns(io[name][0], 0, D), feature_major=False, dest="out", evac=None)

    stages = [step(pe=table_pe), step(act=table_act),
              Stage("pre", gain=io["mix_norm_2"][0]), Stage("turn", kb=KB),
              proj(0, A_QK, evac_feature(qf, A_HD ** -0.5), feature_major=True),
              proj(A_QK, 2 * A_QK, evac_feature(kf, 1.0), feature_major=True), proj(2 * A_QK, o1, evac_token(v)),
              Stage("attention", items=NT * A_PER, max_blocks=NT * A_GROUPS, scale=1.0, setup=setup_a),
              proj(o1, o2, evac_token(qk), loads=loads_b), proj(o2, o3, evac_token(vb)),
              proj(o3, o3 + 2 * D, evac_gates, by="dve"), step(act=gate_act),
              step(dve=norm_dve), step(act=root_act), step(dve=rope_dve), step(pe=turn_pe, act=turn_act),
              Stage("attention", items=NT * B_HEADS, max_blocks=NT, scale=B_HD ** -0.5, setup=setup_b),
              Stage("turn", kb=A_PER * A_HD // P), back("w_branch_a_2"), step(dve=merge(0)),
              Stage("turn", kb=KB, src=ob), back("w_branch_b_2"), step(dve=merge(1)),
              Stage("turn", kb=KB), back("w_out_2"),
              Stage("post", gain=None, norm=False, scale=1.0, bias=None)]
    return loads, stages


def network(io, only=None):
    st = []

    def ffn(gate, up, down, loads=()):
        return Stage("ffn", gate=gate, up=up, down=down, loads=list(loads))

    def first_ffn(l, i, loads=()):
        g, w = io["norm_g"][l], io["ffn_w_in"][l, i]
        return [Stage("pre", gain=g[4 * i]), Stage("turn", kb=KB),
                ffn(w[:, 0:D_FF], w[:, D_FF:2 * D_FF], io["ffn_w_out"][l, i], loads),
                Stage("post", gain=g[4 * i + 1], norm=True, scale=0.5, bias=None)]

    def second_ffn(n, loads=()):
        w = [io[f"ffn{n}_w{i}_2"][0] for i in (1, 3, 2)]
        return [Stage("pre", gain=io[f"ffn{n}_norm_2"][0]), Stage("turn", kb=KB), ffn(*w, loads),
                Stage("post", gain=None, norm=False, scale=0.5, bias=None)]

    for layer in only if only is not None else [0, 1, 2, 3, 4]:
        if isinstance(layer, tuple):
            part, layer = layer
        else:
            part = "all"
        if layer < 4:
            g = io["norm_g"][layer]
            loads, mixer = (lambda: swa(io, 0, g[2], g[3]), lambda: gla(io, g[2], g[3]),
                            lambda: rwkv(io, g[2], g[3]), lambda: swa(io, 1, g[2], g[3]))[layer]()
            before, after, tail = [], [], []
            if part != "mixer":
                before, after = first_ffn(layer, 0, loads), first_ffn(layer, 1)
        else:
            loads, mixer = hybrid(io)
            before, after = ([], []) if part == "mixer" else (second_ffn(1, loads), second_ffn(2))
            tail = [Stage("pre", gain=io["final_norm_2"])]
        if part == "mixer":
            before, after = [Stage("load", loads=loads)], []
        if part == "none":
            before, after = [], []
        st += before + mixer + after + tail
    return joined(st)


def joined(stages):
    out, n = [], 0
    while n < len(stages):
        if stages[n].kind not in ("post", "pre"):
            out.append(stages[n])
            n += 1
            continue
        post = pre = None
        turn = False
        if stages[n].kind == "post":
            post = stages[n]
            n += 1
        if n < len(stages) and stages[n].kind == "pre":
            pre = stages[n]
            n += 1
            if n < len(stages) and stages[n].kind == "turn":
                turn = True
                n += 1
        out.append(Stage("cross", post=post, pre=pre, turn=turn))
    return out


def constants():
    import numpy as np
    q, k = np.arange(P)[:, None] + P, np.arange(2 * P)[None, :]
    window = np.where((q - k >= 0) & (q - k < WINDOW), 0.0, -1e30).astype(np.float32)
    return {"c_window": window, "c_levels": level_masks(), **rwkv_constants(), **hybrid_constants()}


_OUTS = [((1, SEQ, D), "float32")]


def kernel(**inputs):
    import numpy as _np
    import concourse.bacc as _bacc
    from concourse import mybir as _mybir
    from concourse.bass_utils import run_bass_kernel_spmd as _run

    nc = _bacc.Bacc("TRN2", target_bir_lowering=False, num_devices=1)
    arrays, io = {}, {}
    inputs.update(constants())
    for name in inputs:
        a = _np.ascontiguousarray(inputs[name])
        arrays[f"in_{name}_dram"] = a
        io[name] = nc.dram_tensor(f"in_{name}_dram", a.shape, _mybir.dt.from_np(a.dtype), kind="ExternalInput").ap()
    out = nc.dram_tensor("out_0_dram", _OUTS[0][0], F32, kind="ExternalOutput").ap()
    io["t_bias"] = nc.dram_tensor("t_bias", (A_HEADS, P, 2 * SEQ), F32, kind="Internal").ap()
    build(nc, io, out, network(io))
    r = _run(nc, [arrays], core_ids=[0])
    return r.results[0]["out_0_dram"]
```
